# Optimizing a Trainium2 kernel written in Bass

```python
import math
import jax, jax.numpy as jnp
from jax import lax
import numpy as np

D_MODEL = 1024
BATCH = 1
SEQ = 256
DEPTH = 1

GDN_HEADS = 8
GDN_DK = 128
GDN_DV = 128
GDN_CONV = 4
GDN_CHUNK = 64
DIL_PATTERN = ((128, 1), (512, 4), (2048, 16))
DIL_HEADS_PER_GROUP = 4
DIL_HD = 128
DIL_BLOCK = 128
N_EXPERTS = 64
TOP_K = 8
N_GROUPS = 8
TOPK_GROUPS = 4
D_EXPERT = 256
D_SHARED = 256
ROUTE_SCALE = 2.5
MOE_TOKEN_BLOCK = 512
EPS = 1e-6

GDN_QK_W = GDN_HEADS * GDN_DK
GDN_V_W = GDN_HEADS * GDN_DV
N_DIL_GROUPS = len(DIL_PATTERN)
DIL_HEADS = N_DIL_GROUPS * DIL_HEADS_PER_GROUP
DIL_W = DIL_HEADS * DIL_HD
DIL_OUT_W = DIL_HEADS_PER_GROUP * DIL_HD
SPLIT_WIDTHS = (GDN_QK_W, GDN_QK_W, GDN_V_W, GDN_V_W, GDN_HEADS, GDN_HEADS,
                DIL_W, DIL_W, DIL_W, D_MODEL, D_MODEL)
IN_W = sum(SPLIT_WIDTHS)
SPLIT_OFFSETS = tuple(sum(SPLIT_WIDTHS[:i + 1]) for i in range(len(SPLIT_WIDTHS) - 1))


def _rms(t, g):
    t32 = t.astype(jnp.float32)
    return t32 * lax.rsqrt(jnp.mean(t32 * t32, axis=-1, keepdims=True) + EPS) * g.astype(jnp.float32)

def _l2norm(t):
    return t * lax.rsqrt(jnp.sum(t * t, axis=-1, keepdims=True) + EPS)

def causal_depthwise_conv(x, w):
    K, C = w.shape
    return lax.conv_general_dilated(x, w[:, None, :], window_strides=(1,), padding=((K - 1, 0),),
                                    dimension_numbers=('NWC', 'WIO', 'NWC'), feature_group_count=C)

def chunk_gated_delta_rule(q, k, v, g, beta):
    B, H, S, dk = q.shape
    dv = v.shape[-1]
    C = GDN_CHUNK
    N = S // C
    q = q.reshape(B, H, N, C, dk)
    k = k.reshape(B, H, N, C, dk)
    v = v.reshape(B, H, N, C, dv)
    g = g.reshape(B, H, N, C)
    beta = beta.reshape(B, H, N, C)
    gc = jnp.cumsum(g, axis=-1)
    incl = jnp.tril(jnp.ones((C, C), bool))
    strict = jnp.tril(jnp.ones((C, C), bool), -1)
    decay = jnp.exp(jnp.where(incl, gc[..., :, None] - gc[..., None, :], -jnp.inf))
    k_beta = k * beta[..., None]
    a_mat = jnp.where(strict, jnp.einsum('bhnid,bhnjd->bhnij', k_beta, k) * decay, 0.0)
    lmat = a_mat + jnp.eye(C, dtype=a_mat.dtype)
    rhs = jnp.concatenate([v * beta[..., None], k_beta * jnp.exp(gc)[..., None]], axis=-1)
    sol = lax.linalg.triangular_solve(lmat, rhs, left_side=True, lower=True, unit_diagonal=True)
    u, w = sol[..., :dv], sol[..., dv:]
    qk = jnp.einsum('bhnid,bhnjd->bhnij', q, k) * decay
    q_dec = q * jnp.exp(gc)[..., None]
    k_dec = k * jnp.exp(gc[..., -1:] - gc)[..., None]
    g_tot = jnp.exp(gc[..., -1])

    def step(state, xs):
        u_n, w_n, qk_n, qd_n, kd_n, gt_n = xs
        v_new = u_n - jnp.einsum('bhck,bhkv->bhcv', w_n, state)
        o_n = jnp.einsum('bhck,bhkv->bhcv', qd_n, state) + jnp.einsum('bhij,bhjv->bhiv', qk_n, v_new)
        state = state * gt_n[..., None, None] + jnp.einsum('bhck,bhcv->bhkv', kd_n, v_new)
        return state, o_n

    xs = tuple(jnp.moveaxis(t, 2, 0) for t in (u, w, qk, q_dec, k_dec, g_tot))
    state0 = jnp.zeros((B, H, dk, dv), q.dtype)
    _, o = lax.scan(step, state0, xs)
    return jnp.moveaxis(o, 0, 2).reshape(B, H, S, dv)

def gated_deltanet(q, k, v, z, b, a, conv_w, a_log, dt_bias, norm_g):
    B, S, _ = q.shape
    f32 = jnp.float32
    qkv = jnp.concatenate([q, k, v], axis=-1).astype(f32)
    qkv = jax.nn.silu(causal_depthwise_conv(qkv, conv_w.astype(f32)))
    q, k, v = jnp.split(qkv, [GDN_QK_W, 2 * GDN_QK_W], axis=-1)

    def heads(t, d):
        return t.reshape(B, S, GDN_HEADS, d).transpose(0, 2, 1, 3)

    q = _l2norm(heads(q, GDN_DK)) * (GDN_DK ** -0.5)
    k = _l2norm(heads(k, GDN_DK))
    v = heads(v, GDN_DV)
    beta = jax.nn.sigmoid(b.astype(f32)).transpose(0, 2, 1)
    g = (-jnp.exp(a_log.astype(f32)) * jax.nn.softplus(a.astype(f32) + dt_bias.astype(f32))).transpose(0, 2, 1)
    o = chunk_gated_delta_rule(q, k, v, g, beta).transpose(0, 2, 1, 3)
    zg = jax.nn.silu(z.astype(f32).reshape(B, S, GDN_HEADS, GDN_DV))
    o = _rms(o, norm_g) * zg
    return o.reshape(B, S, GDN_V_W)

def dilated_window_attention(q, k, v, window, dilation):
    B, S, h, e = q.shape
    L = S // dilation
    W = window // dilation
    blk = math.gcd(L, DIL_BLOCK)
    nb = L // blk

    def sub(t):
        return t.reshape(B, L, dilation, h, e).transpose(0, 2, 3, 1, 4)

    qs = sub(q).reshape(B, dilation, h, nb, blk, e)
    key_idx = np.arange(nb)[:, None] * blk + np.arange(blk + W)[None, :]
    pad = ((0, 0), (0, 0), (0, 0), (W, 0), (0, 0))
    ks = jnp.pad(sub(k), pad)[:, :, :, key_idx]
    vs = jnp.pad(sub(v), pad)[:, :, :, key_idx]
    dist = np.arange(blk)[:, None] + W - np.arange(blk + W)[None, :]
    valid = (dist >= 0) & (dist <= W) & ((key_idx[:, None, :] - W) >= 0)
    s = jnp.einsum('bdhnqe,bdhnke->bdhnqk', qs, ks) * (e ** -0.5)
    s = jnp.where(valid, s, -jnp.inf)
    m = jnp.max(s, axis=-1, keepdims=True)
    p = jnp.exp(s - m)
    den = jnp.sum(p, axis=-1, keepdims=True)
    o = jnp.einsum('bdhnqk,bdhnke->bdhnqe', p, vs) / den
    lse = (m + jnp.log(den))[..., 0]
    o = o.reshape(B, dilation, h, L, e).transpose(0, 3, 1, 2, 4).reshape(B, S, h, e)
    lse = lse.reshape(B, dilation, h, L).transpose(0, 3, 1, 2).reshape(B, S, h)
    return o, lse

def dilated_mixture(q, k, v, q_norm_g, k_norm_g):
    B, S, _ = q.shape
    q = _rms(q.reshape(B, S, DIL_HEADS, DIL_HD), q_norm_g)
    k = _rms(k.reshape(B, S, DIL_HEADS, DIL_HD), k_norm_g)
    v = v.reshape(B, S, DIL_HEADS, DIL_HD).astype(jnp.float32)
    outs, lses = [], []
    for gi, (win, dil) in enumerate(DIL_PATTERN):
        hs = slice(gi * DIL_HEADS_PER_GROUP, (gi + 1) * DIL_HEADS_PER_GROUP)
        o, lse = dilated_window_attention(q[:, :, hs], k[:, :, hs], v[:, :, hs], win, dil)
        outs.append(o)
        lses.append(lse)
    wts = jax.nn.softmax(jnp.stack(lses), axis=0)
    y = jnp.einsum('gbsh,gbshe->bshe', wts, jnp.stack(outs))
    return y.reshape(B, S, DIL_OUT_W)

def moe_ffn(h, w_router, router_bias, w_gate, w_up, w_down, ws_gate, ws_up, ws_down):
    B, S, D = h.shape
    T = B * S
    f32 = jnp.float32
    ht = h.reshape(T, D)
    scores = jax.nn.sigmoid(ht.astype(f32) @ w_router.astype(f32))
    sel = scores + router_bias.astype(f32)
    grp = sel.reshape(T, N_GROUPS, N_EXPERTS // N_GROUPS)
    grp_score = jnp.sum(lax.top_k(grp, 2)[0], axis=-1)
    _, gidx = lax.top_k(grp_score, TOPK_GROUPS)
    gmask = jnp.sum(jax.nn.one_hot(gidx, N_GROUPS, dtype=f32), axis=1)
    emask = jnp.repeat(gmask, N_EXPERTS // N_GROUPS, axis=1) > 0
    _, eidx = lax.top_k(jnp.where(emask, sel, -jnp.inf), TOP_K)
    wk = jnp.take_along_axis(scores, eidx, axis=-1)
    wk = wk / jnp.sum(wk, axis=-1, keepdims=True) * ROUTE_SCALE
    combine = jnp.einsum('tk,tke->te', wk, jax.nn.one_hot(eidx, N_EXPERTS, dtype=f32)).astype(h.dtype)
    tb = math.gcd(T, MOE_TOKEN_BLOCK)

    def block(args):
        hb, cb = args
        a = jnp.einsum('td,edf->tef', hb, w_gate)
        u = jnp.einsum('td,edf->tef', hb, w_up)
        return jnp.einsum('tef,efd->td', jax.nn.silu(a) * u * cb[..., None], w_down)

    routed = lax.map(block, (ht.reshape(T // tb, tb, D), combine.reshape(T // tb, tb, N_EXPERTS))).reshape(T, D)
    shared = (jax.nn.silu(ht @ ws_gate) * (ht @ ws_up)) @ ws_down
    return (routed + shared).reshape(B, S, D)

def first_inputs(seed: int = 0) -> dict:
    key = jax.random.key(seed)
    ks = jax.random.split(key, 24)
    L, D, E = DEPTH, D_MODEL, N_EXPERTS
    nrm = lambda k, shape, scale: jax.random.normal(k, shape, jnp.float32) * scale
    dt = jnp.exp(jax.random.uniform(ks[7], (L, GDN_HEADS), jnp.float32, math.log(1e-3), math.log(1e-1)))
    return {
        "x": nrm(ks[0], (BATCH, SEQ, D), 1.0),
        "c": nrm(ks[1], (BATCH, D), 1.0),
        "w_ada": nrm(ks[2], (L, D, 6 * D), 0.5 * D ** -0.5),
        "b_ada": nrm(ks[3], (L, 6 * D), 0.02),
        "g_mix": 1.0 + nrm(ks[4], (L, D), 0.05),
        "w_in": nrm(ks[5], (L, D, IN_W), D ** -0.5),
        "gdn_conv_w": nrm(ks[6], (L, GDN_CONV, 2 * GDN_QK_W + GDN_V_W), 0.5),
        "gdn_a_log": jnp.log(jax.random.uniform(ks[8], (L, GDN_HEADS), jnp.float32, 1.0, 16.0)),
        "gdn_dt_bias": dt + jnp.log(-jnp.expm1(-dt)),
        "gdn_norm_g": 1.0 + nrm(ks[9], (L, GDN_DV), 0.05),
        "dil_q_norm_g": 1.0 + nrm(ks[10], (L, DIL_HD), 0.05),
        "dil_k_norm_g": 1.0 + nrm(ks[11], (L, DIL_HD), 0.05),
        "w_up_gdn": nrm(ks[12], (L, GDN_V_W, D), GDN_V_W ** -0.5),
        "w_up_dil": nrm(ks[13], (L, DIL_OUT_W, D), DIL_OUT_W ** -0.5),
        "w_out": nrm(ks[14], (L, D, D), D ** -0.5),
        "g_ffn": 1.0 + nrm(ks[15], (L, D), 0.05),
        "w_router": nrm(ks[16], (L, D, E), D ** -0.5),
        "router_bias": nrm(ks[17], (L, E), 0.01),
        "w_exp_gate": nrm(ks[18], (L, E, D, D_EXPERT), D ** -0.5),
        "w_exp_up": nrm(ks[19], (L, E, D, D_EXPERT), D ** -0.5),
        "w_exp_down": nrm(ks[20], (L, E, D_EXPERT, D), D_EXPERT ** -0.5),
        "w_sh_gate": nrm(ks[21], (L, D, D_SHARED), D ** -0.5),
        "w_sh_up": nrm(ks[22], (L, D, D_SHARED), D ** -0.5),
        "w_sh_down": nrm(ks[23], (L, D_SHARED, D), D_SHARED ** -0.5),
    }

def first_block(x, c, w_ada, b_ada, g_mix, w_in, gdn_conv_w, gdn_a_log, gdn_dt_bias, gdn_norm_g,
              dil_q_norm_g, dil_k_norm_g, w_up_gdn, w_up_dil, w_out, g_ffn, w_router, router_bias,
              w_exp_gate, w_exp_up, w_exp_down, w_sh_gate, w_sh_up, w_sh_down):
    cs = jax.nn.silu(c)
    for l in range(DEPTH):
        mod = (cs @ w_ada[l] + b_ada[l])[:, None, :]
        sh1, sc1, gt1, sh2, sc2, gt2 = jnp.split(mod, 6, axis=-1)
        h = _rms(x, g_mix[l]).astype(x.dtype) * (1.0 + sc1) + sh1
        proj = h @ w_in[l]
        (gq, gk, gv, gz, gb, ga, dil_q, dil_k, dil_v, gate_a, gate_b) = jnp.split(proj, SPLIT_OFFSETS, axis=-1)
        y_a = gated_deltanet(gq, gk, gv, gz, gb, ga, gdn_conv_w[l], gdn_a_log[l], gdn_dt_bias[l],
                             gdn_norm_g[l]).astype(x.dtype)
        y_b = dilated_mixture(dil_q, dil_k, dil_v, dil_q_norm_g[l], dil_k_norm_g[l]).astype(x.dtype)
        merged = jax.nn.sigmoid(gate_a) * (y_a @ w_up_gdn[l]) + jax.nn.sigmoid(gate_b) * (y_b @ w_up_dil[l])
        x = x + gt1 * (merged @ w_out[l])
        h2 = _rms(x, g_ffn[l]).astype(x.dtype) * (1.0 + sc2) + sh2
        x = x + gt2 * moe_ffn(h2, w_router[l], router_bias[l], w_exp_gate[l], w_exp_up[l], w_exp_down[l],
                              w_sh_gate[l], w_sh_up[l], w_sh_down[l])
    return x


DEPTH_2 = 2

N_MIXERS = 2
N_META = 16
N_HEADS = 8
HEAD_DIM = D_MODEL // (2 * N_HEADS)
V_DIM = 2 * HEAD_DIM
CONV_WIDTH = 3
CONV_GROUPS = 8
D_FF = 4 * D_MODEL
Q_BLOCK = 128
RMS_EPS = 1e-6
N_ATTN_LAYERS = (DEPTH_2 + 1) // 2
N_CONV_LAYERS = DEPTH_2 // 2


def _rmsnorm(x, g):
    xf = x.astype(jnp.float32)
    y = xf * lax.rsqrt(jnp.mean(xf * xf, axis=-1, keepdims=True) + RMS_EPS)
    return (y * g.astype(jnp.float32)).astype(x.dtype)

def _alibi_slopes(n_heads):
    return jnp.exp2(-8.0 * jnp.arange(1, n_heads + 1, dtype=jnp.float32) / n_heads)

def _lambda_init(layer_idx):
    return 0.8 - 0.6 * math.exp(-0.3 * layer_idx)

def _query_blocks(total_len):
    blocks = [(0, N_META)]
    start = N_META
    while start < total_len:
        end = min(start + Q_BLOCK, total_len)
        blocks.append((start, end))
        start = end
    return blocks

def _diff_attention(h, w_in, w_out, lam_vec, subln_g, lam_init):
    bsz, L, _ = h.shape
    qkv = jnp.einsum('bld,de->ble', h, w_in)
    q, k, v = jnp.split(qkv, 3, axis=-1)
    q = q.reshape(bsz, L, N_HEADS, 2, HEAD_DIM)
    k = k.reshape(bsz, L, N_HEADS, 2, HEAD_DIM)
    v = v.reshape(bsz, L, N_HEADS, V_DIM)
    lv = lam_vec.astype(jnp.float32)
    lam = jnp.exp(jnp.sum(lv[0] * lv[1])) - jnp.exp(jnp.sum(lv[2] * lv[3])) + lam_init
    slopes = _alibi_slopes(N_HEADS)
    scale = HEAD_DIM ** -0.5
    pos = jnp.arange(L, dtype=jnp.int32)
    outs = []
    for qs, qe in _query_blocks(L):
        s = jnp.einsum('bqhcd,bkhcd->bhcqk', q[:, qs:qe], k[:, :qe]).astype(jnp.float32) * scale
        dist = (pos[qs:qe, None] - pos[None, :qe]).astype(jnp.float32)
        bias = -slopes[:, None, None, None] * dist
        s = jnp.where(dist >= 0, s + bias, -jnp.inf)
        p = jax.nn.softmax(s, axis=-1)
        a = (p[:, :, 0] - lam * p[:, :, 1]).astype(v.dtype)
        outs.append(jnp.einsum('bhqk,bkhe->bqhe', a, v[:, :qe]))
    o = jnp.concatenate(outs, axis=1)
    o = _rmsnorm(o, subln_g) * (1.0 - lam_init)
    return jnp.einsum('ble,ed->bld', o.reshape(bsz, L, N_HEADS * V_DIM), w_out)

def _short_conv(h, w_in, conv_w, w_out):
    bcu = jnp.einsum('bld,de->ble', h, w_in)
    b_gate, c_gate, u = jnp.split(bcu, 3, axis=-1)
    u = c_gate * u
    y = lax.conv_general_dilated(
        u, conv_w[:, None, :].astype(u.dtype), window_strides=(1,),
        padding=[(CONV_WIDTH - 1, 0)], dimension_numbers=('NWC', 'WIO', 'NWC'),
        feature_group_count=D_MODEL)
    return jnp.einsum('bld,de->ble', b_gate * y, w_out)

def _sqrelu_mlp(h, w_up, w_down):
    a = jax.nn.relu(jnp.einsum('bld,df->blf', h, w_up))
    return jnp.einsum('blf,fd->bld', a * a, w_down)

def second_inputs(seed: int = 0) -> dict:
    key = jax.random.key(seed)
    ks = jax.random.split(key, 10)
    x = jax.random.normal(ks[0], (BATCH, SEQ, D_MODEL), jnp.float32)
    meta_tokens = jax.random.normal(ks[1], (N_META, D_MODEL), jnp.float32)
    norm_g = 1.0 + 0.05 * jax.random.normal(ks[2], (DEPTH_2, 4, D_MODEL), jnp.float32)
    w_in = jax.random.normal(ks[3], (DEPTH_2, D_MODEL, 3 * D_MODEL), jnp.float32) * D_MODEL ** -0.5
    w_out = jax.random.normal(ks[4], (DEPTH_2, D_MODEL, D_MODEL), jnp.float32) * D_MODEL ** -0.5
    lambda_params = 0.1 * jax.random.normal(ks[5], (N_ATTN_LAYERS, 4, HEAD_DIM), jnp.float32)
    subln_g = 1.0 + 0.05 * jax.random.normal(ks[6], (N_ATTN_LAYERS, V_DIM), jnp.float32)
    conv_w = jax.random.normal(ks[7], (N_CONV_LAYERS, CONV_WIDTH, D_MODEL), jnp.float32) * CONV_WIDTH ** -0.5
    w_up = jax.random.normal(ks[8], (DEPTH_2, D_MODEL, D_FF), jnp.float32) * D_MODEL ** -0.5
    w_down = jax.random.normal(ks[9], (DEPTH_2, D_FF, D_MODEL), jnp.float32) * D_FF ** -0.5
    return {'x': x, 'meta_tokens': meta_tokens, 'norm_g': norm_g, 'w_in': w_in, 'w_out': w_out,
            'lambda_params': lambda_params, 'subln_g': subln_g, 'conv_w': conv_w,
            'w_up': w_up, 'w_down': w_down}

def second_block(x, meta_tokens, norm_g, w_in, w_out, lambda_params, subln_g, conv_w, w_up, w_down):
    bsz = x.shape[0]
    meta = jnp.broadcast_to(meta_tokens[None].astype(x.dtype), (bsz, N_META, D_MODEL))
    hres = jnp.concatenate([meta, x], axis=1)
    for i in range(DEPTH_2):
        h = _rmsnorm(hres, norm_g[i, 0])
        if i % N_MIXERS == 0:
            m = _diff_attention(h, w_in[i], w_out[i], lambda_params[i // N_MIXERS],
                                subln_g[i // N_MIXERS], _lambda_init(i))
        else:
            m = _short_conv(h, w_in[i], conv_w[i // N_MIXERS], w_out[i])
        hres = hres + _rmsnorm(m, norm_g[i, 1])
        h = _rmsnorm(hres, norm_g[i, 2])
        hres = hres + _rmsnorm(_sqrelu_mlp(h, w_up[i], w_down[i]), norm_g[i, 3])
    return hres[:, N_META:]


def setup_inputs(seed=0):
    out = dict(first_inputs(seed))
    for name, value in second_inputs(seed + 1).items():
        if name != "x":
            out[name + "_2"] = value
    return out


def reference(
    x, c, w_ada, b_ada, g_mix, w_in, gdn_conv_w, gdn_a_log, gdn_dt_bias, gdn_norm_g,
    dil_q_norm_g, dil_k_norm_g, w_up_gdn, w_up_dil, w_out, g_ffn, w_router, router_bias,
    w_exp_gate, w_exp_up, w_exp_down, w_sh_gate, w_sh_up, w_sh_down, meta_tokens_2, norm_g_2,
    w_in_2, w_out_2, lambda_params_2, subln_g_2, conv_w_2, w_up_2, w_down_2,
):
    x = first_block(
        x, c, w_ada, b_ada, g_mix, w_in, gdn_conv_w, gdn_a_log, gdn_dt_bias, gdn_norm_g,
        dil_q_norm_g, dil_k_norm_g, w_up_gdn, w_up_dil, w_out, g_ffn, w_router, router_bias,
        w_exp_gate, w_exp_up, w_exp_down, w_sh_gate, w_sh_up, w_sh_down,
    )
    return second_block(
        x, meta_tokens_2, norm_g_2, w_in_2, w_out_2, lambda_params_2, subln_g_2, conv_w_2,
        w_up_2, w_down_2,
    )


_drawn_inputs = setup_inputs


def setup_inputs(seed=0):
    import zlib

    import numpy as np

    out = dict(_drawn_inputs(seed))
    spreads = {}
    factors = {'dil_q_norm_g': 3.562, 'dil_k_norm_g': 3.084}
    for name, (base, spread) in spreads.items():
        noise = np.random.default_rng([zlib.crc32(name.encode()), seed]).standard_normal(out[name].shape)
        drawn = base * np.exp(spread * noise) if base else spread * noise
        out[name] = __import__('jax').numpy.asarray(drawn.astype(out[name].dtype))
    for name, factor in factors.items():
        out[name] = (out[name] * factor).astype(out[name].dtype)
    return out
```

```python
from contextlib import ExitStack

import concourse.bass as bass
import numpy as np
from concourse import mybir

ALU = mybir.AluOpType
ACT = mybir.ActivationFunctionType
AX = mybir.AxisListType
F32 = mybir.dt.float32

P = 128
D = 1024
KB = 8
T = 256
META = 16
L = T + META
NH = 8
NSLOT = 4
NG = 3
NE = 64
DFF = 4096
EPS = 1e-6
BIG = 1e30
LAM0 = 0.2
NSLOTS = 8
ARENA = 21504
SMALL = [("c", 8), ("b_ada", 48), ("g_mix", 8), ("g_ffn", 8), ("conv", 96), ("gdn_g", 1),
         ("dq_g", 1), ("dk_g", 1), ("norm2", 64), ("conv2", 24), ("subln", 1),
         ("a_log", 8), ("dt", 8), ("rbias", 64), ("lam", 256), ("w_ba", 128), ("w_r", 512)]
LEVELS = [1, 2, 4, 8, 16, 32, 64]
CONST = [("ident", 128), ("ones", 128), ("tri", 128), ("pm1", 128), ("pm2", 128),
         ("lo1", 128)] + [(f"up{s}", 128) for s in LEVELS] + \
        [("dm0", 384), ("dm1", 768), ("nd0", 16), ("nd1", 144), ("nd2", 272), ("eps", 1)]


def columns(table):
    at, out = 0, {}
    for name, n in table:
        out[name] = (at, n)
        at += n
    return out, at


def constants():
    i = np.arange(P)[:, None]
    j = np.arange(P)[None, :]
    out = [np.eye(P), np.ones((P, P)), (i <= j), np.where(j < i, 0.0, BIG), np.where(i <= j, 0.0, BIG)]

    def low(a, b, s):
        return (a // (2 * s) == b // (2 * s)) & (a // s % 2 == 1) & (b // s % 2 == 0)

    out.append(low(i, j, 1))
    out += [low(j, i, s) for s in LEVELS]

    def dil(q, k, g):
        dist = q - k
        if g == 0:
            ok = (dist >= 0) & (dist <= 128)
        else:
            ok = (dist >= 0) & (dist % (4 if g == 1 else 16) == 0)
        return np.where(ok, 0.0, -BIG)

    k2 = np.arange(2 * P)[None, :]
    out += [dil(i, j, g) for g in range(NG)]
    out += [dil(i + P, k2, g) for g in range(NG)]
    for q0, nk in ((0, 16), (16, 144), (144, 272)):
        dist = (i + q0) - np.arange(nk)[None, :]
        out.append(np.where(dist >= 0, -dist, -BIG))
    out.append(np.full((P, 1), EPS))
    return np.ascontiguousarray(np.concatenate([np.broadcast_to(a, (P, a.shape[1])) for a in out], axis=1),
                                dtype=np.float32)


class Tok:

    def __init__(self, q, n):
        self.q, self.n, self.used = q, n, False


class Queue:

    def __init__(self, name, sem):
        self.name, self.sem, self.ops = name, sem, []

    def add(self, fn, waits):
        t = Tok(self, len(self.ops))
        for w in waits:
            if w is not None:
                w.used = True
        self.ops.append((fn, [w for w in waits if w is not None], t))
        return t

    def number(self):
        n = 0
        for _, _, t in self.ops:
            if t.used and t.q is self:
                n += 1
            t.value = n

    def emit(self, eng):
        seen = {}
        for fn, waits, t in self.ops:
            need = {}
            for w in waits:
                s, v = (w.q.sem, w.value)
                if v > need.get(s, (0, 0))[0]:
                    need[s] = (v, 0)
            for s, (v, _) in need.items():
                if seen.get(s, 0) < v:
                    eng.wait_ge(s, v)
                    seen[s] = v
            ins = fn(eng)
            if t.used and t.q is self:
                ins.then_inc(self.sem, 1)


class DmaLine:

    def __init__(self, sem):
        self.sem, self.count = sem, 0

    def start(self, queue, out, in_, waits):
        self.count += 16
        t = Tok(self, self.count)
        t.value = self.count
        queue.add(lambda e: e.dma_start(out, in_).then_inc(self.sem, 16), waits)
        return t


class Buf:

    def __init__(self, ap):
        self.ap, self.free = ap, []

    def __getitem__(self, k):
        return self.ap[k]


class Ring:
    def __init__(self, aps):
        self.bufs, self.n = [Buf(a) for a in aps], 0

    def take(self):
        b = self.bufs[self.n % len(self.bufs)]
        self.n += 1
        return b


def program(nc, ins, out):
    SM, nsm = columns(SMALL)
    CN, ncn = columns(CONST)
    ctx = ExitStack()
    with ctx:
        def sb(name, cols):
            return ctx.enter_context(nc.sbuf_tensor(name, [P, cols], F32))

        def sem(name):
            return ctx.enter_context(nc.semaphore(name))

        pe, act, dve, pool, sp = (Queue(n, sem("s_" + n)) for n in ("pe", "act", "dve", "pool", "sp"))
        psum = [ctx.enter_context(nc.psum_tensor(f"ps{i}", [P, 512], F32)) for i in range(8)]

        wring = sb("wring", NSLOTS * 2048)
        sm_t = sb("sm", nsm)
        cn_t = sb("cn", ncn)
        R = sb("R", KB * L)[:, :].rearrange("p (k t) -> p k t", k=KB)
        H = sb("H", KB * L)[:, :].rearrange("p (k t) -> p k t", k=KB)
        ar = sb("arena", ARENA)
        used = [0]

        def arena(at, n):
            used[0] = max(used[0], at + n)
            assert at + n <= ARENA, (at, n)
            return ar[:, at:at + n]

        def sm(name, a=0, n=None):
            o, w = SM[name]
            return sm_t[:, o + a:o + a + (w - a if n is None else n)]

        def cn(name, a=0, n=None):
            o, w = CN[name]
            return cn_t[:, o + a:o + a + (w - a if n is None else n)]

        ident, ones = cn("ident"), cn("ones")

        lines = [DmaLine(sem(f"s_w{i}")) for i in range(NSLOTS)]
        slots = Ring([wring[:, i * 2048:(i + 1) * 2048] for i in range(NSLOTS)])

        def load(src):
            i = slots.n % NSLOTS
            b = slots.take()
            b.tok = lines[i].start(sp, b.ap, src, b.free)
            b.k = b.ap.rearrange("p (k n) -> p k n", k=KB)
            return b

        misc = [DmaLine(sem(f"s_m{i}")) for i in range(4)]
        t_cn = misc[0].start(act, cn_t[:, :], ins["cn"], [])
        t_sm = misc[1].start(act, sm_t[:, :], ins["small"], [])
        t_x = misc[2].start(act, R, ins["x"], [])

        def mm(out_ap, pairs, waits, start=True, stop=True, skip=False):
            def f(e):
                n = len(pairs)
                for i, (a, b) in enumerate(pairs):
                    r = e.matmul(out_ap, a, b, start=start and i == 0, stop=stop and i == n - 1,
                                 skip_group_check=skip)
                return r
            return pe.add(f, waits)

        def tr(out_ap, in_ap, waits, n=P):
            return pe.add(lambda e: e.transpose(out_ap, in_ap, cn_t[0:n, CN["ident"][0]:CN["ident"][0] + n]), waits)

        def actf(o, i, func, waits, **kw):
            return act.add(lambda e: e.activation(o, i, func, **kw), waits)

        def tt(q, o, a, b, op, waits):
            return q.add(lambda e: e.tensor_tensor(o, a, b, op), waits)

        def ts(q, o, a, s1, s2, op0, op1, waits):
            if s2 is None:
                return q.add(lambda e: e.tensor_scalar(o, a, s1, None, op0), waits)
            return q.add(lambda e: e.tensor_scalar(o, a, s1, s2, op0, op1), waits)

        def stt(o, a, s, b, op0, op1, waits):
            return dve.add(lambda e: e.scalar_tensor_tensor(out=o, in0=a, scalar=s, in1=b, op0=op0, op1=op1), waits)

        def copy(q, o, a, waits):
            if q is act:
                return actf(o, a, ACT.Copy, waits)
            return q.add(lambda e: e.tensor_copy(o, a), waits)

        def recip(o, a, waits):
            return dve.add(lambda e: e.reciprocal(o, a), waits)

        def memset(q, o, v, waits):
            return q.add(lambda e: e.memset(o, v), waits)

        def rmax(o, a, ax, waits):
            return dve.add(lambda e: e.tensor_reduce(o, a, ax, ALU.max), waits)

        banks = Ring([p[:, :] for p in psum])
        eps = cn("eps")
        s1r = Ring([sb(f"st{i}", 512)[:, :] for i in range(4)])

        def rstd(src, n, scale, waits):
            b = s1r.take()
            t1 = actf(b[:, 0:n], src, ACT.Sqrt, list(waits) + b.free + [t_cn], bias=eps, scale=scale)
            t2 = recip(b[:, 0:n], b[:, 0:n], [t1])
            return b, t1, t2

        sqr = Ring([sb(f"sq{i}", 512)[:, :] for i in range(2)])

        def norm(c0, gcol, t_src, shift=None, scale_toks=(), x=None, xo=None, t_war=()):
            x = R if x is None else x
            xo = H if xo is None else xo
            n = L - c0
            bk = banks.take()
            for k in range(KB):
                s = sqr.take()
                t = tt(pool if k % 2 else dve, s[:, 0:n], x[:, k, c0:L], x[:, k, c0:L], ALU.mult, list(t_src) + s.free)
                tm = mm(bk[:, 0:n], [(ones, s[:, 0:n])], [t, t_cn] + bk.free, start=k == 0, stop=k == KB - 1)
                s.free = [tm]
            rs, ta, tb = rstd(bk[:, 0:n], n, 1.0 / D, [tm])
            bk.free = [ta]
            out_t = None
            for k in range(KB):
                out_t = stt(xo[:, k, c0:L], x[:, k, c0:L], gcol(k), rs[:, 0:n], ALU.mult, ALU.mult,
                            [tb] + list(scale_toks) + list(t_war))
                if shift is not None:
                    out_t = ts(dve, xo[:, k, c0:L], xo[:, k, c0:L], shift(k), None, ALU.add, None, [out_t])
            rs.free = [out_t]
            return out_t

        csl = sb("csl", 8)
        mod = sb("mod", 48)
        t_cs = actf(csl[:, :], sm("c"), ACT.Silu, [t_sm])

        def ada(units):
            bk = banks.take()
            for n, u in enumerate(units):
                w = load(ins["w_ada"][u])
                for m in range(2):
                    col = 2 * n + m
                    t = mm(bk[:, col:col + 1], [(w.k[:, k, m * P:(m + 1) * P], csl[:, k:k + 1]) for k in range(KB)],
                           [w.tok, t_cs] + bk.free)
                w.free = [t]
            a, b = 2 * units[0], 2 * units[-1] + 2
            t2 = tt(dve, mod[:, a:b], bk[:, 0:b - a], sm("b_ada", a, b - a), ALU.add, [t, t_sm])
            bk.free = [t2]
            return t2

        t_mod1 = ada(range(0, 8))
        s1g = sb("s1g", 8)
        t = ts(dve, s1g[:, :], mod[:, 8:16], 1.0, None, ALU.add, None, [t_mod1])
        t_s1g = tt(dve, s1g[:, :], s1g[:, :], sm("g_mix"), ALU.mult, [t])
        t_h = norm(META, lambda k: s1g[:, k:k + 1], [t_x], shift=lambda k: mod[:, k:k + 1], scale_toks=[t_s1g])
        HX = H[:, :, META:L]

        def proj(w, m, o, waits, x=HX):
            return mm(o, [(w.k[:, k, m * P:(m + 1) * P], x[:, k, :]) for k in range(KB)], [w.tok] + list(waits))

        gb = sb("gb", 160)
        beta, gg, gc, egc, nbeg, kdf, tmp16 = (gb[:, 16 * i:16 * i + 16].rearrange("p (t h) -> p t h", t=2) for i in range(7))
        ea = gb[:, 112:120]
        tw = gb[:, 120:152]
        bk = banks.take()
        ba = bk[:, 0:32].rearrange("p (t c) -> p t c", t=2)
        wba = sm("w_ba").rearrange("p (k n) -> p k n", k=KB)
        for i in range(2):
            t = mm(ba[:, i, :], [(HX[:, k, i * P:(i + 1) * P], wba[:, k, :]) for k in range(KB)], [t_h, t_sm] + bk.free)
        t_e = actf(ea, sm("a_log"), ACT.Exp, [t_sm])
        t1 = actf(beta, ba[:, :, 0:8], ACT.Exp, [t], scale=-1.0)
        t2 = tt(dve, gg, ba[:, :, 8:16], sm("dt").unsqueeze(1).to_broadcast([P, 2, 8]), ALU.add, [t, t1])
        bk.free = [t2]
        t3 = ts(dve, beta, beta, 1.0, None, ALU.add, None, [t1])
        t_beta = recip(beta, beta, [t3])
        ab = tmp16
        t4 = actf(ab, gg, ACT.Abs, [t2])
        t5 = actf(ab, ab, ACT.Exp, [t4], scale=-1.0)
        t6 = actf(ab, ab, ACT.Ln, [t5], bias=1.0)
        t7 = stt(gg, gg, 0.0, ab, ALU.max, ALU.add, [t6])
        t8 = stt(gg, gg, -1.0, ea.unsqueeze(1).to_broadcast([P, 2, 8]), ALU.mult, ALU.mult, [t7, t_e])
        t_g = t8
        bk = banks.take()
        g2 = gb[:, 16:32]
        ta = mm(bk[:, 0:16], [(cn("tri"), g2)], [t_g] + bk.free)
        ta = mm(bk[:, 16:24], [(ones, gb[:, 16:24])], [t_g])
        t9 = copy(dve, gb[:, 32:48], bk[:, 0:16], [ta])
        t10 = tt(dve, kdf[:, 0, :], bk[:, 16:24], gc[:, 0, :], ALU.subtract, [t9])
        bk.free = [t10]
        t11 = actf(kdf[:, 0, :], kdf[:, 0, :], ACT.Exp, [t10])
        t12 = actf(egc, gc, ACT.Exp, [t9])
        t13 = stt(nbeg, egc, -1.0, beta, ALU.mult, ALU.mult, [t12, t_beta])
        t_gc, t_kdf, t_nbeg = t9, t11, t13

        QKV = arena(0, 6144).rearrange("p (b t) -> p b t", b=24)
        conv = sm("conv").rearrange("p (b j) -> p b j", b=24)
        t_qkv = [None] * 24
        for u in range(12):
            w = load(ins["w_in"][u])
            bk = banks.take()
            for m in range(2):
                t = proj(w, m, bk[:, m * T:(m + 1) * T], [t_h] + bk.free)
            w.free = [t]
            for m in range(2):
                b = 2 * u + m
                x = bk[:, m * T:(m + 1) * T]
                y = QKV[:, b, :]
                tc = ts(dve, y, x, conv[:, b, 3:4], None, ALU.mult, None, [t, t_sm])
                for j in range(1, 4):
                    tc = stt(y[:, j:T], x[:, 0:T - j], conv[:, b, 3 - j:4 - j], y[:, j:T], ALU.mult, ALU.add, [tc])
                t_qkv[b] = tc
            bk.free = [tc]
            ys = arena(2 * u * T, 2 * T)
            ts_ = actf(ys, ys, ACT.Silu, [tc])
            t_qkv[2 * u] = t_qkv[2 * u + 1] = ts_
        for u in range(8):
            ys = arena(2 * u * T, 2 * T)
            s = sqr.take()
            t = actf(s[:, :], ys, ACT.Square, [t_qkv[2 * u]] + s.free)
            bk = banks.take()
            tm = mm(bk[:, :], [(ones, s[:, :])], [t] + bk.free)
            s.free = [tm]
            rs, ta, tb = rstd(bk[:, :], 512, 1.0, [tm])
            bk.free = [ta]
            t = stt(ys, ys, float(P) ** -0.5 if u < 4 else 1.0, rs[:, :], ALU.mult, ALU.mult, [tb])
            rs.free = [t]
            t_qkv[2 * u] = t_qkv[2 * u + 1] = t

        base = 8192
        NB = 2
        work = []
        for s in range(NB):
            work.append({n: Buf(arena(base + (s * 9 + i) * 512, 512).rearrange("p (m j) -> p m j", m=4))
                         for i, n in enumerate(("A", "AT", "M", "N", "P", "UO", "D2", "QK", "X"))})
        base2 = base + NB * 9 * 512
        hw = [{n: Buf(arena(base2 + (s * 8 + i) * 128, 128)) for i, n in
               enumerate(("vb0", "vb1", "kd", "u0", "S1", "r1", "u1", "qd"))} for s in range(2)]
        base3 = base2 + 2 * 8 * 128
        Y = arena(base3, 2048).rearrange("p (h t) -> p h t", h=8)
        Z = arena(6144, 2048).rearrange("p (h t) -> p h t", h=8)
        base4 = base3 + 2048

        def q_(h, i):
            return QKV[:, h, i * P:(i + 1) * P]

        def k_(h, i):
            return QKV[:, 8 + h, i * P:(i + 1) * P]

        def v_(h, i):
            return QKV[:, 16 + h, i * P:(i + 1) * P]

        def bc4(x):
            return x.unsqueeze(1).to_broadcast([P, 4, P])

        def b4(bank):
            return bank.ap.rearrange("p (m j) -> p m j", m=4)

        def zproj(u):
            w = load(ins["w_in"][12 + u])
            bk = banks.take()
            for m in range(2):
                t = proj(w, m, bk[:, m * T:(m + 1) * T], [t_h] + bk.free)
            w.free = [t]
            t2 = actf(arena(6144 + 2 * u * T, 2 * T), bk[:, :], ACT.Silu, [t])
            bk.free = [t2]
            return t2

        t_z = [zproj(u) for u in range(4)]
        t_y = [None] * 8
        for half in range(2):
            grp = [(2 * half + s, work[s]) for s in range(NB)]
            st = {}
            for b, W in grp:
                heads = (2 * b, 2 * b + 1)
                mats = [(h, i) for h in heads for i in range(2)]
                tq = t_qkv[2 * b]
                tk = t_qkv[8 + 2 * b]
                kk, gbk = banks.take(), banks.take()
                for n, (h, i) in enumerate(mats):
                    t_kk = mm(kk[:, n * P:(n + 1) * P], [(k_(h, i), k_(h, i))], [tk] + kk.free)
                for n, (h, i) in enumerate(mats):
                    t_gb = mm(gbk[:, n * P:(n + 1) * P],
                              [(gg[:, i, h:h + 1].to_broadcast([P, P]), cn("tri"))], [t_g] + gbk.free)
                X, A, D2 = W["X"], W["A"], W["D2"]
                t_eg = []
                for n, (h, i) in enumerate(mats):
                    t = ts(dve, X[:, n, :], gbk[:, n * P:(n + 1) * P], gc[:, i, h:h + 1], None, ALU.subtract, None,
                           [t_gb, t_gc] + X.free)
                t1 = tt(pool, A[:, :, :], X[:, :, :], bc4(cn("pm1")), ALU.add, [t] + A.free)
                t2 = tt(dve, D2[:, :, :], X[:, :, :], bc4(cn("pm2")), ALU.subtract, [t] + D2.free)
                t1 = actf(A[:, :, :], A[:, :, :], ACT.Exp, [t1], scale=-1.0)
                t2 = actf(D2[:, :, :], D2[:, :, :], ACT.Exp, [t2])
                t_x = actf(X[:, :, :], b4(gbk), ACT.Exp, [t1, t2, t])
                gbk.free = [t, t_x]
                t3 = tt(dve, A[:, :, :], b4(kk), A[:, :, :], ALU.mult, [t1, t_kk])
                kk.free = [t3]
                for n, (h, i) in enumerate(mats):
                    t3b = ts(dve, A[:, n, :], A[:, n, :], beta[:, i, h:h + 1], None, ALU.mult, None, [t3, t_beta])
                atb = banks.take()
                for n in range(4):
                    t4 = tr(atb[:, n * P:(n + 1) * P], A[:, n, :], [t3b] + atb.free)
                AT, M, N, UO = W["AT"], W["M"], W["N"], W["UO"]
                t5 = copy(act, AT[:, :, :], b4(atb), [t4] + AT.free)
                atb.free = [t5]
                t6 = tt(pool, M[:, :, :], A[:, :, :], bc4(cn("lo1")), ALU.mult, [t3b] + M.free)
                t6 = tt(pool, M[:, :, :], bc4(ident), M[:, :, :], ALU.subtract, [t6])
                t7 = tt(dve, N[:, :, :], AT[:, :, :], bc4(cn("up1")), ALU.mult, [t5] + N.free)
                t7 = tt(dve, N[:, :, :], bc4(ident), N[:, :, :], ALU.subtract, [t7])
                t8 = tt(pool, UO[:, :, :], AT[:, :, :], bc4(cn("up2")), ALU.mult, [t5] + UO.free)
                qk = banks.take()
                for n, (h, i) in enumerate(mats):
                    t_qk = mm(qk[:, n * P:(n + 1) * P], [(k_(h, i), q_(h, i))], [tq, tk] + qk.free)
                QK = W["QK"]
                t9 = tt(dve, QK[:, :, :], b4(qk), D2[:, :, :], ALU.mult, [t_qk, t2] + QK.free)
                qk.free = [t9]
                D2.free = [t9]
                st[b] = dict(m=t6, n=t7, uo=t8, qk=t9, x=t_x, mats=mats)
            for s in LEVELS[1:]:
                last = s == 64
                for b, W in grp:
                    S = st[b]
                    M, N, UO, PB, AT = W["M"], W["N"], W["UO"], W["P"], W["AT"]
                    p1 = banks.take()
                    for n in range(4):
                        tp = mm(p1[:, n * P:(n + 1) * P], [(UO[:, n, :], M[:, n, :])], [S["uo"], S["m"]] + p1.free)
                    tpc = copy(act, PB[:, :, :], b4(p1), [tp] + PB.free)
                    p1.free = [tpc]
                    S["pc"], S["tp"] = tpc, tp
                    if not last:
                        S["uo2"] = tt(pool, UO[:, :, :], AT[:, :, :], bc4(cn(f"up{2 * s}")), ALU.mult, [tp])
                for b, W in grp:
                    S = st[b]
                    M, N, PB = W["M"], W["N"], W["P"]
                    p3 = banks.take()
                    for n in range(4):
                        tn = mm(p3[:, n * P:(n + 1) * P], [(PB[:, n, :], N[:, n, :])], [S["pc"], S["n"]] + p3.free)
                    if not last:
                        p2 = banks.take()
                        for n in range(4):
                            tmm = mm(p2[:, n * P:(n + 1) * P], [(N[:, n, :], PB[:, n, :])], [S["pc"], S["n"]] + p2.free)
                        t2 = tt(dve, M[:, :, :], M[:, :, :], b4(p2), ALU.subtract, [tmm, S["tp"]])
                        p2.free = [t2]
                        S["m"] = t2
                        PB.free = [tmm]
                        S["uo"] = S["uo2"]
                    else:
                        PB.free = [tn]
                        tmm = None
                    t3 = tt(dve, N[:, :, :], N[:, :, :], b4(p3), ALU.subtract, [tn, tmm])
                    p3.free = [t3]
                    S["n"] = t3
            for b, W in grp:
                S = st[b]
                W["A"].free = W["AT"].free = W["M"].free = W["UO"].free = [S["n"]]
            for b, W in grp:
                S = st[b]
                N, QK, X = W["N"], W["QK"], W["X"]
                hs = (2 * b, 2 * b + 1)
                t = {}
                for h in hs:
                    w_ = hw[h % 2]
                    n0 = 2 * (h % 2)
                    tb = banks.take()
                    ta = tr(tb[:, 0:P], v_(h, 0), [t_qkv[16 + h]] + tb.free)
                    ta = tr(tb[:, P:2 * P], v_(h, 1), [])
                    ta = tr(tb[:, 2 * P:3 * P], k_(h, 0), [t_qkv[8 + h]])
                    e0 = ts(dve, w_["vb0"].ap, tb[:, 0:P], beta[:, 0, h:h + 1], None, ALU.mult, None, [ta, t_beta] + w_["vb0"].free)
                    e1 = ts(dve, w_["vb1"].ap, tb[:, P:2 * P], beta[:, 1, h:h + 1], None, ALU.mult, None, [ta] + w_["vb1"].free)
                    e2 = ts(dve, w_["kd"].ap, tb[:, 2 * P:3 * P], kdf[:, 0, h:h + 1], None, ALU.mult, None, [ta, t_kdf] + w_["kd"].free)
                    tb.free = [e2]
                    e3 = tt(dve, w_["qd"].ap, q_(h, 1), X[:, n0 + 1, :], ALU.mult, [S["x"], t_qkv[h]] + w_["qd"].free)
                    t[h] = [e0, e1, e2, e3]
                for h in hs:
                    w_, n0 = hw[h % 2], 2 * (h % 2)
                    bu = banks.take()
                    a = mm(bu[:, 0:P], [(N[:, n0, :], w_["vb0"].ap)], [S["n"], t[h][0]] + bu.free)
                    w_["vb0"].free = [a]
                    c = copy(act, w_["u0"].ap, bu[:, 0:P], [a] + w_["u0"].free)
                    bu.free = [c]
                    t[h].append(c)
                for h in hs:
                    w_, n0 = hw[h % 2], 2 * (h % 2)
                    bu = banks.take()
                    a = mm(bu[:, 0:P], [(w_["kd"].ap, w_["u0"].ap)], [t[h][4], t[h][2]] + bu.free)
                    w_["kd"].free = [a]
                    c = copy(act, w_["S1"].ap, bu[:, 0:P], [a] + w_["S1"].free)
                    bu.free = [c]
                    t[h].append(c)
                for h in hs:
                    w_, n0 = hw[h % 2], 2 * (h % 2)
                    bu = banks.take()
                    a = mm(bu[:, 0:P], [(k_(h, 1), w_["S1"].ap)], [t[h][5]] + bu.free)
                    c = stt(w_["r1"].ap, bu[:, 0:P], nbeg[:, 1, h:h + 1], w_["vb1"].ap, ALU.mult, ALU.add,
                            [a, t_nbeg, t[h][1]] + w_["r1"].free)
                    bu.free = [c]
                    w_["vb1"].free = [c]
                    t[h].append(c)
                for h in hs:
                    w_, n0 = hw[h % 2], 2 * (h % 2)
                    bu = banks.take()
                    a = mm(bu[:, 0:P], [(N[:, n0 + 1, :], w_["r1"].ap)], [t[h][6]] + bu.free)
                    w_["r1"].free = [a]
                    c = copy(act, w_["u1"].ap, bu[:, 0:P], [a] + w_["u1"].free)
                    bu.free = [c]
                    t[h].append(c)
                W["N"].free = [a]
                for h in hs:
                    w_, n0 = hw[h % 2], 2 * (h % 2)
                    bo = banks.take()
                    a = mm(bo[:, 0:P], [(w_["u0"].ap, QK[:, n0, :])], [t[h][4], S["qk"]] + bo.free)
                    a = mm(bo[:, P:2 * P], [(w_["S1"].ap, w_["qd"].ap), (w_["u1"].ap, QK[:, n0 + 1, :])],
                           [t[h][7], t[h][3], t[h][5]])
                    for nm in ("u0", "S1", "qd", "u1"):
                        w_[nm].free = [a]
                    W["QK"].free = [a]
                    W["X"].free = [t[h][3]]
                    c = copy(act, Y[:, h, :], bo[:, 0:T], [a])
                    bo.free = [c]
                    s = sqr.take()
                    d = actf(s[:, 0:T], Y[:, h, :], ACT.Square, [c] + s.free)
                    bs = banks.take()
                    e = mm(bs[:, 0:T], [(ones, s[:, 0:T])], [d] + bs.free)
                    s.free = [e]
                    rs, f1, f2 = rstd(bs[:, 0:T], T, 1.0 / P, [e])
                    bs.free = [f1]
                    g1 = stt(Y[:, h, :], Y[:, h, :], sm("gdn_g"), rs[:, 0:T], ALU.mult, ALU.mult, [f2])
                    rs.free = [g1]
                    t_y[h] = tt(dve, Y[:, h, :], Y[:, h, :], Z[:, h, :], ALU.mult, [g1, t_z[h // 2]])

        t_mod2 = ada(range(8, 24))
        QD = arena(0, 6144).rearrange("p (b t) -> p b t", b=24)
        VD = arena(8192, 3072).rearrange("p (t n) -> p t n", t=2)
        t_fr = [t_y[7], t_y[6]]
        t_qd = [None] * 24
        for u in range(12):
            w = load(ins["w_in"][16 + u])
            bk = banks.take()
            for m in range(2):
                t = proj(w, m, bk[:, m * T:(m + 1) * T], [t_h] + bk.free)
            w.free = [t]
            ys = arena(2 * u * T, 2 * T)
            c = copy(act, ys, bk[:, :], [t] + t_fr)
            s = sqr.take()
            d = actf(s[:, :], bk[:, :], ACT.Square, [t] + s.free)
            bk.free = [d]
            bs = banks.take()
            e = mm(bs[:, :], [(ones, s[:, :])], [d] + bs.free)
            s.free = [e]
            rs, f1, f2 = rstd(bs[:, :], 512, 1.0 / P, [e])
            bs.free = [f1]
            t = stt(ys, ys, sm("dq_g" if u < 6 else "dk_g"), rs[:, :], ALU.mult, ALU.mult, [f2, c])
            rs.free = [t]
            t_qd[2 * u] = t_qd[2 * u + 1] = t
        t_vd = []
        for u in range(6):
            w = load(ins["w_in"][28 + u])
            bk = banks.take()
            for i in range(2):
                t = mm(bk[:, i * T:(i + 1) * T], [(HX[:, k, i * P:(i + 1) * P], w.k[:, k, :]) for k in range(KB)],
                       [w.tok, t_h] + bk.free)
            w.free = [t]
            c = copy(act if u % 2 else dve, VD[:, :, u * 256:(u + 1) * 256], bk.ap.rearrange("p (t n) -> p t n", t=2), [t] + t_fr)
            bk.free = [c]
            t_vd.append(c)
        YB = arena(6144, 1024).rearrange("p (h t) -> p h t", h=4)
        o = 11264
        pr = Ring([arena(o + i * 768, 768) for i in range(2)])
        ptr = Ring([arena(o + 1536 + i * 768, 768) for i in range(2)])
        str_ = Ring([sb(f"sms{i}", 8)[:, :] for i in range(4)])
        t_yb = []
        for s in range(NSLOT):
            yb = banks.take()
            for i in range(2):
                nk = P * (i + 1)
                b1 = banks.take()
                b2 = banks.take() if i else None
                where = []
                for g in range(NG):
                    h = g * NSLOT + s
                    o_ = (b2 if i and g == 2 else b1)
                    c0 = 0 if (i and g == 2) else g * nk
                    t = mm(o_[:, c0:c0 + nk], [(QD[:, h, i * P:(i + 1) * P], QD[:, 12 + h, 0:nk])],
                           [t_qd[h], t_qd[12 + h]] + o_.free)
                pb = pr.take()
                sc = float(P) ** -0.5
                dmk = cn("dm1") if i else cn("dm0")
                if i:
                    ta = stt(pb[:, 0:512], b1[:, 0:512], sc, dmk[:, 0:512], ALU.mult, ALU.add, [t] + pb.free)
                    tb = stt(pb[:, 512:768], b2[:, 0:256], sc, dmk[:, 512:768], ALU.mult, ALU.add, [t])
                    b1.free, b2.free = [ta], [tb]
                    n = 768
                else:
                    tb = stt(pb[:, 0:384], b1[:, 0:384], sc, dmk, ALU.mult, ALU.add, [t] + pb.free)
                    b1.free = [tb]
                    n = 384
                sv = str_.take()
                t = rmax(sv[:, 0:1], pb[:, 0:n], AX.X, [tb] + sv.free)
                t = ts(dve, sv[:, 1:2], sv[:, 0:1], -1.0, None, ALU.mult, None, [t])
                t = actf(pb[:, 0:n], pb[:, 0:n], ACT.Exp, [t], bias=sv[:, 1:2], accum_out=sv[:, 2:3])
                t = recip(sv[:, 3:4], sv[:, 2:3], [t])
                t = ts(dve, pb[:, 0:n], pb[:, 0:n], sv[:, 3:4], None, ALU.mult, None, [t])
                sv.free = [t]
                pt = ptr.take()
                nb = n // P
                c = None
                for j0 in range(0, nb, 4):
                    bt = banks.take()
                    j1 = min(nb, j0 + 4)
                    for j in range(j0, j1):
                        tx = tr(bt[:, (j - j0) * P:(j - j0 + 1) * P], pb[:, j * P:(j + 1) * P], [t] + bt.free)
                    c1 = copy(act, pt[:, j0 * P:j1 * P], bt[:, 0:(j1 - j0) * P], [tx] + pt.free)
                    bt.free = [c1]
                pb.free = [tx]
                pairs = []
                for g in range(NG):
                    h = g * NSLOT + s
                    for kt in range(i + 1):
                        j = g * (i + 1) + kt
                        pairs.append((VD[:, kt, h * P:(h + 1) * P], pt[:, j * P:(j + 1) * P]))
                t = mm(yb[:, i * P:(i + 1) * P], pairs, [c1] + t_vd + yb.free)
                pt.free = [t]
            c = copy(dve, YB[:, s, :], yb[:, 0:T], [t])
            yb.free = [c]
            t_yb.append(c)

        MG = arena(0, 2048).rearrange("p (m t) -> p m t", m=8)
        gr = Ring([arena(14336 + i * 512, 512) for i in range(4)])
        t_mg = None
        wd_ = None
        for u in range(4):
            gs = []
            for gi in range(2):
                w = load(ins["w_in"][(34 if gi == 0 else 38) + u])
                bk = banks.take()
                for m in range(2):
                    t = proj(w, m, bk[:, m * T:(m + 1) * T], [t_h] + bk.free)
                w.free = [t]
                g = gr.take()
                c = actf(g.ap, bk[:, :], ACT.Sigmoid, [t] + g.free)
                bk.free = [c]
                gs.append((g, c))
            w = load(ins["w_up_gdn"][u])
            bk = banks.take()
            for m in range(2):
                t = mm(bk[:, m * T:(m + 1) * T], [(w.k[:, k, m * P:(m + 1) * P], Y[:, k, :]) for k in range(KB)],
                       [w.tok] + t_y + bk.free)
            w.free = [t]
            ga, ta = gs[0]
            t1 = tt(dve, ga.ap, ga.ap, bk[:, :], ALU.mult, [t, ta])
            bk.free = [t1]
            if u % 2 == 0:
                wd_ = load(ins["w_up_dil"][u // 2])
            wk = wd_.ap.rearrange("p (k n) -> p k n", k=4)
            bk = banks.take()
            for m in range(2):
                c0 = ((u % 2) * 2 + m) * P
                t = mm(bk[:, m * T:(m + 1) * T], [(wk[:, k, c0:c0 + P], YB[:, k, :]) for k in range(4)],
                       [wd_.tok] + t_yb + bk.free)
            wd_.free = [t]
            gb_, tb = gs[1]
            t2 = tt(dve, gb_.ap, gb_.ap, bk[:, :], ALU.mult, [t, tb])
            bk.free = [t2]
            t_mg = tt(dve, MG[:, 2 * u:2 * u + 2, :], ga.ap.rearrange("p (m t) -> p m t", m=2),
                      gb_.ap.rearrange("p (m t) -> p m t", m=2), ALU.add, [t1, t2])
            ga.free = gb_.free = [t_mg]
        for u in range(4):
            w = load(ins["w_out"][u])
            bk = banks.take()
            for m in range(2):
                t = proj(w, m, bk[:, m * T:(m + 1) * T], [t_mg] + bk.free, x=MG)
            w.free = [t]
            for m in range(2):
                j = 2 * u + m
                t_r = stt(R[:, j, META:L], bk[:, m * T:(m + 1) * T], mod[:, 16 + j:17 + j], R[:, j, META:L],
                          ALU.mult, ALU.add, [t, t_mod2])
            bk.free = [t_r]

        t = ts(dve, s1g[:, :], mod[:, 32:40], 1.0, None, ALU.add, None, [t_mod2])
        t_s2 = tt(dve, s1g[:, :], s1g[:, :], sm("g_ffn"), ALU.mult, [t])
        t_h2 = norm(META, lambda k: s1g[:, k:k + 1], [t_r], shift=lambda k: mod[:, 24 + k:25 + k], scale_toks=[t_s2])
        rt = arena(0, 1024)
        sco = rt[:, 0:128].rearrange("p (t e) -> p t e", t=2)
        sel = rt[:, 128:256].rearrange("p (t e) -> p t e", t=2)
        cmb = rt[:, 256:384].rearrange("p (t e) -> p t e", t=2)
        mk = rt[:, 384:512].rearrange("p (t e) -> p t e", t=2)
        g8 = rt[:, 512:640].rearrange("p (t g e) -> p t g e", t=2, g=8)
        gs8 = rt[:, 640:656].rearrange("p (t g) -> p t g", t=2)
        m8 = rt[:, 656:672].rearrange("p (t g) -> p t g", t=2)
        gm = rt[:, 672:688].rearrange("p (t g) -> p t g", t=2)
        sm2 = rt[:, 688:692]
        CT = arena(1024, T)
        bk = banks.take()
        wr = sm("w_r").rearrange("p (k n) -> p k n", k=KB)
        for i in range(2):
            t = mm(bk[:, i * 64:(i + 1) * 64], [(HX[:, k, i * P:(i + 1) * P], wr[:, k, :]) for k in range(KB)], [t_h2] + bk.free)
        t = actf(sco, bk[:, 0:128].rearrange("p (t e) -> p t e", t=2), ACT.Sigmoid, [t])
        bk.free = [t]
        t = tt(dve, sel, sco, sm("rbias").unsqueeze(1).to_broadcast([P, 2, 64]), ALU.add, [t])
        for i in range(2):
            for g in range(8):
                tl = dve.add(lambda e, i=i, g=g: e.max(g8[:, i, g, :], sel[:, i, 8 * g:8 * g + 8]), [t])
        t = tt(dve, gs8, g8[:, :, :, 0], g8[:, :, :, 1], ALU.add, [tl])
        for i in range(2):
            tl = dve.add(lambda e, i=i: e.max(m8[:, i, :], gs8[:, i, :]), [t])
        t = dve.add(lambda e: e.memset(m8[:, :, 4:8], BIG), [tl])
        for i in range(2):
            tl = dve.add(lambda e, i=i: e.match_replace(gm[:, i, :], m8[:, i, :], gs8[:, i, :], -BIG), [t])
        t = ts(dve, gm, gm, -BIG, None, ALU.is_equal, None, [tl])
        gmb = gm.unsqueeze(3).to_broadcast([P, 2, 8, 8])
        mk4 = mk.rearrange("p t (g e) -> p t g e", g=8)
        t1 = tt(dve, mk4, sel.rearrange("p t (g e) -> p t g e", g=8), gmb, ALU.mult, [t])
        t2 = ts(dve, gm, gm, -1.0, BIG, ALU.add, ALU.mult, [t1])
        t = tt(dve, mk4, mk4, gmb, ALU.add, [t2])
        for i in range(2):
            tl = dve.add(lambda e, i=i: e.max(m8[:, i, :], mk[:, i, :]), [t])
        for i in range(2):
            t = dve.add(lambda e, i=i: e.match_replace(sel[:, i, :], m8[:, i, :], mk[:, i, :], 2 * BIG), [tl])
        t = ts(dve, sel, sel, 2 * BIG, None, ALU.is_equal, None, [t])
        t = tt(dve, cmb, sco, sel, ALU.mult, [t])
        t = dve.add(lambda e: e.tensor_reduce(sm2[:, 0:2], cmb, AX.X, ALU.add), [t])
        t = recip(sm2[:, 2:4], sm2[:, 0:2], [t])
        for i in range(2):
            t_c = ts(dve, cmb[:, i, :], cmb[:, i, :], sm2[:, 2 + i:3 + i], 2.5, ALU.mult, ALU.mult, [t])
        bk = banks.take()
        for i in range(2):
            t = tr(bk[0:64, i * P:(i + 1) * P], cmb[:, i, :], [t_c] + bk.free)
        t_ct = copy(dve, CT[0:64, :], bk[0:64, 0:T], [t])
        bk.free = [t_ct]

        acc = [banks.bufs[i] for i in range(4)]
        mb = Ring([p[:, :] for p in psum[4:8]])
        for i in range(4):
            mb.bufs[i].free = banks.bufs[4 + i].free
        ar_ = Ring([arena(2048 + i * 512, 512) for i in range(3)])
        cbs = Ring([arena(2048 + 1536 + i * 512, 512) for i in range(3)])
        acc_started = [False] * 4
        prev = None

        def down(e, a, ta, w, half):
            wk = w.ap.rearrange("p (f n) -> p f n", f=2)
            for j in range(KB):
                bi = j // 2
                for f in range(2):
                    st_ = not acc_started[bi]
                    acc_started[bi] = True
                    t = mm(acc[bi][:, (j % 2) * T:(j % 2 + 1) * T],
                           [(wk[:, f, j * P:(j + 1) * P], a[:, f * T:(f + 1) * T])],
                           [ta, w.tok] + acc[bi].free, start=st_, stop=(e == NE), skip=True)
            w.free = [t]
            a.free = [t]
            return t

        for e in range(NE + 1):
            wg = load(ins["w_eg"][e] if e < NE else ins["w_sg"])
            wu = load(ins["w_eu"][e] if e < NE else ins["w_su"])
            bg, bu = mb.take(), mb.take()
            for f in range(2):
                tg = proj(wg, f, bg[:, f * T:(f + 1) * T], [t_h2] + bg.free)
            wg.free = [tg]
            for f in range(2):
                tu = proj(wu, f, bu[:, f * T:(f + 1) * T], [t_h2] + bu.free)
            wu.free = [tu]
            wdn = load(ins["w_ed"][e] if e < NE else ins["w_sd"])
            a = ar_.take()
            t1 = actf(a.ap, bg[:, :], ACT.Silu, [tg] + a.free)
            bg.free = [t1]
            if prev is not None:
                down(*prev, 0)
            if e < NE:
                cb = cbs.take()
                bgc = bg
                tcb = mm(bgc[:, 0:T], [(cn_t[0:64, CN["ident"][0] + e:CN["ident"][0] + e + 1].to_broadcast([64, P]), CT[0:64, :])],
                         [t1, t_ct])
                tcc = copy(act, cb[:, 0:T], bgc[:, 0:T], [tcb] + cb.free)
                bgc.free = [tcc]
                t2 = tt(dve, a.ap, a.ap, bu[:, :], ALU.mult, [t1, tu])
                bu.free = [t2]
                t3 = tt(dve, a.ap.rearrange("p (f t) -> p f t", f=2), a.ap.rearrange("p (f t) -> p f t", f=2),
                        cb[:, 0:T].unsqueeze(1).to_broadcast([P, 2, T]), ALU.mult, [t2, tcc])
                cb.free = [t3]
            else:
                t3 = tt(dve, a.ap, a.ap, bu[:, :], ALU.mult, [t1, tu])
                bu.free = [t3]
            prev = (e, a, t3, wdn)
        t_acc = down(*prev, 0)
        for j in range(KB):
            t_r = stt(R[:, j, META:L], acc[j // 2][:, (j % 2) * T:(j % 2 + 1) * T], mod[:, 40 + j:41 + j], R[:, j, META:L],
                      ALU.mult, ALU.add, [t_acc])
            acc[j // 2].free = [t_r]
        for i in range(4):
            banks.bufs[4 + i].free = mb.bufs[i].free + [t_acc]

        n2 = sm("norm2").rearrange("p (i k) -> p i k", i=8)

        def one(bk):
            return bk[:, 0:L]

        BIGB = arena(0, 32 * L).rearrange("p (b t) -> p b t", b=32)
        OT = arena(32 * L, KB * L).rearrange("p (b t) -> p b t", b=KB)
        MT = arena(40 * L, KB * L).rearrange("p (b t) -> p b t", b=KB)
        o2 = 48 * L

        def project_all(wname, u0, nu, x, tx, evac):
            for u in range(nu):
                w = load(ins[wname][u0 + u])
                for m in range(2):
                    bk = banks.take()
                    t = proj(w, m, one(bk), list(tx) + bk.free, x=x)
                    bk.free = evac(2 * u + m, one(bk), t)
                w.free = [t]

        def mixer_out(layer, x, tx, gi, c0=0):
            toks = []

            def ev(b, ps, t):
                c = copy(act if b % 2 else dve, MT[:, b, :], ps, [t])
                toks.append(c)
                return [c]
            project_all("w_out2", 4 * layer, 4, x, tx, ev)
            t = norm(0, lambda k: n2[:, gi, k:k + 1], toks, x=MT, xo=MT, t_war=[])
            for k in range(KB):
                t2 = tt(dve if k % 2 else pool, R[:, k, :], R[:, k, :], MT[:, k, :], ALU.add, [t])
                toks.append(t2)
            return toks[-2:]

        def mlp(layer, tr_, c0):
            th = norm(0, lambda k: n2[:, 4 * layer + 2, k:k + 1], tr_)
            n = L - c0
            toks = []

            def ev(b, ps, t):
                c = actf(BIGB[:, b, c0:L], ps[:, 0:n], ACT.Relu, [t])
                c2 = tt(dve, BIGB[:, b, c0:L], BIGB[:, b, c0:L], ps[:, 0:n], ALU.mult, [c])
                toks.append(c2)
                return [c2]
            for u in range(16):
                w = load(ins["w_up2"][16 * layer + u])
                for m in range(2):
                    bk = banks.take()
                    t = proj(w, m, bk[:, 0:n], [th] + bk.free, x=H[:, :, c0:L])
                    bk.free = ev(2 * u + m, bk[:, 0:n], t)
                w.free = [t]
            dt_ = []
            for g in range(4):
                bks = [banks.take(), banks.take()]
                for kc in range(4):
                    w = load(ins["w_down2"][(4 * layer + g) * 4 + kc])
                    for m in range(2):
                        t = mm(bks[m][:, 0:n], [(w.k[:, k, m * P:(m + 1) * P], BIGB[:, 8 * kc + k, c0:L]) for k in range(KB)],
                               [w.tok, toks[8 * kc + 7]] + bks[m].free, start=kc == 0, stop=kc == 3)
                    w.free = [t]
                for m in range(2):
                    c = copy(act if m else dve, MT[:, 2 * g + m, c0:L], bks[m][:, 0:n], [t])
                    bks[m].free = [c]
                    dt_.append(c)
            t = norm(c0, lambda k: n2[:, 4 * layer + 3, k:k + 1], dt_, x=MT, xo=MT)
            r = []
            for k in range(KB):
                r.append(tt(dve if k % 2 else pool, R[:, k, c0:L], R[:, k, c0:L], MT[:, k, c0:L], ALU.add, [t]))
            return r[-2:]

        t_hh = norm(0, lambda k: n2[:, 0, k:k + 1], [t_r])
        lm = sb("lm", 8)
        lv = sm("lam").rearrange("p (a d) -> p a d", a=4)
        s = sqr.take()
        sv_ = s[:, 0:128].rearrange("p (a d) -> p a d", a=2)
        lv2 = sm("lam").rearrange("p (a b d) -> p a b d", a=2, b=2)
        t = tt(dve, sv_, lv2[:, :, 0, :], lv2[:, :, 1, :], ALU.mult, [t_sm] + s.free)
        t = dve.add(lambda e: e.tensor_reduce(lm[:, 0:2], sv_, AX.X, ALU.add), [t])
        s.free = [t]
        t = actf(lm[:, 0:2], lm[:, 0:2], ACT.Exp, [t])
        t = tt(dve, lm[:, 2:3], lm[:, 0:1], lm[:, 1:2], ALU.subtract, [t])
        t_lam = ts(dve, lm[:, 2:3], lm[:, 2:3], LAM0, None, ALU.add, None, [t])
        t_sub = ts(dve, lm[:, 3:4], sm("subln"), 1.0 - LAM0, None, ALU.mult, None, [t_sm])

        tqk = [None] * 16

        def ev_qk(b, ps, t):
            c = actf(BIGB[:, b, :], ps, ACT.Copy, [t], scale=0.125 if b < 8 else 1.0)
            tqk[b] = c
            return [c]
        t_r_all = [t_r]
        project_all("w_in2", 0, 8, H, [t_hh], ev_qk)
        VV = arena(16 * L, 3 * 1024).rearrange("p (t n) -> p t n", t=3)
        QT = [(0, 16), (16, 128), (144, 128)]
        t_vz = memset(pool, VV[:, 0, :], 0.0, [t_r])
        t_vv = []
        for u in range(4):
            w = load(ins["w_in2"][8 + u])
            for i, (q0, nq) in enumerate(QT):
                bk = banks.take()
                t = mm(bk[0:nq, 0:256], [(H[:, k, q0:q0 + nq], w.k[:, k, :]) for k in range(KB)], [w.tok, t_hh] + bk.free)
                c = copy(dve, VV[0:nq, i, u * 256:(u + 1) * 256], bk[0:nq, 0:256], [t, t_vz])
                bk.free = [c]
                t_vv.append(c)
            w.free = [t]
        o3 = 48 * L
        ps_ = Ring([arena(o3 + i * 544, 544).rearrange("p (c k) -> p c k", c=2) for i in range(3)])
        at_ = Ring([arena(o3 + 1632 + i * 384, 384).rearrange("p (j q) -> p j q", j=3) for i in range(2)])
        for b in at_.bufs:
            b.free = [memset(pool, b[:, 0, :], 0.0, [t_r])]
        obanks, sbanks = Ring([]), Ring([])
        obanks.bufs, sbanks.bufs = banks.bufs[0:2], banks.bufs[2:8]
        t_ot = []
        for h in range(NH):
            slope = 2.0 ** (-(h + 1))
            ob = obanks.take()
            for i, (q0, nq) in enumerate(QT):
                nk = q0 + nq
                bc = [sbanks.take(), sbanks.take()]
                for c in range(2):
                    t = mm(bc[c][0:nq, 0:nk], [(BIGB[64 * c:64 * c + 64, h, q0:q0 + nq], BIGB[64 * c:64 * c + 64, 8 + h, 0:nk])],
                           [tqk[h], tqk[8 + h]] + bc[c].free)
                pb = ps_.take()
                for c in range(2):
                    tb = stt(pb[0:nq, c, 0:nk], cn(f"nd{i}")[0:nq, :], slope, bc[c][0:nq, 0:nk], ALU.mult, ALU.add, [t] + pb.free)
                    bc[c].free = [tb]
                sv = str_.take()
                t = rmax(sv[0:nq, 0:2], pb[0:nq, :, 0:nk], AX.X, [tb] + sv.free)
                t = ts(dve, sv[0:nq, 2:4], sv[0:nq, 0:2], -1.0, None, ALU.mult, None, [t])
                for c in range(2):
                    te = actf(pb[0:nq, c, 0:nk], pb[0:nq, c, 0:nk], ACT.Exp, [t], bias=sv[0:nq, 2 + c:3 + c],
                              accum_out=sv[0:nq, 4 + c:5 + c])
                t = recip(sv[0:nq, 6:8], sv[0:nq, 4:6], [te])
                t = ts(dve, sv[0:nq, 7:8], sv[0:nq, 7:8], lm[0:nq, 2:3], None, ALU.mult, None, [t, t_lam])
                t1 = ts(dve, pb[0:nq, 1, 0:nk], pb[0:nq, 1, 0:nk], sv[0:nq, 7:8], None, ALU.mult, None, [t])
                t1 = stt(pb[0:nq, 0, 0:nk], pb[0:nq, 0, 0:nk], sv[0:nq, 6:7], pb[0:nq, 1, 0:nk], ALU.mult, ALU.subtract, [t1])
                sv.free = [t1]
                bt = sbanks.take()
                for j in range(i + 1):
                    k0, n_ = QT[j]
                    tx = tr(bt[0:n_, j * P:j * P + nq], pb[0:nq, 0, k0:k0 + n_], [t1] + bt.free, n=nq)
                at = at_.take()
                c1 = copy(act, at[0:16, 0, 0:nq], bt[0:16, 0:nq], [tx] + at.free)
                if i:
                    c1 = copy(act, at[:, 1:i + 1, 0:nq], bt[:, P:(i + 1) * P].rearrange("p (j q) -> p j q", j=i), [tx])
                bt.free = [c1]
                pb.free = [tx]
                t = mm(ob[:, q0:q0 + nq], [(VV[:, j, h * P:(h + 1) * P], at[:, j, 0:nq]) for j in range(i + 1)],
                       [c1] + t_vv + ob.free)
                at.free = [t]
            c = copy(act, OT[:, h, :], one(ob), [t])
            s = sqr.take()
            d = actf(s[:, 0:L], one(ob), ACT.Square, [t] + s.free)
            ob.free = [d]
            bs = sbanks.take()
            e = mm(bs[:, 0:L], [(ones, s[:, 0:L])], [d] + bs.free)
            s.free = [e]
            rs, f1, f2 = rstd(bs[:, 0:L], L, 1.0 / P, [e])
            bs.free = [f1]
            t = stt(OT[:, h, :], OT[:, h, :], lm[:, 3:4], rs[:, 0:L], ALU.mult, ALU.mult, [f2, c, t_sub])
            rs.free = [t]
            t_ot.append(t)
        tr_ = mixer_out(0, OT, [t_ot[-1]], 1)
        tr_ = mlp(0, tr_, 0)

        t_hh = norm(0, lambda k: n2[:, 4, k:k + 1], tr_)
        tb_ = [None] * 24

        def ev_b(b, ps, t):
            c = copy(act, BIGB[:, b, :], ps, [t])
            tb_[b] = c
            return [c]
        cv = sm("conv2").rearrange("p (b j) -> p b j", b=8)
        project_all("w_in2", 12, 12, H, [t_hh], ev_b)
        for k in range(KB):
            u_, y_ = BIGB[:, 16 + k, :], BIGB[:, 24 + k, :]
            t = tt(pool, u_, u_, BIGB[:, 8 + k, :], ALU.mult, [tb_[8 + k], tb_[16 + k]])
            t = ts(dve, y_, u_, cv[:, k, 2:3], None, ALU.mult, None, [t])
            for j in (1, 2):
                t = stt(y_[:, j:L], u_[:, 0:L - j], cv[:, k, 2 - j:3 - j], y_[:, j:L], ALU.mult, ALU.add, [t])
            t = tt(dve, OT[:, k, :], y_, BIGB[:, k, :], ALU.mult, [t, tb_[k]])
        tr_ = mixer_out(1, OT, [t], 5)
        tr_ = mlp(1, tr_, META)
        t_out = misc[3].start(sp, out, R[:, :, META:L], tr_)
        sp.ops.append((None, [t_out], Tok(sp, len(sp.ops))))

        for q in (pe, act, dve, pool, sp):
            q.number()
        block = ctx.enter_context(nc.Block())

        @block.tensor
        def _(e):
            pe.emit(e)

        @block.scalar
        def _(e):
            act.emit(e)

        @block.vector
        def _(e):
            dve.emit(e)

        @block.gpsimd
        def _(e):
            pool.emit(e)

        @block.sync
        def _(e):
            sp.ops.pop()
            sp.emit(e)
            e.wait_ge(t_out.q.sem, t_out.value)


def tile_weights(w, cols=256):
    K, N = w.shape
    return np.ascontiguousarray(w.reshape(K // P, P, N // cols, cols).transpose(2, 1, 0, 3)).reshape(N // cols, P, -1)


def by_feature(v):
    v = np.asarray(v)
    return v.reshape(-1, P).T


def kernel(**inputs):
    import concourse.bacc as bacc
    from concourse.bass_utils import run_bass_kernel_spmd

    a = {k: np.asarray(v) for k, v in inputs.items()}
    wi = a["w_in"][0]
    q3, z, ba, rest = wi[:, :3072], wi[:, 3072:4096], wi[:, 4096:4112], wi[:, 4112:]
    w_in = np.concatenate([tile_weights(x) for x in (q3, z, rest)])
    every = lambda v: np.broadcast_to(np.asarray(v).reshape(1, -1), (P, v.size))
    small = {
        "c": by_feature(a["c"][0]), "b_ada": by_feature(a["b_ada"][0]), "g_mix": by_feature(a["g_mix"][0]),
        "g_ffn": by_feature(a["g_ffn"][0]),
        "conv": a["gdn_conv_w"][0].reshape(4, 24, P).transpose(2, 1, 0).reshape(P, 96),
        "gdn_g": a["gdn_norm_g"].reshape(P, 1), "dq_g": a["dil_q_norm_g"].reshape(P, 1),
        "dk_g": a["dil_k_norm_g"].reshape(P, 1),
        "norm2": by_feature(a["norm_g_2"]),
        "conv2": a["conv_w_2"][0].reshape(3, 8, P).transpose(2, 1, 0).reshape(P, 24),
        "subln": a["subln_g_2"].reshape(P, 1), "a_log": every(a["gdn_a_log"]), "dt": every(a["gdn_dt_bias"]),
        "rbias": every(a["router_bias"]), "lam": every(a["lambda_params_2"]),
        "w_ba": ba.reshape(8, P, 16).transpose(1, 0, 2).reshape(P, 128),
        "w_r": a["w_router"][0].reshape(8, P, 64).transpose(1, 0, 2).reshape(P, 512),
    }
    x = np.concatenate([a["meta_tokens_2"], a["x"][0]], axis=0)
    arrays = {
        "x": x.T.reshape(8, P, L).transpose(1, 0, 2),
        "small": np.concatenate([small[n] for n, _ in SMALL], axis=1),
        "cn": constants(),
        "w_ada": tile_weights(a["w_ada"][0]),
        "w_in": w_in,
        "w_up_gdn": tile_weights(a["w_up_gdn"][0]),
        "w_up_dil": tile_weights(a["w_up_dil"][0], 512),
        "w_out": tile_weights(a["w_out"][0]),
        "w_eg": a["w_exp_gate"][0].reshape(NE, 8, P, 256).transpose(0, 2, 1, 3).reshape(NE, P, 2048),
        "w_eu": a["w_exp_up"][0].reshape(NE, 8, P, 256).transpose(0, 2, 1, 3).reshape(NE, P, 2048),
        "w_ed": a["w_exp_down"][0].reshape(NE, 2, P, 1024).transpose(0, 2, 1, 3).reshape(NE, P, 2048),
        "w_sg": tile_weights(a["w_sh_gate"][0])[0],
        "w_su": tile_weights(a["w_sh_up"][0])[0],
        "w_sd": tile_weights(a["w_sh_down"][0], 1024)[0],
        "w_in2": np.concatenate([tile_weights(a["w_in_2"][i]) for i in range(2)]),
        "w_out2": np.concatenate([tile_weights(a["w_out_2"][i]) for i in range(2)]),
        "w_up2": np.concatenate([tile_weights(a["w_up_2"][i]) for i in range(2)]),
        "w_down2": np.ascontiguousarray(a["w_down_2"].reshape(2, 4, 8, P, 4, 256).transpose(0, 4, 1, 3, 2, 5)).reshape(32, P, 2048),
    }
    nc = bacc.Bacc("TRN2", target_bir_lowering=False, num_devices=1)
    arrays = {f"in_{k}": np.ascontiguousarray(v) for k, v in arrays.items()}
    ins = {k[3:]: nc.dram_tensor(k, v.shape, F32, kind="ExternalInput").ap() for k, v in arrays.items()}
    out = nc.dram_tensor("out_0", (P, KB, T), F32, kind="ExternalOutput").ap()
    program(nc, ins, out)
    r = run_bass_kernel_spmd(nc, [arrays], core_ids=[0])
    y = r.results[0]["out_0"]
    return y.transpose(1, 0, 2).reshape(D, T).T.reshape(1, T, D)
```

```python
from contextlib import ExitStack

import concourse.bass as bass
import numpy as np
from concourse import mybir

ALU = mybir.AluOpType
ACT = mybir.ActivationFunctionType
AX = mybir.AxisListType
F32 = mybir.dt.float32
F32R = mybir.dt.float32r

P = 128
D = 1024
KB = 8
T = 256
META = 16
L = T + META
NH = 8
NSLOT = 4
NG = 3
NE = 64
DFF = 4096
EPS = 1e-6
BIG = 1e30
LAM0 = 0.2
RAW = 4
SMALL = [("c", 8), ("b_ada", 48), ("g_mix", 8), ("g_ffn", 8), ("conv", 96), ("gdn_g", 1),
         ("dq_g", 1), ("dk_g", 1), ("norm2", 64), ("conv2", 24), ("subln", 1),
         ("a_log", 8), ("dt", 8), ("rbias", 64)]
LEVELS = [1, 2, 4, 8, 16, 32, 64]
CONST = {"cn": [("ident", 128), ("ones", 128), ("tri", 128), ("eps", 1)],
         "cg": [("pm1", 128), ("pm2", 128), ("lo1", 128)] + [(f"up{s}", 128) for s in LEVELS],
         "cd": [("dm0", 384), ("dm1", 768)],
         "c2": [("nd0", 16), ("nd1", 144), ("nd2", 272)]}


def columns(table):
    at, out = 0, {}
    for name, n in table:
        out[name] = (at, n)
        at += n
    return out, at


def constants():
    i = np.arange(P)[:, None]
    j = np.arange(P)[None, :]
    k2 = np.arange(2 * P)[None, :]

    def low(a, b, s):
        return (a // (2 * s) == b // (2 * s)) & (a // s % 2 == 1) & (b // s % 2 == 0)

    def dil(q, k, g):
        dist = q - k
        ok = (dist >= 0) & ((dist <= 128) if g == 0 else (dist % (4 if g == 1 else 16) == 0))
        return np.where(ok, 0.0, -BIG)

    def away(q0, nk):
        dist = (i + q0) - np.arange(nk)[None, :]
        return np.where(dist >= 0, -dist, -BIG)

    parts = {
        "cn": [np.eye(P), np.ones((P, P)), i <= j, np.full((P, 1), EPS)],
        "cg": [np.where(j < i, 0.0, BIG), np.where(i <= j, 0.0, BIG), low(i, j, 1)] + [low(j, i, s) for s in LEVELS],
        "cd": [dil(i, j, g) for g in range(NG)] + [dil(i + P, k2, g) for g in range(NG)],
        "c2": [away(0, 16), away(16, 144), away(144, 272)],
    }
    return {n: np.concatenate(p, axis=1).astype(np.float32) for n, p in parts.items()}


class Tok:

    def __init__(self, q, n):
        self.q, self.n, self.used = q, n, False


class Queue:

    def __init__(self, name, sem):
        self.name, self.sem, self.ops = name, sem, []

    def add(self, fn, waits):
        t = Tok(self, len(self.ops))
        for w in waits:
            if w is not None:
                w.used = True
        self.ops.append((fn, [w for w in waits if w is not None], t))
        return t

    def number(self):
        n = 0
        for _, _, t in self.ops:
            if t.used and t.q is self:
                n += 1
            t.value = n

    def emit(self, eng):
        seen = {}
        for fn, waits, t in self.ops:
            need = {}
            for w in waits:
                s, v = (w.q.sem, w.value)
                if v > need.get(s, (0, 0))[0]:
                    need[s] = (v, 0)
            for s, (v, _) in need.items():
                if seen.get(s, 0) < v:
                    eng.wait_ge(s, v)
                    seen[s] = v
            ins = fn(eng)
            if t.used and t.q is self:
                ins.then_inc(self.sem, 1)


class DmaLine:

    def __init__(self, sem):
        self.sem, self.count = sem, 0

    def start(self, queue, out, in_, waits):
        self.count += 16
        t = Tok(self, self.count)
        t.value = self.count
        queue.add(lambda e: e.dma_start(out, in_).then_inc(self.sem, 16), waits)
        return t


class Buf:

    def __init__(self, ap):
        self.ap, self._free, self.held = ap, [], False

    def __getitem__(self, k):
        return self.ap[k]

    @property
    def free(self):
        return self._free

    @free.setter
    def free(self, toks):
        self._free, self.held = list(toks), False


class Ring:
    def __init__(self, aps):
        self.bufs, self.n = [Buf(a) for a in aps], 0

    def take(self):
        for _ in self.bufs:
            b = self.bufs[self.n % len(self.bufs)]
            self.n += 1
            if not b.held:
                b.held = True
                return b
        raise AssertionError("every buffer is held")


def stream_plan():
    out = [("w_ada", n) for n in range(8)]
    for p in range(4):
        for j, n in enumerate((p, 4 + p, 8 + p, 12 + p)):
            out += [("w_in", n), ("w_ada", 8 + 4 * p + j)]
    out += [("w_in", n) for n in range(16, 38)] + [("w_up_gdn", n) for n in range(4)]
    out += [("w_in", n) for n in range(38, 42)] + [("w_up_dil", n) for n in range(2)] + [("w_out", n) for n in range(4)]
    for e in range(NE + 1):
        out += [("w_eg", e), ("w_eu", e)]
        if e:
            out.append(("w_ed", e - 1))
    out.append(("w_ed", NE))
    for p in range(4):
        out += [("w_in2", p), ("w_in2", 4 + p), ("w_in2", 8 + p)]
    for i in range(2):
        out += [("w_out2", 4 * i + n) for n in range(4)]
        out += [("w_up2", 16 * i + n) for n in range(16)] + [("w_down2", 16 * i + n) for n in range(16)]
        if i == 0:
            out += [("w_in2", 12 + 4 * j + p) for p in range(4) for j in range(3)]
    return out


def weave(main, side, num, den):
    n = 0
    for _ in main:
        n += num
        while n >= den:
            n -= den
            next(side, None)


def drain(g):
    for _ in g:
        pass


def program(nc, ins, out):
    SM, nsm = columns(SMALL)
    CN, ncn = columns(CONST["cn"])
    ctx = ExitStack()
    with ctx:
        def sb(name, cols, dt=F32, scope=ctx):
            return scope.enter_context(nc.sbuf_tensor(name, [P, cols], dt))

        def sbr(name, cols, scope=ctx):
            return sb(name + "_h", cols, F32R, scope)[:, :], sb(name + "_l", cols, F32R, scope)[:, :]

        def sem(name):
            return ctx.enter_context(nc.semaphore(name))

        pe, act, dve, pool, sp = (Queue(n, sem("s_" + n)) for n in ("pe", "act", "dve", "pool", "sp"))
        psum = [ctx.enter_context(nc.psum_tensor(f"ps{i}", [P, 512], F32)) for i in range(8)]

        raw = sb("wraw", RAW * 2048)
        sm_t = sb("sm", nsm)
        cn_t = sb("cn", ncn)
        R = sb("R", KB * L)[:, :].rearrange("p (k t) -> p k t", k=KB)
        HH, HL = (a.rearrange("p (k t) -> p k t", k=KB) for a in sbr("H", KB * L))
        YR = sbr("Y", KB * L)
        wpair = [sbr(f"w{i}", 2048) for i in range(2)]

        def sm(name, a=0, n=None):
            o, w = SM[name]
            return sm_t[:, o + a:o + a + (w - a if n is None else n)]

        def cn(name, a=0, n=None):
            o, w = CN[name]
            return cn_t[:, o + a:o + a + (w - a if n is None else n)]

        ident, ones = cn("ident"), cn("ones")

        def fetch(name, scope, waits):
            table, total = columns(CONST[name])
            t_ = sb("k" + name, total, scope=scope)

            def get(n):
                o, w = table[n]
                return t_[:, o:o + w]
            get.tok = DmaLine(sem("s_" + name)).start(sp, t_[:, :], ins[name], waits)
            return get

        def fetch_all(name, cols, scope, waits):
            t_ = sb("k" + name, cols, scope=scope)[:, :]
            return t_, DmaLine(sem("s_" + name)).start(sp, t_, ins[name], waits)

        misc = [DmaLine(sem(f"s_m{i}")) for i in range(4)]
        t_sm = misc[1].start(act, sm_t[:, :], ins["small"], [])
        t_x = misc[2].start(act, R, ins["x"], [])
        t_cn = misc[0].start(act, cn_t[:, :], ins["cn"], [])

        plan = stream_plan()
        lines = [DmaLine(sem(f"s_w{i}")) for i in range(RAW)]
        raws = [Buf(raw[:, i * 2048:(i + 1) * 2048]) for i in range(RAW)]
        state = {"at": 0, "loaded": 0, "split": 0, "pairs": 0, "used": 0}
        units = {}

        def source(name, n):
            if n == NE and name in ("w_eg", "w_eu", "w_ed"):
                return ins[{"w_eg": "w_sg", "w_eu": "w_su", "w_ed": "w_sd"}[name]]
            return ins[name][n]

        class Unit:
            pass

        def f32(ap):
            return ap.bitcast(F32)

        def weights(*key):
            n = state["at"]
            assert plan[n] == key, (plan[n], key)
            state["at"] += 1
            while state["loaded"] < min(len(plan), n + RAW):
                m = state["loaded"]
                b = raws[m % RAW]
                u = units[m] = Unit()
                u.raw, u.k = b, b.ap.rearrange("p (k n) -> p k n", k=KB)
                u.tok = lines[m % RAW].start(sp, b.ap, source(*plan[m]), b.free)
                state["loaded"] += 1
            m = state["split"]
            while m < min(len(plan), n + RAW):
                if plan[m][0] != "w_ada":
                    if state["pairs"] - state["used"] == 2:
                        break
                    u = units[m]
                    i = state["pairs"] % 2
                    state["pairs"] += 1
                    u.h, u.l = wpair[i]
                    before = pair_free[i]
                    th = copy(act, u.h, u.raw.ap, [u.tok] + before)
                    u.split = tt(dve, u.l, u.raw.ap, f32(u.h), ALU.subtract, [th] + before)
                    u.raw.free = [u.split]
                    u.i = i
                m += 1
            state["split"] = m
            return units.pop(n)

        pair_free = [[], []]

        def used_up(u, t):
            if hasattr(u, "i"):
                pair_free[u.i] = [t]
                state["used"] += 1
            else:
                u.raw.free = [t]

        def block_of(u, k, c0, n=P, parts=KB):
            w = 2048 // parts
            return u.h[:, k * w + c0:k * w + c0 + n], u.l[:, k * w + c0:k * w + c0 + n]

        def mm(out_ap, pairs, waits, start=True, stop=True, skip=False):
            def f(e):
                n = len(pairs)
                for i, (a, b) in enumerate(pairs):
                    r = e.matmul(out_ap, a, b, start=start and i == 0, stop=stop and i == n - 1,
                                 skip_group_check=skip)
                return r
            return pe.add(f, waits)

        def mm3(out_ap, pairs, waits, start=True, stop=True, skip=False):
            ab = []
            for (ah, al), (bh, bl) in pairs:
                ab += [(ah, bh), (ah, bl), (al, bh)]
            return mm(out_ap, ab, waits, start, stop, skip)

        def two(pair, *idx):
            return pair[0][idx], pair[1][idx]

        def tr(out_ap, in_ap, waits, n=P):
            return pe.add(lambda e: e.transpose(out_ap, in_ap, cn_t[0:n, CN["ident"][0]:CN["ident"][0] + n]), waits)

        def actf(o, i, func, waits, **kw):
            return act.add(lambda e: e.activation(o, i, func, **kw), waits)

        def tt(q, o, a, b, op, waits):
            return q.add(lambda e: e.tensor_tensor(o, a, b, op), waits)

        def ts(q, o, a, s1, s2, op0, op1, waits):
            if s2 is None:
                return q.add(lambda e: e.tensor_scalar(o, a, s1, None, op0), waits)
            return q.add(lambda e: e.tensor_scalar(o, a, s1, s2, op0, op1), waits)

        def stt(o, a, s, b, op0, op1, waits):
            return dve.add(lambda e: e.scalar_tensor_tensor(out=o, in0=a, scalar=s, in1=b, op0=op0, op1=op1), waits)

        def copy(q, o, a, waits):
            if q is act:
                return actf(o, a, ACT.Copy, waits)
            return q.add(lambda e: e.tensor_copy(o, a), waits)

        def recip(o, a, waits):
            return dve.add(lambda e: e.reciprocal(o, a), waits)

        def memset(q, o, v, waits):
            return q.add(lambda e: e.memset(o, v), waits)

        def rmax(o, a, ax, waits):
            return dve.add(lambda e: e.tensor_reduce(o, a, ax, ALU.max), waits)

        banks = Ring([p[:, :] for p in psum])
        eps = cn("eps")
        s1r = Ring([sb(f"st{i}", 512)[:, :] for i in range(4)])

        def rstd(src, n, scale, waits):
            b = s1r.take()
            t1 = actf(b[:, 0:n], src, ACT.Sqrt, list(waits) + b.free + [t_cn], bias=eps, scale=scale)
            t2 = recip(b[:, 0:n], b[:, 0:n], [t1])
            return b, t1, t2

        def split(oh, ol, src, waits, q=act):
            th = copy(q, oh, src, waits)
            return tt(dve, ol, src, f32(oh), ALU.subtract, [th] + list(waits))

        sqr = Ring([sb(f"sq{i}", 512)[:, :] for i in range(3)])
        tfr = Ring([sb(f"tf{i}", 512)[:, :] for i in range(3)])

        def norm(c0, x, t_src, gcol, put, t_g=None):
            n = L - c0
            bk = banks.take()
            for k in range(KB):
                s = sqr.take()
                w = [t_src[k]] + s.free
                a = x[:, k, c0:L]
                if k % 3 == 0:
                    t = actf(s[:, 0:n], a, ACT.Square, w)
                else:
                    t = tt(pool if k % 3 == 2 else dve, s[:, 0:n], a, a, ALU.mult, w)
                tm = mm(bk[:, 0:n], [(ones, s[:, 0:n])], [t, t_cn] + bk.free, start=k == 0, stop=k == KB - 1)
                s.free = [tm]
            rs, ta, tb = rstd(bk[:, 0:n], n, 1.0 / D, [tm])
            bk.free = [ta]
            out_t = []
            for k in range(KB):
                f = tfr.take()
                t = stt(f[:, 0:n], x[:, k, c0:L], gcol(k), rs[:, 0:n], ALU.mult, ALU.mult, [tb, t_g, t_src[k]] + f.free)
                r, last = put(k, f[:, 0:n], t)
                f.free = last
                out_t.append(r)
            rs.free = [t]
            return out_t

        def norm_h(c0, t_src, gcol, shift=None, t_g=None, war=()):
            def put(k, f, t):
                h, l = HH[:, k, c0:L], HL[:, k, c0:L]
                if shift is not None:
                    t = ts(dve, f, f, shift(k), None, ALU.add, None, [t])
                th = copy(act, h, f, [t] + list(war))
                tl = tt(dve, l, f, f32(h), ALU.subtract, [th])
                return tl, [tl]
            return norm(c0, R, t_src, gcol, put, t_g)

        csl = sb("csl", 8)
        mod = sb("mod", 48)
        s1g = sb("s1g", 8)
        gb = sb("gb", 160)
        lm = sb("lm", 8)
        str_ = Ring([sb(f"sms{i}", 8)[:, :] for i in range(6)])
        t_cs = actf(csl[:, :], sm("c"), ACT.Silu, [t_sm])

        def ada(n, bk, at):
            w = weights("w_ada", n)
            for m in range(2):
                t = mm(bk[:, at + m:at + m + 1], [(w.k[:, k, m * P:(m + 1) * P], csl[:, k:k + 1]) for k in range(KB)],
                       [w.tok, t_cs] + bk.free)
            used_up(w, t)
            t2 = tt(dve, mod[:, 2 * n:2 * n + 2], bk[:, at:at + 2], sm("b_ada", 2 * n, 2), ALU.add, [t, t_sm])
            return t2

        for n in range(8):
            bk = banks.take()
            t_mod1 = ada(n, bk, 0)
            bk.free = [t_mod1]
        t = ts(dve, s1g[:, :], mod[:, 8:16], 1.0, None, ALU.add, None, [t_mod1])
        t_s1g = tt(dve, s1g[:, :], s1g[:, :], sm("g_mix"), ALU.mult, [t])
        t_h = norm_h(META, [t_x] * KB, lambda k: s1g[:, k:k + 1], shift=lambda k: mod[:, k:k + 1], t_g=t_s1g)
        HX = (HH[:, :, META:L], HL[:, :, META:L])

        def proj(w, m, o, waits, x=HX, tx=None, k0=0, k1=KB):
            for k in range(k0, k1):
                t = mm3(o, [(block_of(w, k, m * P), two(x, slice(None), k, slice(None)))],
                        [w.split, tx[k] if tx else None] + (list(waits) if k == 0 else []), start=k == 0, stop=k == KB - 1)
            return t

        def unit2(key, waits, x=HX, tx=None):
            w = weights(*key)
            bk = banks.take()
            for m in range(2):
                for k in (0, 4):
                    t = proj(w, m, bk[:, m * T:(m + 1) * T], bk.free if m == 0 else [], x=x, tx=tx, k0=k, k1=k + 4)
                    if (m, k) != (1, 4):
                        yield None
            used_up(w, t)
            yield bk, t

        beta, gg, gc, egc, nbeg, kdf, tmp16 = (gb[:, 16 * i:16 * i + 16].rearrange("p (t h) -> p t h", t=2) for i in range(7))
        ea = gb[:, 112:120]
        s0 = ExitStack()
        wb_ = sbr("wb", 128, s0)
        wb, t_wb = fetch_all("w_ba", 128, s0, [])
        t_wba = split(wb_[0], wb_[1], wb, [t_wb])
        bk = banks.take()
        ba = bk[:, 0:32].rearrange("p (t c) -> p t c", t=2)
        for i in range(2):
            t = mm3(ba[:, i, :], [(two(HX, slice(None), k, slice(i * P, (i + 1) * P)),
                                   (wb_[0][:, 16 * k:16 * k + 16], wb_[1][:, 16 * k:16 * k + 16])) for k in range(KB)],
                    t_h + [t_wba] + bk.free)
        s0.close()
        t_wb = t
        t_e = actf(ea, sm("a_log"), ACT.Exp, [t_sm])
        t1 = actf(beta, ba[:, :, 0:8], ACT.Exp, [t], scale=-1.0)
        t2 = tt(dve, gg, ba[:, :, 8:16], sm("dt").unsqueeze(1).to_broadcast([P, 2, 8]), ALU.add, [t, t1])
        bk.free = [t2]
        t3 = ts(dve, beta, beta, 1.0, None, ALU.add, None, [t1])
        t_beta = recip(beta, beta, [t3])
        ab = tmp16
        t4 = actf(ab, gg, ACT.Abs, [t2])
        t5 = actf(ab, ab, ACT.Exp, [t4], scale=-1.0)
        t6 = actf(ab, ab, ACT.Ln, [t5], bias=1.0)
        t7 = stt(gg, gg, 0.0, ab, ALU.max, ALU.add, [t6])
        t_g = stt(gg, gg, -1.0, ea.unsqueeze(1).to_broadcast([P, 2, 8]), ALU.mult, ALU.mult, [t7, t_e])
        bk = banks.take()
        ta = mm(bk[:, 0:16], [(cn("tri"), gb[:, 16:32])], [t_g] + bk.free)
        ta = mm(bk[:, 16:24], [(ones, gb[:, 16:24])], [t_g])
        t_gc = copy(dve, gb[:, 32:48], bk[:, 0:16], [ta])
        t10 = tt(dve, kdf[:, 0, :], bk[:, 16:24], gc[:, 0, :], ALU.subtract, [t_gc])
        bk.free = [t10]
        t_kdf = actf(kdf[:, 0, :], kdf[:, 0, :], ACT.Exp, [t10])
        t12 = actf(egc, gc, ACT.Exp, [t_gc])
        t_nbeg = stt(nbeg, egc, -1.0, beta, ALU.mult, ALU.mult, [t12, t_beta])

        sd = ExitStack()
        QD = sb("QD", 6144, scope=sd)[:, :].rearrange("p (b t) -> p b t", b=24)
        sg = ExitStack()
        cg = fetch("cg", sg, [t_wb])
        qkvz = [Buf(sb(f"qkvz{i}", 2048, scope=sg)[:, :].rearrange("p (b t) -> p b t", b=8)) for i in range(2)]
        for q_b in qkvz:
            q_b.free = [t_wb]
        conv = sm("conv").rearrange("p (b j) -> p b j", b=24)

        def project_pair(p, S):
            B = qkvz[p % 2]
            S["B"] = B.ap
            for j in range(4):
                for r in unit2(("w_in", 4 * j + p), [], tx=t_h):
                    if r is None:
                        yield
                bk, t = r
                ys = B[:, 2 * j:2 * j + 2, :]
                if j == 3:
                    t2 = actf(ys, bk.ap.rearrange("p (m t) -> p m t", m=2), ACT.Silu, [t] + B.free)
                    bk.free = [t2]
                    S["z"] = t2
                else:
                    for m in range(2):
                        b = 8 * j + 2 * p + m
                        x = bk[:, m * T:(m + 1) * T]
                        y = B[:, 2 * j + m, :]
                        tc = ts(dve, y, x, conv[:, b, 3:4], None, ALU.mult, None, [t, t_sm] + B.free)
                        for i in range(1, 4):
                            tc = stt(y[:, i:T], x[:, 0:T - i], conv[:, b, 3 - i:4 - i], y[:, i:T], ALU.mult, ALU.add, [tc])
                    bk.free = [tc]
                    S["qkv"[j]] = actf(ys, ys, ACT.Silu, [tc])
                a = banks.take()
                a.free = [ada(8 + 4 * p + j, a, 0)]
                S["mod"] = a.free[0]
                yield
            for j in range(2):
                ys = B[:, 2 * j:2 * j + 2, :]
                s = sqr.take()
                s2 = s.ap.rearrange("p (m t) -> p m t", m=2)
                t = actf(s2, ys, ACT.Square, [S["qk"[j]]] + s.free)
                bk = banks.take()
                tm = mm(bk[:, :], [(ones, s[:, :])], [t] + bk.free)
                s.free = [tm]
                rs, ta, tb = rstd(bk[:, :], 512, 1.0, [tm])
                bk.free = [ta]
                t = stt(ys, ys, float(P) ** -0.5 if j == 0 else 1.0, rs.ap.rearrange("p (m t) -> p m t", m=2), ALU.mult, ALU.mult, [tb])
                rs.free = [t]
                S["qk"[j]] = t
                yield

        W = {n: Buf(sb("g" + n, 512, scope=sg)[:, :].rearrange("p (m j) -> p m j", m=4))
             for n in ("A", "AT", "M", "N", "P", "UO", "D2", "QK", "X")}
        hw = [{n: Buf(sb(f"h{n}{s}", 128, scope=sg)[:, :]) for n in
               ("vb0", "vb1", "kd", "u0", "S1", "r1", "u1", "qd")} for s in range(2)]
        YH = tuple(a[:, 0:2048].rearrange("p (h t) -> p h t", h=8) for a in YR)
        t_y = [None] * 8

        def bc4(x):
            return x.unsqueeze(1).to_broadcast([P, 4, P])

        def b4(bank):
            return bank.ap.rearrange("p (m j) -> p m j", m=4)

        def delta(p, S0):
            B = S0["B"]

            def cols(b, i):
                return B[:, b, i * P:(i + 1) * P]

            q_ = lambda m, i: cols(m, i)
            k_ = lambda m, i: cols(2 + m, i)
            v_ = lambda m, i: cols(4 + m, i)
            mats = [(m, i) for m in range(2) for i in range(2)]
            tq, tk, tv = S0["q"], S0["k"], S0["v"]
            kk, gbk = banks.take(), banks.take()
            for n, (m, i) in enumerate(mats):
                t_kk = mm(kk[:, n * P:(n + 1) * P], [(k_(m, i), k_(m, i))], [tk] + kk.free)
            for n, (m, i) in enumerate(mats):
                h = 2 * p + m
                t_gb = mm(gbk[:, n * P:(n + 1) * P],
                          [(gg[:, i, h:h + 1].to_broadcast([P, P]), cn("tri"))], [t_g] + gbk.free)
            yield
            X, A, D2, AT, M, N, UO, QK, PB = (W[n] for n in ("X", "A", "D2", "AT", "M", "N", "UO", "QK", "P"))
            for n, (m, i) in enumerate(mats):
                h = 2 * p + m
                t = ts(dve, X[:, n, :], gbk[:, n * P:(n + 1) * P], gc[:, i, h:h + 1], None, ALU.subtract, None,
                       [t_gb, t_gc] + X.free)
            t1 = tt(pool, A[:, :, :], X[:, :, :], bc4(cg("pm1")), ALU.add, [t] + A.free)
            t2 = tt(dve, D2[:, :, :], X[:, :, :], bc4(cg("pm2")), ALU.subtract, [t] + D2.free)
            t1 = actf(A[:, :, :], A[:, :, :], ACT.Exp, [t1], scale=-1.0)
            t2 = actf(D2[:, :, :], D2[:, :, :], ACT.Exp, [t2])
            t_x = actf(X[:, :, :], b4(gbk), ACT.Exp, [t1, t2, t])
            gbk.free = [t, t_x]
            t3 = tt(dve, A[:, :, :], b4(kk), A[:, :, :], ALU.mult, [t1, t_kk])
            kk.free = [t3]
            for n, (m, i) in enumerate(mats):
                h = 2 * p + m
                t3b = ts(dve, A[:, n, :], A[:, n, :], beta[:, i, h:h + 1], None, ALU.mult, None, [t3, t_beta])
            yield
            qk = banks.take()
            for n, (m, i) in enumerate(mats):
                t_qk = mm(qk[:, n * P:(n + 1) * P], [(k_(m, i), q_(m, i))], [tq, tk] + qk.free)
            t_qkd = tt(dve, QK[:, :, :], b4(qk), D2[:, :, :], ALU.mult, [t_qk, t2] + QK.free)
            qk.free = [t_qkd]
            D2.free = [t_qkd]
            yield
            atb = banks.take()
            for n in range(4):
                t4 = tr(atb[:, n * P:(n + 1) * P], A[:, n, :], [t3b] + atb.free)
            t5 = copy(act, AT[:, :, :], b4(atb), [t4] + AT.free)
            atb.free = [t5]
            t6 = tt(pool, M[:, :, :], A[:, :, :], bc4(cg("lo1")), ALU.mult, [t3b] + M.free)
            t_m = tt(pool, M[:, :, :], bc4(ident), M[:, :, :], ALU.subtract, [t6])
            t7 = tt(dve, N[:, :, :], AT[:, :, :], bc4(cg("up1")), ALU.mult, [t5] + N.free)
            t_n = tt(dve, N[:, :, :], bc4(ident), N[:, :, :], ALU.subtract, [t7])
            t_uo = tt(pool, UO[:, :, :], AT[:, :, :], bc4(cg("up2")), ALU.mult, [t5] + UO.free)
            yield
            tt_ = {}
            for m in range(2):
                h = 2 * p + m
                w_ = hw[m]
                tb = banks.take()
                ta = tr(tb[:, 0:P], v_(m, 0), [tv] + tb.free)
                ta = tr(tb[:, P:2 * P], v_(m, 1), [])
                ta = tr(tb[:, 2 * P:3 * P], k_(m, 0), [tk])
                e0 = ts(dve, w_["vb0"].ap, tb[:, 0:P], beta[:, 0, h:h + 1], None, ALU.mult, None, [ta, t_beta] + w_["vb0"].free)
                e1 = ts(dve, w_["vb1"].ap, tb[:, P:2 * P], beta[:, 1, h:h + 1], None, ALU.mult, None, [ta] + w_["vb1"].free)
                e2 = ts(dve, w_["kd"].ap, tb[:, 2 * P:3 * P], kdf[:, 0, h:h + 1], None, ALU.mult, None, [ta, t_kdf] + w_["kd"].free)
                tb.free = [e2]
                e3 = tt(pool, w_["qd"].ap, q_(m, 1), X[:, 2 * m + 1, :], ALU.mult, [t_x, tq] + w_["qd"].free)
                tt_[m] = [e0, e1, e2, e3]
            X.free = [tt_[1][3]]
            yield
            for s in LEVELS[1:]:
                last = s == 64
                p1 = banks.take()
                for n in range(4):
                    tp = mm(p1[:, n * P:(n + 1) * P], [(UO[:, n, :], M[:, n, :])], [t_uo, t_m] + p1.free)
                tpc = copy(act, PB[:, :, :], b4(p1), [tp] + PB.free)
                p1.free = [tpc]
                if not last:
                    t_uo = tt(pool, UO[:, :, :], AT[:, :, :], bc4(cg(f"up{2 * s}")), ALU.mult, [tp])
                yield
                p3 = banks.take()
                tmm = None
                if not last:
                    p2 = banks.take()
                    for n in range(4):
                        tmm = mm(p2[:, n * P:(n + 1) * P], [(N[:, n, :], PB[:, n, :])], [tpc, t_n] + p2.free)
                    t_m = tt(dve, M[:, :, :], M[:, :, :], b4(p2), ALU.subtract, [tmm, tp])
                    p2.free = [t_m]
                for n in range(4):
                    tn = mm(p3[:, n * P:(n + 1) * P], [(PB[:, n, :], N[:, n, :])], [tpc, t_n] + p3.free)
                PB.free = [tn]
                t_n = tt(dve, N[:, :, :], N[:, :, :], b4(p3), ALU.subtract, [tn, tmm])
                p3.free = [t_n]
                yield
            A.free = AT.free = M.free = UO.free = [t_n, t_m, t_uo]

            def small(dst, lhs, rhs, waits, lfree, q=act):
                bu = banks.take()
                a = mm(bu[:, 0:P], [(lhs, rhs)], list(waits) + bu.free)
                c = copy(q, dst.ap, bu[:, 0:P], [a] + dst.free)
                bu.free = [c]
                for f in lfree:
                    f.free = [a]
                return a, c

            for m in range(2):
                w_ = hw[m]
                tt_[m].append(small(w_["u0"], N[:, 2 * m, :], w_["vb0"].ap, [t_n, tt_[m][0]], [w_["vb0"]])[1])
            yield
            for m in range(2):
                w_ = hw[m]
                tt_[m].append(small(w_["S1"], w_["kd"].ap, w_["u0"].ap, [tt_[m][4], tt_[m][2]], [w_["kd"]])[1])
            yield
            for m in range(2):
                w_ = hw[m]
                bu = banks.take()
                a = mm(bu[:, 0:P], [(k_(m, 1), w_["S1"].ap)], [tt_[m][5]] + bu.free)
                c = stt(w_["r1"].ap, bu[:, 0:P], nbeg[:, 1, 2 * p + m:2 * p + m + 1], w_["vb1"].ap, ALU.mult, ALU.add,
                        [a, t_nbeg, tt_[m][1]] + w_["r1"].free)
                bu.free = [c]
                w_["vb1"].free = [c]
                tt_[m].append(c)
            yield
            for m in range(2):
                w_ = hw[m]
                a, c = small(w_["u1"], N[:, 2 * m + 1, :], w_["r1"].ap, [tt_[m][6]], [w_["r1"]])
                tt_[m].append(c)
            N.free = [a]
            yield
            outs = []
            for m in range(2):
                w_ = hw[m]
                bo = banks.take()
                a = mm(bo[:, 0:P], [(w_["u0"].ap, QK[:, 2 * m, :])], [tt_[m][4], t_qkd] + bo.free)
                a = mm(bo[:, P:2 * P], [(w_["S1"].ap, w_["qd"].ap), (w_["u1"].ap, QK[:, 2 * m + 1, :])],
                       [tt_[m][7], tt_[m][3], tt_[m][5]])
                for nm in ("u0", "S1", "qd", "u1"):
                    w_[nm].free = [a]
                f = tfr.take()
                c = copy(dve, f[:, 0:T], bo[:, 0:T], [a] + f.free)
                bo.free = [c]
                s = sqr.take()
                d = tt(pool, s[:, 0:T], f[:, 0:T], f[:, 0:T], ALU.mult, [c] + s.free)
                outs.append((f, s, d))
            QK.free = [a]
            yield
            for m in range(2):
                h = 2 * p + m
                f, s, d = outs[m]
                bs = banks.take()
                e = mm(bs[:, 0:T], [(ones, s[:, 0:T])], [d] + bs.free)
                s.free = [e]
                rs, f1, f2 = rstd(bs[:, 0:T], T, 1.0 / P, [e])
                bs.free = [f1]
                g1 = stt(f[:, 0:T], f[:, 0:T], sm("gdn_g"), rs[:, 0:T], ALU.mult, ALU.mult, [f2])
                rs.free = [g1]
                g2 = tt(pool, f[:, 0:T], f[:, 0:T], B[:, 6 + m, :], ALU.mult, [g1, S0["z"]])
                t_y[h] = split(YH[0][:, h, :], YH[1][:, h, :], f[:, 0:T], [g2])
                f.free = [t_y[h]]
            qkvz[p % 2].free = [g2, t_y[2 * p], t_y[2 * p + 1], a]
            yield

        t_qd = [None] * 24
        t_vd = []

        def project_dil():
            for u in range(12):
                for r in unit2(("w_in", 16 + u), [], tx=t_h):
                    if r is None:
                        yield
                bk, t = r
                ys = QD[:, 2 * u:2 * u + 2, :]
                y1 = bk.ap.rearrange("p (m t) -> p m t", m=2)
                c = copy(dve, ys, y1, [t])
                s = sqr.take()
                d = tt(pool, s.ap.rearrange("p (m t) -> p m t", m=2), ys, ys, ALU.mult, [c] + s.free)
                bk.free = [c]
                bs = banks.take()
                e = mm(bs[:, :], [(ones, s[:, :])], [d] + bs.free)
                s.free = [e]
                rs, f1, f2 = rstd(bs[:, :], 512, 1.0 / P, [e])
                bs.free = [f1]
                t = stt(ys, ys, sm("dq_g" if u < 6 else "dk_g"), rs.ap.rearrange("p (m t) -> p m t", m=2), ALU.mult, ALU.mult, [f2, c])
                rs.free = [t]
                t_qd[2 * u] = t_qd[2 * u + 1] = t
                yield

        Ss = [{} for _ in range(4)]
        drain(project_pair(0, Ss[0]))
        dil = project_dil()
        for p in range(4):
            side = project_pair(p + 1, Ss[p + 1]) if p < 3 else dil
            weave(delta(p, Ss[p]), side, 1 if p < 3 else 3, 1 if p < 3 else 2)
            if p < 3:
                drain(side)
        drain(dil)
        t_mod2 = Ss[3]["mod"]
        sg.close()

        se = ExitStack()
        YB = tuple(a.rearrange("p (h t) -> p h t", h=4) for a in sbr("YB", 1024, se))
        GA = sb("GA", 2048, scope=se)[:, :].rearrange("p (m t) -> p m t", m=8)
        sf = ExitStack()
        VD = sb("VD", 3072, scope=sf)[:, :].rearrange("p (t n) -> p t n", t=2)
        pr = Ring([sb(f"pr{i}", 768, scope=sf)[:, :] for i in range(2)])
        ptr = Ring([sb(f"pt{i}", 768, scope=sf)[:, :] for i in range(2)])
        over = [t_y[6], t_y[7]] + qkvz[0].free + qkvz[1].free + W["QK"].free + W["N"].free + W["A"].free + W["X"].free + \
            [x for w_ in hw for b in w_.values() for x in b.free]
        for b in pr.bufs + ptr.bufs:
            b.free = over
        cd = fetch("cd", sf, over)
        t_yb = []

        def project_v():
            for u in range(6):
                w = weights("w_in", 28 + u)
                bk = banks.take()
                for i in range(2):
                    for k in range(KB):
                        t = mm3(bk[:, i * T:(i + 1) * T], [(two(HX, slice(None), k, slice(i * P, (i + 1) * P)), block_of(w, k, 0, 256))],
                                [w.split, t_h[k]] + bk.free, start=k == 0, stop=k == KB - 1)
                used_up(w, t)
                c = copy(act, VD[:, :, u * 256:(u + 1) * 256], bk.ap.rearrange("p (t n) -> p t n", t=2), [t] + over)
                bk.free = [c]
                t_vd.append(c)
                yield


        def dil_attention():
            for s in range(NSLOT):
                yb = banks.take()
                for i in range(2):
                    nk = P * (i + 1)
                    b1 = banks.take()
                    b2 = banks.take() if i else None
                    for g in range(NG):
                        h = g * NSLOT + s
                        o_ = (b2 if i and g == 2 else b1)
                        c0 = 0 if (i and g == 2) else g * nk
                        t = mm(o_[:, c0:c0 + nk], [(QD[:, h, i * P:(i + 1) * P], QD[:, 12 + h, 0:nk])],
                               [t_qd[h], t_qd[12 + h]] + o_.free)
                    pb = pr.take()
                    sc = float(P) ** -0.5
                    dmk = cd("dm1") if i else cd("dm0")
                    if i:
                        ta = stt(pb[:, 0:512], b1[:, 0:512], sc, dmk[:, 0:512], ALU.mult, ALU.add, [t, cd.tok] + pb.free)
                        tb = stt(pb[:, 512:768], b2[:, 0:256], sc, dmk[:, 512:768], ALU.mult, ALU.add, [t])
                        b1.free, b2.free = [ta], [tb]
                        n = 768
                    else:
                        tb = stt(pb[:, 0:384], b1[:, 0:384], sc, dmk, ALU.mult, ALU.add, [t, cd.tok] + pb.free)
                        b1.free = [tb]
                        n = 384
                    sv = str_.take()
                    t = rmax(sv[:, 0:1], pb[:, 0:n], AX.X, [tb] + sv.free)
                    t = ts(dve, sv[:, 1:2], sv[:, 0:1], -1.0, None, ALU.mult, None, [t])
                    t = actf(pb[:, 0:n], pb[:, 0:n], ACT.Exp, [t], bias=sv[:, 1:2], accum_out=sv[:, 2:3])
                    t = recip(sv[:, 3:4], sv[:, 2:3], [t])
                    t = ts(dve, pb[:, 0:n], pb[:, 0:n], sv[:, 3:4], None, ALU.mult, None, [t])
                    sv.free = [t]
                    yield
                    pt = ptr.take()
                    nb = n // P
                    for j0 in range(0, nb, 4):
                        bt = banks.take()
                        j1 = min(nb, j0 + 4)
                        for j in range(j0, j1):
                            tx = tr(bt[:, (j - j0) * P:(j - j0 + 1) * P], pb[:, j * P:(j + 1) * P], [t] + bt.free)
                        c1 = copy(act, pt[:, j0 * P:j1 * P], bt[:, 0:(j1 - j0) * P], [tx] + pt.free)
                        bt.free = [c1]
                    pb.free = [tx]
                    yield
                    pairs = []
                    for g in range(NG):
                        h = g * NSLOT + s
                        for kt in range(i + 1):
                            j = g * (i + 1) + kt
                            pairs.append((VD[:, kt, h * P:(h + 1) * P], pt[:, j * P:(j + 1) * P]))
                    t = mm(yb[:, i * P:(i + 1) * P], pairs, [c1] + t_vd + yb.free)
                    pt.free = [t]
                c = copy(act, YB[0][:, s, :], yb[:, 0:T], [t] + over)
                c = tt(dve, YB[1][:, s, :], yb[:, 0:T], f32(YB[0][:, s, :]), ALU.subtract, [c])
                yb.free = [c]
                t_yb.append(c)
                yield

        t_ga, t_gb_ = [None] * 4, [None] * 4

        def gate(first, G, tg, war):
            for u in range(4):
                for r in unit2(("w_in", first + u), [], tx=t_h):
                    if r is None:
                        yield
                bk, t = r
                c = actf(G[:, 2 * u:2 * u + 2, :], bk.ap.rearrange("p (m t) -> p m t", m=2), ACT.Sigmoid, [t] + war)
                bk.free = [c]
                tg[u] = c
                yield

        def up_gdn():
            for u in range(4):
                for r in unit2(("w_up_gdn", u), [], x=YH, tx=t_y):
                    if r is None:
                        yield
                bk, t = r
                g = GA[:, 2 * u:2 * u + 2, :]
                c = tt(dve, g, g, bk.ap.rearrange("p (m t) -> p m t", m=2), ALU.mult, [t, t_ga[u]])
                bk.free = [c]
                t_ga[u] = c
                tg = t
                yield
            over2.append(tg)

        def side_work():
            yield from gate(34, GA, t_ga, over)
            yield from up_gdn()

        over2 = []
        drain(project_v())
        gt = side_work()
        weave(dil_attention(), gt, 3, 2)
        drain(gt)
        sf.close()
        GB = sb("GB", 2048, scope=se)[:, :].rearrange("p (m t) -> p m t", m=8)
        drain(gate(38, GB, t_gb_, t_yb))
        t_mg = [None] * KB
        for u in range(2):
            w = weights("w_up_dil", u)
            for v in range(2):
                bk = banks.take()
                for m in range(2):
                    t = mm3(bk[:, m * T:(m + 1) * T],
                            [(block_of(w, k, (2 * v + m) * P, parts=4), two(YB, slice(None), k, slice(None))) for k in range(4)],
                            [w.split] + t_yb + bk.free)
                j = 4 * u + 2 * v
                b, a = GB[:, j:j + 2, :], GA[:, j:j + 2, :]
                c = tt(dve, b, b, bk.ap.rearrange("p (m t) -> p m t", m=2), ALU.mult, [t, t_gb_[j // 2]])
                bk.free = [c]
                c = tt(pool, b, b, a, ALU.add, [c, t_ga[j // 2]])
                t_mg[j] = t_mg[j + 1] = split(YH[0][:, j:j + 2, :], YH[1][:, j:j + 2, :], b, [c] + over2)
            used_up(w, t)
        t_r = [None] * KB
        for u in range(4):
            for r in unit2(("w_out", u), [], x=YH, tx=t_mg):
                pass
            bk, t = r
            for m in range(2):
                j = 2 * u + m
                t_r[j] = stt(R[:, j, META:L], bk[:, m * T:(m + 1) * T], mod[:, 16 + j:17 + j], R[:, j, META:L],
                             ALU.mult, ALU.add, [t, t_mod2])
            bk.free = [t_r[2 * u + 1]]
        se.close()
        sd.close()

        t = ts(dve, s1g[:, :], mod[:, 32:40], 1.0, None, ALU.add, None, [t_mod2])
        t_s2 = tt(dve, s1g[:, :], s1g[:, :], sm("g_ffn"), ALU.mult, [t])
        t_h2 = norm_h(META, t_r, lambda k: s1g[:, k:k + 1], shift=lambda k: mod[:, 24 + k:25 + k], t_g=t_s2)
        sx = ExitStack()
        rt = sb("rt", 704, scope=sx)
        sco = rt[:, 0:128].rearrange("p (t e) -> p t e", t=2)
        sel = rt[:, 128:256].rearrange("p (t e) -> p t e", t=2)
        cmb = rt[:, 256:384].rearrange("p (t e) -> p t e", t=2)
        mk = rt[:, 384:512].rearrange("p (t e) -> p t e", t=2)
        g8 = rt[:, 512:640].rearrange("p (t g e) -> p t g e", t=2, g=8)
        gs8 = rt[:, 640:656].rearrange("p (t g) -> p t g", t=2)
        m8 = rt[:, 656:672].rearrange("p (t g) -> p t g", t=2)
        gm = rt[:, 672:688].rearrange("p (t g) -> p t g", t=2)
        sm2 = rt[:, 688:692]
        CT = sb("CT", T, scope=sx)[:, :]
        wr_ = sbr("wr", 512, sx)
        wr, t_wr = fetch_all("w_r", 512, sx, [t_r[7]])
        t_wr = split(wr_[0], wr_[1], wr, [t_wr, t_r[7]])
        bk = banks.take()
        for i in range(2):
            t = mm3(bk[:, i * 64:(i + 1) * 64],
                    [(two(HX, slice(None), k, slice(i * P, (i + 1) * P)),
                      (wr_[0][:, 64 * k:64 * k + 64], wr_[1][:, 64 * k:64 * k + 64])) for k in range(KB)],
                    t_h2 + [t_wr] + bk.free)
        t = actf(sco, bk[:, 0:128].rearrange("p (t e) -> p t e", t=2), ACT.Sigmoid, [t])
        bk.free = [t]
        t = tt(dve, sel, sco, sm("rbias").unsqueeze(1).to_broadcast([P, 2, 64]), ALU.add, [t])
        for i in range(2):
            for g in range(8):
                tl = dve.add(lambda e, i=i, g=g: e.max(g8[:, i, g, :], sel[:, i, 8 * g:8 * g + 8]), [t])
        t = tt(dve, gs8, g8[:, :, :, 0], g8[:, :, :, 1], ALU.add, [tl])
        for i in range(2):
            tl = dve.add(lambda e, i=i: e.max(m8[:, i, :], gs8[:, i, :]), [t])
        t = dve.add(lambda e: e.memset(m8[:, :, 4:8], BIG), [tl])
        for i in range(2):
            tl = dve.add(lambda e, i=i: e.match_replace(gm[:, i, :], m8[:, i, :], gs8[:, i, :], -BIG), [t])
        t = ts(dve, gm, gm, -BIG, None, ALU.is_equal, None, [tl])
        gmb = gm.unsqueeze(3).to_broadcast([P, 2, 8, 8])
        mk4 = mk.rearrange("p t (g e) -> p t g e", g=8)
        t1 = tt(dve, mk4, sel.rearrange("p t (g e) -> p t g e", g=8), gmb, ALU.mult, [t])
        t2 = ts(dve, gm, gm, -1.0, BIG, ALU.add, ALU.mult, [t1])
        t = tt(dve, mk4, mk4, gmb, ALU.add, [t2])
        for i in range(2):
            tl = dve.add(lambda e, i=i: e.max(m8[:, i, :], mk[:, i, :]), [t])
        for i in range(2):
            t = dve.add(lambda e, i=i: e.match_replace(sel[:, i, :], m8[:, i, :], mk[:, i, :], 2 * BIG), [tl])
        t = ts(dve, sel, sel, 2 * BIG, None, ALU.is_equal, None, [t])
        t = tt(dve, cmb, sco, sel, ALU.mult, [t])
        t = dve.add(lambda e: e.tensor_reduce(sm2[:, 0:2], cmb, AX.X, ALU.add), [t])
        t = recip(sm2[:, 2:4], sm2[:, 0:2], [t])
        for i in range(2):
            t_c = ts(dve, cmb[:, i, :], cmb[:, i, :], sm2[:, 2 + i:3 + i], 2.5, ALU.mult, ALU.mult, [t])
        bk = banks.take()
        for i in range(2):
            t = tr(bk[0:64, i * P:(i + 1) * P], cmb[:, i, :], [t_c] + bk.free)
        t_ct = copy(dve, CT[0:64, :], bk[0:64, 0:T], [t])
        bk.free = [t_ct]

        acc = banks.bufs[0:4]
        mb = Ring([])
        mb.bufs = banks.bufs[4:8]
        afr = Ring([sb(f"af{i}", 512, scope=sx)[:, :] for i in range(2)])
        arr = [sbr(f"ar{i}", 512, sx) for i in range(2)]
        arr_free = [[], []]
        cbs = Ring([sb(f"cb{i}", 256, scope=sx)[:, :] for i in range(2)])
        for b in acc:
            assert not b.held

        def down(e, i, ta):
            w = weights("w_ed", e)
            ah, al = arr[i]
            for j in range(KB):
                bi = j // 2
                t = mm3(acc[bi][:, (j % 2) * T:(j % 2 + 1) * T],
                        [(block_of(w, f, j * P, parts=2), (ah[:, f * T:(f + 1) * T], al[:, f * T:(f + 1) * T])) for f in range(2)],
                        [ta, w.split] + acc[bi].free, start=(e == 0 and j % 2 == 0), stop=(e == NE), skip=True)
            used_up(w, t)
            arr_free[i] = [t]
            return t

        prev = None
        for e in range(NE + 1):
            bg, bu = mb.take(), mb.take()
            w = weights("w_eg", e)
            for f in range(2):
                tg = proj(w, f, bg[:, f * T:(f + 1) * T], bg.free, tx=t_h2)
            used_up(w, tg)
            w = weights("w_eu", e)
            if e < NE:
                bc, cb = mb.take(), cbs.take()
                tcb = mm(bc[:, 0:T], [(cn_t[0:64, CN["ident"][0] + e:CN["ident"][0] + e + 1].to_broadcast([64, P]), CT[0:64, :])],
                         [t_ct] + bc.free)
                tcc = copy(act, cb[:, 0:T], bc[:, 0:T], [tcb] + cb.free)
                bc.free = [tcc]
            for f in range(2):
                tu = proj(w, f, bu[:, f * T:(f + 1) * T], bu.free, tx=t_h2)
            used_up(w, tu)
            a = afr.take()
            t1 = actf(a.ap, bg[:, :], ACT.Silu, [tg] + a.free)
            bg.free = [t1]
            if prev is not None:
                down(*prev)
            a3 = a.ap.rearrange("p (f t) -> p f t", f=2)
            if e < NE:
                t1 = tt(pool, a3, a3, cb[:, 0:T].unsqueeze(1).to_broadcast([P, 2, T]), ALU.mult, [t1, tcc])
                cb.free = [t1]
            t2 = tt(dve, a.ap, a.ap, bu[:, :], ALU.mult, [t1, tu])
            bu.free = [t2]
            i = e % 2
            t3 = split(arr[i][0], arr[i][1], a.ap, [t2] + arr_free[i])
            a.free = [t3]
            prev = (e, i, t3)
        t_acc = down(*prev)
        for j in range(KB):
            t_r[j] = stt(R[:, j, META:L], acc[j // 2][:, (j % 2) * T:(j % 2 + 1) * T], mod[:, 40 + j:41 + j], R[:, j, META:L],
                         ALU.mult, ALU.add, [t_acc])
            acc[j // 2].free = [t_r[j]]
        sx.close()

        n2 = sm("norm2").rearrange("p (i k) -> p i k", i=8)
        s2 = ExitStack()
        MT = sb("MT", KB * L, scope=s2)[:, :].rearrange("p (b t) -> p b t", b=KB)
        HF = (HH, HL)
        OT = tuple(a.rearrange("p (b t) -> p b t", b=KB) for a in YR)
        QT = [(0, 16), (16, 128), (144, 128)]

        def one(bk):
            return bk[:, 0:L]

        def add_mix(t_src, gi, c0):
            def put(k, f, t):
                t = tt(pool, R[:, k, c0:L], R[:, k, c0:L], f, ALU.add, [t])
                return t, [t]
            return norm(c0, MT, t_src, lambda k: n2[:, gi, k:k + 1], put)

        def mixer_out(layer, tx):
            toks = []
            for u in range(4):
                w = weights("w_out2", 4 * layer + u)
                for m in range(2):
                    bk = banks.take()
                    t = proj(w, m, one(bk), bk.free, x=OT, tx=tx)
                    c = copy(act if m else dve, MT[:, 2 * u + m, :], one(bk), [t])
                    bk.free = [c]
                    toks.append(c)
                used_up(w, t)
            return add_mix(toks, 4 * layer + 1, 0)

        def mlp(layer, tr_, c0):
            th = norm_h(0, tr_, lambda k: n2[:, 4 * layer + 2, k:k + 1])
            n = L - c0
            sc_ = ExitStack()
            X2 = tuple(a.rearrange("p (b t) -> p b t", b=32) for a in sbr(f"X{layer}", 32 * L, sc_))
            toks = []
            for u in range(16):
                w = weights("w_up2", 16 * layer + u)
                for m in range(2):
                    bk = banks.take()
                    t = proj(w, m, bk[:, 0:n], bk.free, x=(HH[:, :, c0:L], HL[:, :, c0:L]), tx=th)
                    b = 2 * u + m
                    f = tfr.take()
                    c = actf(f[:, 0:n], bk[:, 0:n], ACT.Relu, [t] + f.free)
                    c2 = tt(dve, f[:, 0:n], f[:, 0:n], bk[:, 0:n], ALU.mult, [c])
                    bk.free = [c2]
                    c3 = split(X2[0][:, b, c0:L], X2[1][:, b, c0:L], f[:, 0:n], [c2])
                    f.free = [c3]
                    toks.append(c3)
                used_up(w, t)
            dt_ = []
            for g in range(4):
                bks = [banks.take(), banks.take()]
                for kc in range(4):
                    w = weights("w_down2", 16 * layer + 4 * g + kc)
                    for m in range(2):
                        for k in range(KB):
                            t = mm3(bks[m][:, 0:n], [(block_of(w, k, m * P), two(X2, slice(None), 8 * kc + k, slice(c0, L)))],
                                    [w.split, toks[8 * kc + k]] + bks[m].free, start=kc == 0 and k == 0, stop=kc == 3 and k == KB - 1)
                    used_up(w, t)
                for m in range(2):
                    c = copy(act if m else dve, MT[:, 2 * g + m, c0:L], bks[m][:, 0:n], [t])
                    bks[m].free = [c]
                    dt_.append(c)
            sc_.close()
            return add_mix(dt_, 4 * layer + 3, c0)

        t_hh = norm_h(0, t_r, lambda k: n2[:, 0, k:k + 1])
        sa = ExitStack()
        lam_, t_l = fetch_all("lam", 256, sa, [t_acc])
        s = sqr.take()
        sv_ = s[:, 0:128].rearrange("p (a d) -> p a d", a=2)
        lv2 = lam_.rearrange("p (a b d) -> p a b d", a=2, b=2)
        t = tt(dve, sv_, lv2[:, :, 0, :], lv2[:, :, 1, :], ALU.mult, [t_l] + s.free)
        t = dve.add(lambda e: e.tensor_reduce(lm[:, 0:2], sv_, AX.X, ALU.add), [t])
        s.free = [t]
        t = actf(lm[:, 0:2], lm[:, 0:2], ACT.Exp, [t])
        t = tt(dve, lm[:, 2:3], lm[:, 0:1], lm[:, 1:2], ALU.subtract, [t])
        t_lam = ts(dve, lm[:, 2:3], lm[:, 2:3], LAM0, None, ALU.add, None, [t])
        t_sub = ts(dve, lm[:, 3:4], sm("subln"), 1.0 - LAM0, None, ALU.mult, None, [t_sm])

        QK2 = sb("QK2", 16 * L, scope=sa)[:, :].rearrange("p (b t) -> p b t", b=16)
        VV = sb("VV", 3072, scope=sa)[:, :].rearrange("p (t n) -> p t n", t=3)
        ps_ = Ring([sb(f"pp{i}", 544, scope=sa)[:, :].rearrange("p (c k) -> p c k", c=2) for i in range(3)])
        at_ = Ring([sb(f"at{i}", 384, scope=sa)[:, :].rearrange("p (j q) -> p j q", j=3) for i in range(2)])
        t_over = t_acc
        t_vz = memset(pool, VV[:, 0, :], 0.0, [t_over, t_r[7]])
        for b in at_.bufs:
            b.free = [memset(pool, b[:, 0, :], 0.0, [t_over, t_r[7]])]
        for b in ps_.bufs:
            b.free = [t_over, t_r[7], t3]
        c2 = fetch("c2", sa, [t_over, t_r[7], t3])
        tqk = [None] * 16
        t_vv = [None] * 4
        t_ot = [None] * NH

        def project_heads(p):
            for j in range(2):
                w = weights("w_in2", 4 * j + p)
                for m in range(2):
                    bk = banks.take()
                    for k in (0, 4):
                        t = proj(w, m, one(bk), bk.free, x=HF, tx=t_hh, k0=k, k1=k + 4)
                        if k == 0:
                            yield
                    b = 8 * j + 2 * p + m
                    c = actf(QK2[:, b, :], one(bk), ACT.Copy, [t, t_over, t3], scale=1.0 if j else 0.125)
                    bk.free = [c]
                    tqk[b] = c
                    if m == 1:
                        used_up(w, t)
                    yield
            w = weights("w_in2", 8 + p)
            for i, (q0, nq) in enumerate(QT):
                bk = banks.take()
                for k in range(KB):
                    t = mm3(bk[:, 0:256], [(two(HF, slice(None), k, slice(q0, q0 + P)), block_of(w, k, 0, 256))],
                            [w.split, t_hh[k]] + bk.free, start=k == 0, stop=k == KB - 1)
                c = copy(dve, VV[0:nq, i, p * 256:(p + 1) * 256], bk[0:nq, 0:256], [t, t_vz])
                bk.free = [c]
                if i == 2:
                    used_up(w, t)
                yield
            t_vv[p] = c

        def attend(p):
            for h in (2 * p, 2 * p + 1):
                slope = 2.0 ** (-(h + 1))
                ob = banks.take()
                for i, (q0, nq) in enumerate(QT):
                    nk = q0 + nq
                    bc = [banks.take(), banks.take()]
                    for c in range(2):
                        t = mm(bc[c][0:nq, 0:nk], [(QK2[64 * c:64 * c + 64, h, q0:q0 + nq], QK2[64 * c:64 * c + 64, 8 + h, 0:nk])],
                               [tqk[h], tqk[8 + h]] + bc[c].free)
                    pb = ps_.take()
                    for c in range(2):
                        tb = stt(pb[0:nq, c, 0:nk], c2(f"nd{i}")[0:nq, :], slope, bc[c][0:nq, 0:nk], ALU.mult, ALU.add, [t, c2.tok] + pb.free)
                        bc[c].free = [tb]
                    sv = str_.take()
                    t = rmax(sv[0:nq, 0:2], pb[0:nq, :, 0:nk], AX.X, [tb] + sv.free)
                    t = ts(dve, sv[0:nq, 2:4], sv[0:nq, 0:2], -1.0, None, ALU.mult, None, [t])
                    for c in range(2):
                        te = actf(pb[0:nq, c, 0:nk], pb[0:nq, c, 0:nk], ACT.Exp, [t], bias=sv[0:nq, 2 + c:3 + c],
                                  accum_out=sv[0:nq, 4 + c:5 + c])
                    t = recip(sv[0:nq, 6:8], sv[0:nq, 4:6], [te])
                    t = ts(dve, sv[0:nq, 7:8], sv[0:nq, 7:8], lm[0:nq, 2:3], None, ALU.mult, None, [t, t_lam])
                    t1 = ts(dve, pb[0:nq, 1, 0:nk], pb[0:nq, 1, 0:nk], sv[0:nq, 7:8], None, ALU.mult, None, [t])
                    t1 = stt(pb[0:nq, 0, 0:nk], pb[0:nq, 0, 0:nk], sv[0:nq, 6:7], pb[0:nq, 1, 0:nk], ALU.mult, ALU.subtract, [t1])
                    sv.free = [t1]
                    yield
                    bt = banks.take()
                    for j in range(i + 1):
                        k0, n_ = QT[j]
                        tx = tr(bt[0:n_, j * P:j * P + nq], pb[0:nq, 0, k0:k0 + n_], [t1] + bt.free, n=nq)
                    at = at_.take()
                    c1 = copy(act, at[0:16, 0, 0:nq], bt[0:16, 0:nq], [tx] + at.free)
                    if i:
                        c1 = copy(act, at[:, 1:i + 1, 0:nq], bt[:, P:(i + 1) * P].rearrange("p (j q) -> p j q", j=i), [tx])
                    bt.free = [c1]
                    pb.free = [tx]
                    yield
                    t = mm(ob[:, q0:q0 + nq], [(VV[:, j, h * P:(h + 1) * P], at[:, j, 0:nq]) for j in range(i + 1)],
                           [c1, t_vv[p]] + ob.free)
                    at.free = [t]
                f = tfr.take()
                c = copy(act, f[:, 0:L], one(ob), [t] + f.free)
                ob.free = [c]
                s = sqr.take()
                d = tt(pool, s[:, 0:L], f[:, 0:L], f[:, 0:L], ALU.mult, [c] + s.free)
                yield
                bs = banks.take()
                e = mm(bs[:, 0:L], [(ones, s[:, 0:L])], [d] + bs.free)
                s.free = [e]
                rs, f1, f2 = rstd(bs[:, 0:L], L, 1.0 / P, [e])
                bs.free = [f1]
                t = stt(f[:, 0:L], f[:, 0:L], lm[:, 3:4], rs[:, 0:L], ALU.mult, ALU.mult, [f2, c, t_sub])
                rs.free = [t]
                t_ot[h] = split(OT[0][:, h, :], OT[1][:, h, :], f[:, 0:L], [t])
                f.free = [t_ot[h]]
                yield

        drain(project_heads(0))
        for p in range(4):
            side = project_heads(p + 1) if p < 3 else iter(())
            weave(attend(p), side, 1, 1)
            drain(side)
        tr_ = mixer_out(0, t_ot)
        sa.close()
        tr_ = mlp(0, tr_, 0)

        t_hh = norm_h(0, tr_, lambda k: n2[:, 4, k:k + 1])
        sa = ExitStack()
        BCU = sb("BCU", 24 * L, scope=sa)[:, :].rearrange("p (b t) -> p b t", b=24)
        yv = Ring([sb(f"yv{i}", L, scope=sa)[:, :] for i in range(2)])
        cv = sm("conv2").rearrange("p (b j) -> p b j", b=8)
        t_ot = [None] * KB
        for p in range(4):
            tb_ = {}
            for j in range(3):
                w = weights("w_in2", 12 + 4 * j + p)
                for m in range(2):
                    bk = banks.take()
                    t = proj(w, m, one(bk), bk.free, x=HF, tx=t_hh)
                    c = copy(act, BCU[:, 8 * j + 2 * p + m, :], one(bk), [t, tr_[7]])
                    bk.free = [c]
                    tb_[j, m] = c
                used_up(w, t)
            for m in range(2):
                k = 2 * p + m
                u_ = BCU[:, 16 + k, :]
                y_ = yv.take()
                t = tt(pool, u_, u_, BCU[:, 8 + k, :], ALU.mult, [tb_[1, m], tb_[2, m]])
                t = ts(dve, y_.ap, u_, cv[:, k, 2:3], None, ALU.mult, None, [t] + y_.free)
                for j in (1, 2):
                    t = stt(y_[:, j:L], u_[:, 0:L - j], cv[:, k, 2 - j:3 - j], y_[:, j:L], ALU.mult, ALU.add, [t])
                t = tt(pool, y_.ap, y_.ap, BCU[:, k, :], ALU.mult, [t, tb_[0, m]])
                t_ot[k] = split(OT[0][:, k, :], OT[1][:, k, :], y_.ap, [t])
                y_.free = [t_ot[k]]
        tr_ = mixer_out(1, t_ot)
        sa.close()
        tr_ = mlp(1, tr_, META)
        t_out = misc[3].start(sp, out, R[:, :, META:L], tr_)

        s2.close()

        for q in (pe, act, dve, pool, sp):
            q.number()
        block = ctx.enter_context(nc.Block())

        @block.tensor
        def _(e):
            pe.emit(e)

        @block.scalar
        def _(e):
            act.emit(e)

        @block.vector
        def _(e):
            dve.emit(e)

        @block.gpsimd
        def _(e):
            pool.emit(e)

        @block.sync
        def _(e):
            sp.emit(e)
            e.wait_ge(t_out.q.sem, t_out.value)


def tile_weights(w, cols=256):
    K, N = w.shape
    return np.ascontiguousarray(w.reshape(K // P, P, N // cols, cols).transpose(2, 1, 0, 3)).reshape(N // cols, P, -1)


def by_feature(v):
    v = np.asarray(v)
    return v.reshape(-1, P).T


def kernel(**inputs):
    import concourse.bacc as bacc
    from concourse.bass_utils import run_bass_kernel_spmd

    a = {k: np.asarray(v) for k, v in inputs.items()}
    wi = a["w_in"][0]
    q3, z, ba, rest = wi[:, :3072], wi[:, 3072:4096], wi[:, 4096:4112], wi[:, 4112:]
    w_in = np.concatenate([tile_weights(x) for x in (q3, z, rest)])
    every = lambda v: np.broadcast_to(np.asarray(v).reshape(1, -1), (P, v.size))
    small = {
        "c": by_feature(a["c"][0]), "b_ada": by_feature(a["b_ada"][0]), "g_mix": by_feature(a["g_mix"][0]),
        "g_ffn": by_feature(a["g_ffn"][0]),
        "conv": a["gdn_conv_w"][0].reshape(4, 24, P).transpose(2, 1, 0).reshape(P, 96),
        "gdn_g": a["gdn_norm_g"].reshape(P, 1), "dq_g": a["dil_q_norm_g"].reshape(P, 1),
        "dk_g": a["dil_k_norm_g"].reshape(P, 1),
        "norm2": by_feature(a["norm_g_2"]),
        "conv2": a["conv_w_2"][0].reshape(3, 8, P).transpose(2, 1, 0).reshape(P, 24),
        "subln": a["subln_g_2"].reshape(P, 1), "a_log": every(a["gdn_a_log"]), "dt": every(a["gdn_dt_bias"]),
        "rbias": every(a["router_bias"]), 
    }
    extra = {
        "lam": every(a["lambda_params_2"]),
        "w_ba": ba.reshape(8, P, 16).transpose(1, 0, 2).reshape(P, 128),
        "w_r": a["w_router"][0].reshape(8, P, 64).transpose(1, 0, 2).reshape(P, 512),
    }
    x = np.concatenate([a["meta_tokens_2"], a["x"][0]], axis=0)
    arrays = {
        "x": x.T.reshape(8, P, L).transpose(1, 0, 2),
        "small": np.concatenate([small[n] for n, _ in SMALL], axis=1),
        **constants(),
        **extra,
        "w_ada": tile_weights(a["w_ada"][0]),
        "w_in": w_in,
        "w_up_gdn": tile_weights(a["w_up_gdn"][0]),
        "w_up_dil": tile_weights(a["w_up_dil"][0], 512),
        "w_out": tile_weights(a["w_out"][0]),
        "w_eg": a["w_exp_gate"][0].reshape(NE, 8, P, 256).transpose(0, 2, 1, 3).reshape(NE, P, 2048),
        "w_eu": a["w_exp_up"][0].reshape(NE, 8, P, 256).transpose(0, 2, 1, 3).reshape(NE, P, 2048),
        "w_ed": a["w_exp_down"][0].reshape(NE, 2, P, 1024).transpose(0, 2, 1, 3).reshape(NE, P, 2048),
        "w_sg": tile_weights(a["w_sh_gate"][0])[0],
        "w_su": tile_weights(a["w_sh_up"][0])[0],
        "w_sd": tile_weights(a["w_sh_down"][0], 1024)[0],
        "w_in2": np.concatenate([tile_weights(a["w_in_2"][i]) for i in range(2)]),
        "w_out2": np.concatenate([tile_weights(a["w_out_2"][i]) for i in range(2)]),
        "w_up2": np.concatenate([tile_weights(a["w_up_2"][i]) for i in range(2)]),
        "w_down2": np.ascontiguousarray(a["w_down_2"].reshape(2, 4, 8, P, 4, 256).transpose(0, 4, 1, 3, 2, 5)).reshape(32, P, 2048),
    }
    nc = bacc.Bacc("TRN2", target_bir_lowering=False, num_devices=1)
    arrays = {f"in_{k}": np.ascontiguousarray(v) for k, v in arrays.items()}
    ins = {k[3:]: nc.dram_tensor(k, v.shape, F32, kind="ExternalInput").ap() for k, v in arrays.items()}
    out = nc.dram_tensor("out_0", (P, KB, T), F32, kind="ExternalOutput").ap()
    program(nc, ins, out)
    r = run_bass_kernel_spmd(nc, [arrays], core_ids=[0])
    y = r.results[0]["out_0"]
    return y.transpose(1, 0, 2).reshape(D, T).T.reshape(1, T, D)
```

```python
from contextlib import ExitStack

import concourse.bass as bass
import numpy as np
from concourse import mybir

ALU = mybir.AluOpType
ACT = mybir.ActivationFunctionType
AX = mybir.AxisListType
F32 = mybir.dt.float32
F32R = mybir.dt.float32r

P = 128
D = 1024
KB = 8
T = 256
META = 16
L = T + META
NH = 8
NSLOT = 4
NG = 3
NE = 64
DFF = 4096
EPS = 1e-6
BIG = 1e30
LAM0 = 0.2
RAW = 4
SMALL = [("c", 8), ("b_ada", 48), ("g_mix", 8), ("g_ffn", 8), ("conv", 96), ("gdn_g", 1),
         ("dq_g", 1), ("dk_g", 1), ("norm2", 64), ("conv2", 24), ("subln", 1),
         ("a_log", 8), ("dt", 8), ("rbias", 64)]
LEVELS = [1, 2, 4, 8, 16, 32, 64]
CONST = {"cn": [("ident", 128), ("ones", 128), ("tri", 128), ("eps", 1)],
         "cg": [("pm1", 128), ("pm2", 128), ("lo1", 128)] + [(f"up{s}", 128) for s in LEVELS],
         "cd": [("dm0", 384), ("dm1", 768)],
         "c2": [("nd0", 16), ("nd1", 144), ("nd2", 272)]}


def columns(table):
    at, out = 0, {}
    for name, n in table:
        out[name] = (at, n)
        at += n
    return out, at


def constants():
    i = np.arange(P)[:, None]
    j = np.arange(P)[None, :]
    k2 = np.arange(2 * P)[None, :]

    def low(a, b, s):
        return (a // (2 * s) == b // (2 * s)) & (a // s % 2 == 1) & (b // s % 2 == 0)

    def dil(q, k, g):
        dist = q - k
        ok = (dist >= 0) & ((dist <= 128) if g == 0 else (dist % (4 if g == 1 else 16) == 0))
        return np.where(ok, 0.0, -BIG)

    def away(q0, nk):
        dist = (i + q0) - np.arange(nk)[None, :]
        return np.where(dist >= 0, -dist, -BIG)

    parts = {
        "cn": [np.eye(P), np.ones((P, P)), i <= j, np.full((P, 1), EPS)],
        "cg": [np.where(j < i, 0.0, BIG), np.where(i <= j, 0.0, BIG), low(i, j, 1)] + [low(j, i, s) for s in LEVELS],
        "cd": [dil(i, j, g) for g in range(NG)] + [dil(i + P, k2, g) for g in range(NG)],
        "c2": [away(0, 16), away(16, 144), away(144, 272)],
    }
    return {n: np.concatenate(p, axis=1).astype(np.float32) for n, p in parts.items()}


class Tok:

    def __init__(self, q, n):
        self.q, self.n, self.used = q, n, False


class Queue:

    def __init__(self, name, sem):
        self.name, self.sem, self.ops = name, sem, []

    def add(self, fn, waits):
        t = Tok(self, len(self.ops))
        for w in waits:
            if w is not None:
                w.used = True
        self.ops.append((fn, [w for w in waits if w is not None], t))
        return t

    def number(self):
        n = 0
        for _, _, t in self.ops:
            if t.used and t.q is self:
                n += 1
            t.value = n

    def emit(self, eng):
        seen = {}
        for fn, waits, t in self.ops:
            need = {}
            for w in waits:
                s, v = (w.q.sem, w.value)
                if v > need.get(s, (0, 0))[0]:
                    need[s] = (v, 0)
            for s, (v, _) in need.items():
                if seen.get(s, 0) < v:
                    eng.wait_ge(s, v)
                    seen[s] = v
            ins = fn(eng)
            if t.used and t.q is self:
                ins.then_inc(self.sem, 1)


class DmaLine:

    def __init__(self, sem):
        self.sem, self.count = sem, 0

    def start(self, queue, out, in_, waits):
        self.count += 16
        t = Tok(self, self.count)
        t.value = self.count
        queue.add(lambda e: e.dma_start(out, in_).then_inc(self.sem, 16), waits)
        return t


class Buf:

    def __init__(self, ap):
        self.ap, self._free, self.held = ap, [], False

    def __getitem__(self, k):
        return self.ap[k]

    @property
    def free(self):
        return self._free

    @free.setter
    def free(self, toks):
        self._free, self.held = list(toks), False


class Ring:
    def __init__(self, aps):
        self.bufs, self.n = [Buf(a) for a in aps], 0

    def take(self):
        for _ in self.bufs:
            b = self.bufs[self.n % len(self.bufs)]
            self.n += 1
            if not b.held:
                b.held = True
                return b
        raise AssertionError("every buffer is held")


def stream_plan():
    out = [("w_ada", n) for n in range(8)]
    for p in range(4):
        for j, n in enumerate((p, 4 + p, 8 + p, 12 + p)):
            out += [("w_in", n), ("w_ada", 8 + 4 * p + j)]
    out += [("w_in", n) for n in range(34, 42)]
    out += [("w_in", 16 + n + o) for o in range(2) for n in range(0, 18, 2)]
    out += [("w_up_gdn", n) for n in range(4)] + [("w_up_dil", n) for n in range(2)] + [("w_out", n) for n in range(4)]
    before = None
    for e in [NE] + list(range(NE)):
        out += [("w_eg", e), ("w_eu", e)]
        if before is not None:
            out.append(("w_ed", before))
        before = e
    out.append(("w_ed", before))
    for p in range(4):
        out += [("w_in2", p), ("w_in2", 4 + p), ("w_in2", 8 + p)]
    for i in range(2):
        out += [("w_out2", 4 * i + n) for n in range(4)]
        out += [("w_up2", 16 * i + n) for n in range(16)] + [("w_down2", 16 * i + n) for n in range(16)]
        if i == 0:
            out += [("w_in2", 12 + 4 * j + p) for p in range(4) for j in range(3)]
    return out


def weave(mains, side, num, den):
    n = 0
    mains = list(mains)
    while mains:
        for g in list(mains):
            if next(g, mains) is mains:
                mains.remove(g)
                continue
            n += num
            while n >= den:
                n -= den
                next(side, None)


def drain(g):
    for _ in g:
        pass


def program(nc, ins, out):
    SM, nsm = columns(SMALL)
    CN, ncn = columns(CONST["cn"])
    ctx = ExitStack()
    with ctx:
        def sb(name, cols, dt=F32, scope=ctx):
            return scope.enter_context(nc.sbuf_tensor(name, [P, cols], dt))

        def sbr(name, cols, scope=ctx):
            return sb(name + "_h", cols, F32R, scope)[:, :], sb(name + "_l", cols, F32R, scope)[:, :]

        def sem(name):
            return ctx.enter_context(nc.semaphore(name))

        pe, act, dve, pool, sp = (Queue(n, sem("s_" + n)) for n in ("pe", "act", "dve", "pool", "sp"))
        psum = [ctx.enter_context(nc.psum_tensor(f"ps{i}", [P, 512], F32)) for i in range(8)]

        raw = sb("wraw", RAW * 2048)
        sm_t = sb("sm", nsm)
        cn_t = sb("cn", ncn)
        R = sb("R", KB * L)[:, :].rearrange("p (k t) -> p k t", k=KB)
        HH, HL = (a.rearrange("p (k t) -> p k t", k=KB) for a in sbr("H", KB * L))
        YR = sbr("Y", KB * L)
        wpair = [sbr(f"w{i}", 2048) for i in range(2)]

        def sm(name, a=0, n=None):
            o, w = SM[name]
            return sm_t[:, o + a:o + a + (w - a if n is None else n)]

        def cn(name, a=0, n=None):
            o, w = CN[name]
            return cn_t[:, o + a:o + a + (w - a if n is None else n)]

        ident, ones = cn("ident"), cn("ones")

        def fetch(name, scope, waits):
            table, total = columns(CONST[name])
            t_ = sb("k" + name, total, scope=scope)

            def get(n):
                o, w = table[n]
                return t_[:, o:o + w]
            get.tok = DmaLine(sem("s_" + name)).start(sp, t_[:, :], ins[name], waits)
            return get

        def fetch_all(name, cols, scope, waits):
            t_ = sb("k" + name, cols, scope=scope)[:, :]
            return t_, DmaLine(sem("s_" + name)).start(sp, t_, ins[name], waits)

        misc = [DmaLine(sem(f"s_m{i}")) for i in range(4)]
        t_sm = misc[1].start(act, sm_t[:, :], ins["small"], [])
        t_x = misc[2].start(act, R, ins["x"], [])
        t_cn = misc[0].start(act, cn_t[:, :], ins["cn"], [])

        plan = stream_plan()
        lines = [DmaLine(sem(f"s_w{i}")) for i in range(RAW)]
        raws = [Buf(raw[:, i * 2048:(i + 1) * 2048]) for i in range(RAW)]
        state = {"at": 0, "loaded": 0, "split": 0, "pairs": 0, "eager": False}
        units = {}

        def source(name, n):
            if n == NE and name in ("w_eg", "w_eu", "w_ed"):
                return ins[{"w_eg": "w_sg", "w_eu": "w_su", "w_ed": "w_sd"}[name]]
            return ins[name][n]

        class Unit:
            pass

        def f32(ap):
            return ap.bitcast(F32)

        def weights(*key):
            n = state["at"]
            assert plan[n] == key, (plan[n], key)
            state["at"] += 1
            while state["loaded"] < min(len(plan), n + RAW):
                m = state["loaded"]
                b = raws[m % RAW]
                u = units[m] = Unit()
                u.raw, u.k = b, b.ap.rearrange("p (k n) -> p k n", k=KB)
                u.tok = lines[m % RAW].start(sp, b.ap, source(*plan[m]), b.free)
                u.part, u.half = [None, None], False
                state["loaded"] += 1
            if n >= 7:
                split_next()
            return units.pop(n)

        pair_free = [[[], []], [[], []]]

        def split_next():
            while state["split"] < state["loaded"]:
                if plan[state["split"]][0] != "w_ada":
                    u = units[state["split"]]
                    i = state["pairs"] % 2
                    free = pair_free[i]
                    u.i, (u.h, u.l) = i, wpair[i]
                    a, b, c = (x.rearrange("p (k m n) -> p m k n", k=KB, m=2) for x in (u.h, u.l, u.raw.ap))
                    todo = [m for m in range(2) if u.part[m] is None and free[m] is not None]
                    if len(todo) == 2:
                        th = copy(act, u.h, u.raw.ap, [u.tok] + free[0] + free[1])
                        u.part = [tt(dve, u.l, u.raw.ap, f32(u.h), ALU.subtract, [th] + free[0] + free[1])] * 2
                    else:
                        for m in todo:
                            th = copy(act, a[:, m], c[:, m], [u.tok] + free[m])
                            u.part[m] = tt(dve, b[:, m], c[:, m], f32(a[:, m]), ALU.subtract, [th] + free[m])
                    for m in todo:
                        free[m] = None
                    if None in u.part:
                        return
                    u.split = u.part[1]
                    u.raw.free = [u.split]
                    state["pairs"] += 1
                state["split"] += 1

        def half_used(u, t):
            if not state["eager"]:
                return
            u.half = True
            pair_free[u.i][0] = [t]
            split_next()

        def used(m, u, t):
            half_used(u, t) if m == 0 else used_up(u, t)

        def used_up(u, t):
            if hasattr(u, "i"):
                pair_free[u.i][1] = [t]
                if not u.half:
                    pair_free[u.i][0] = [t]
                if state["eager"]:
                    split_next()
            else:
                u.raw.free = [t]

        def block_of(u, k, c0, n=P, parts=KB):
            w = 2048 // parts
            return u.h[:, k * w + c0:k * w + c0 + n], u.l[:, k * w + c0:k * w + c0 + n]

        def mm(out_ap, pairs, waits, start=True, stop=True, skip=False):
            def f(e):
                n = len(pairs)
                for i, (a, b) in enumerate(pairs):
                    r = e.matmul(out_ap, a, b, start=start and i == 0, stop=stop and i == n - 1,
                                 skip_group_check=skip)
                return r
            return pe.add(f, waits)

        def mm3(out_ap, pairs, waits, start=True, stop=True, skip=False):
            ab = []
            for (ah, al), (bh, bl) in pairs:
                ab += [(ah, bh), (ah, bl), (al, bh)]
            return mm(out_ap, ab, waits, start, stop, skip)

        def two(pair, *idx):
            return pair[0][idx], pair[1][idx]

        def tr(out_ap, in_ap, waits, n=P):
            return pe.add(lambda e: e.transpose(out_ap, in_ap, cn_t[0:n, CN["ident"][0]:CN["ident"][0] + n]), waits)

        def actf(o, i, func, waits, **kw):
            return act.add(lambda e: e.activation(o, i, func, **kw), waits)

        def tt(q, o, a, b, op, waits):
            return q.add(lambda e: e.tensor_tensor(o, a, b, op), waits)

        def ts(q, o, a, s1, s2, op0, op1, waits):
            if s2 is None:
                return q.add(lambda e: e.tensor_scalar(o, a, s1, None, op0), waits)
            return q.add(lambda e: e.tensor_scalar(o, a, s1, s2, op0, op1), waits)

        def stt(o, a, s, b, op0, op1, waits):
            return dve.add(lambda e: e.scalar_tensor_tensor(out=o, in0=a, scalar=s, in1=b, op0=op0, op1=op1), waits)

        def copy(q, o, a, waits):
            if q is act:
                return actf(o, a, ACT.Copy, waits)
            return q.add(lambda e: e.tensor_copy(o, a), waits)

        def recip(o, a, waits):
            return dve.add(lambda e: e.reciprocal(o, a), waits)

        def memset(q, o, v, waits):
            return q.add(lambda e: e.memset(o, v), waits)

        def rmax(o, a, ax, waits):
            return dve.add(lambda e: e.tensor_reduce(o, a, ax, ALU.max), waits)

        banks = Ring([p[:, :] for p in psum])
        eps = cn("eps")
        s1r = Ring([sb(f"st{i}", 512)[:, :] for i in range(4)])

        def rstd(src, n, scale, waits):
            b = s1r.take()
            t1 = actf(b[:, 0:n], src, ACT.Sqrt, list(waits) + b.free + [t_cn], bias=eps, scale=scale)
            t2 = recip(b[:, 0:n], b[:, 0:n], [t1])
            return b, t1, t2

        class Rstd:

            def __init__(self, sq, at, scale, waits):
                self.sv, self.bk, self.at = str_.take(), banks.take(), at
                nt = len(at)
                for i, c in enumerate(at):
                    self.sq = mm(self.bk[:, i:i + 1], [(sq[:, c:c + P], ones[:, 0:1])], list(waits) + self.bk.free)
                r_ = self.sv[:, 0:nt]
                self.t1 = actf(r_, self.bk[:, 0:nt], ACT.Sqrt, [self.sq, t_cn] + self.sv.free, bias=eps, scale=scale)
                self.t2 = recip(r_, r_, [self.t1])

            def spread(self):
                for i, c in enumerate(self.at):
                    t = mm(self.bk[:, c:c + P], [(self.sv[:, i:i + 1].to_broadcast([P, P]), ident)], [self.t1, self.t2])
                self.sv.free = [t]
                return self.bk, t

        def split(oh, ol, src, waits, low=pool):
            th = copy(act, oh, src, waits)
            return tt(low, ol, src, f32(oh), ALU.subtract, [th] + list(waits))

        sqr = Ring([sb(f"sq{i}", 512)[:, :] for i in range(3)])
        tfr = Ring([sb(f"tf{i}", 512)[:, :] for i in range(3)])

        FOUR = tuple(i * P for i in range(4))
        junk = sb("junk", 1)[:, :]

        class Stats:

            def __init__(self, n, lag=0, by=(act, dve, pool), bank=None):
                self.bk, self.n, self.k, self.lag, self.by = bank or banks.take(), n, 0, lag, by
                self.squares = []

            def sum_up(self, lag):
                while len(self.squares) > lag:
                    k, s, t = self.squares.pop(0)
                    self.t = mm(self.bk[:, 0:self.n], [(ones, s[:, 0:self.n])], [t, t_cn] + self.bk.free, start=k == 0, stop=k == KB - 1)
                    s.free = [self.t]

            def add(self, a, tok):
                s, n, k = sqr.take(), self.n, self.k
                w = [tok] + s.free
                q = self.by[k % len(self.by)]
                if q is act:
                    t = actf(s[:, 0:n], a, ACT.Square, w)
                else:
                    t = tt(q, s[:, 0:n], a, a, ALU.mult, w)
                if k == KB - 2:
                    actf(junk, eps, ACT.Sqrt, [t_cn])
                self.squares.append((k, s, t))
                self.sum_up(self.lag)
                self.k += 1

            def done(self):
                assert self.k == KB
                self.sum_up(0)
                rs, ta, tb = rstd(self.bk[:, 0:self.n], self.n, 1.0 / D, [self.t])
                self.bk.free = [ta]
                return rs, tb

        def scaled(x, c0, rs, t_src, gcol, put, t_g=None):
            n = L - c0
            rs, tb = rs
            out_t = []
            for k in range(KB):
                f = tfr.take()
                t = stt(f[:, 0:n], x[:, k, c0:L], gcol(k), rs[:, 0:n], ALU.mult, ALU.mult, [tb, t_g, t_src[k]] + f.free)
                r, f.free = put(k, f[:, 0:n], t)
                out_t.append(r)
            rs.free = [t]
            return out_t

        def to_h(c0, rs, t_src, gcol, shift=None, t_g=None):
            def put(k, f, t):
                h, l = HH[:, k, c0:L], HL[:, k, c0:L]
                if shift is not None:
                    t = ts(dve, f, f, shift(k), None, ALU.add, None, [t])
                th = copy(act, h, f, [t])
                tl = tt(pool, l, f, f32(h), ALU.subtract, [th])
                return tl, [tl]
            return scaled(R, c0, rs, t_src, gcol, put, t_g)

        csl = sb("csl", 8)
        mod = sb("mod", 48)
        s1g = sb("s1g", 8)
        gb = sb("gb", 160)
        lm = sb("lm", 8)
        str_ = Ring([sb(f"sms{i}", 8)[:, :] for i in range(6)])
        sd, sg = ExitStack(), ExitStack()
        qkvz = [Buf(sb(f"qkvz{i}", 2048, scope=sd if i < 2 else sg)[:, :].rearrange("p (b t) -> p b t", b=8)) for i in range(4)]
        wb_ = sbr("wb", 128, sg)
        wb, t_wb = fetch_all("w_ba", 128, sg, [])
        t_cs = actf(csl[:, :], sm("c"), ACT.Silu, [t_sm])

        def ada(n, bk, at):
            w = weights("w_ada", n)
            if n < 8:
                ta = ts(dve, w.k[:, 0, :], w.k[:, 0, :], csl[:, 0:1], None, ALU.mult, None, [w.tok, t_cs])
                for k in range(1, 6):
                    ta = stt(w.k[:, k, :], w.k[:, k, :], csl[:, k:k + 1], w.k[:, k - 1, :], ALU.mult, ALU.add, [ta])
                for k in (6, 7):
                    tb = actf(w.k[:, k, :], w.k[:, k, :], ACT.Copy, [w.tok, t_cs], scale=csl[:, k:k + 1])
                for m in range(2):
                    t = mm(bk[:, at + m:at + m + 1], [(w.k[:, k, m * P:(m + 1) * P], ones[:, 0:1]) for k in (6, 7, 5)],
                           [ta, tb, t_cn] + bk.free)
            else:
                for m in range(2):
                    t = mm(bk[:, at + m:at + m + 1], [(w.k[:, k, m * P:(m + 1) * P], csl[:, k:k + 1]) for k in range(KB)],
                           [w.tok, t_cs] + bk.free)
            used_up(w, t)
            if n < 8:
                return t
            t2 = tt(dve, mod[:, 2 * n:2 * n + 2], bk[:, at:at + 2], sm("b_ada", 2 * n, 2), ALU.add, [t, t_sm])
            return t2

        st = Stats(T)
        for k in range(KB):
            st.add(R[:, k, META:L], t_x)
        rs0 = st.done()
        bk = banks.take()
        for n in range(8):
            t_mod1 = ada(n, bk, 2 * n)
        t_mod1 = tt(dve, mod[:, 0:16], bk[:, 0:16], sm("b_ada", 0, 16), ALU.add, [t_mod1, t_sm])
        bk.free = [t_mod1]
        t = ts(dve, s1g[:, :], mod[:, 8:16], 1.0, None, ALU.add, None, [t_mod1])
        t_s1g = tt(dve, s1g[:, :], s1g[:, :], sm("g_mix"), ALU.mult, [t])
        t_h = to_h(META, rs0, [t_x] * KB, lambda k: s1g[:, k:k + 1], shift=lambda k: mod[:, k:k + 1], t_g=t_s1g)
        HX = (HH[:, :, META:L], HL[:, :, META:L])

        def proj(w, m, o, waits, x=HX, tx=None, k0=0, k1=KB):
            for k in range(k0, k1):
                t = mm3(o, [(block_of(w, k, m * P), two(x, slice(None), k, slice(None)))],
                        [w.part[m], tx[k] if tx else None] + (list(waits) if k == 0 else []), start=k == 0, stop=k == KB - 1)
            return t

        def unit2(key, waits, x=HX, tx=None):
            w = weights(*key)
            bk = banks.take()
            for m in range(2):
                for k in (0, 4):
                    t = proj(w, m, bk[:, m * T:(m + 1) * T], bk.free if m == 0 else [], x=x, tx=tx, k0=k, k1=k + 4)
                    if (m, k) == (0, 4):
                        half_used(w, t)
                    if (m, k) != (1, 4):
                        yield None
            used_up(w, t)
            yield bk, t

        GA, GB = qkvz[0].ap, qkvz[1].ap
        cg = fetch("cg", sg, [])
        conv = sm("conv").rearrange("p (b j) -> p b j", b=24)

        def project_pair(p, S):
            B = qkvz[p]
            S["B"] = B.ap
            for j in range(4):
                for r in unit2(("w_in", 4 * j + p), [], tx=t_h):
                    if r is None:
                        yield
                bk, t = r
                a = banks.take()
                a.free = [ada(8 + 4 * p + j, a, 0)]
                S["mod"] = a.free[0]
                ys = B[:, 2 * j:2 * j + 2, :]
                if j == 3:
                    t2 = actf(ys, bk.ap.rearrange("p (m t) -> p m t", m=2), ACT.Silu, [t] + B.free)
                    bk.free = [t2]
                    S["z"] = t2
                else:
                    for m in range(2):
                        b = 8 * j + 2 * p + m
                        x = bk[:, m * T:(m + 1) * T]
                        y = B[:, 2 * j + m, :]
                        tc = ts(dve, y, x, conv[:, b, 3:4], None, ALU.mult, None, [t, t_sm] + B.free)
                        for i in range(1, 4):
                            tc = stt(y[:, i:T], x[:, 0:T - i], conv[:, b, 3 - i:4 - i], y[:, i:T], ALU.mult, ALU.add, [tc])
                    bk.free = [tc]
                    S["qkv"[j]] = actf(ys, ys, ACT.Silu, [tc])
                yield
            rs = []
            for j in range(2):
                ys = B[:, 2 * j:2 * j + 2, :]
                s = sqr.take()
                s2 = s.ap.rearrange("p (m t) -> p m t", m=2)
                t = actf(s2, ys, ACT.Square, [S["qk"[j]]] + s.free)
                rs.append(Rstd(s, FOUR, 1.0, [t]))
                s.free = [rs[j].sq]
                yield
            for j in range(2):
                ys = B[:, 2 * j:2 * j + 2, :]
                b, t = rs[j].spread()
                t = stt(ys, ys, float(P) ** -0.5 if j == 0 else 1.0, b.ap.rearrange("p (m t) -> p m t", m=2), ALU.mult, ALU.mult, [t])
                b.free = [t]
                S["qk"[j]] = t
                yield

        Ws = [{n: Buf(sb(f"g{n}{s}", 512, scope=sg)[:, :].rearrange("p (m j) -> p m j", m=4))
               for n in ("A", "AT", "M", "N", "D2", "X")} for s in range(2)]
        hws = [[{n: Buf(sb(f"h{n}{s}{m}", 128, scope=sg)[:, :]) for n in
                 ("vb0", "vb1", "kd", "u0", "S1", "u1", "qd")} for m in range(2)] for s in range(2)]
        for h in hws:
            for m in range(2):
                h[m]["r1"] = h[m]["vb0"]
        YH = tuple(a[:, 0:2048].rearrange("p (h t) -> p h t", h=8) for a in YR)
        t_y = [None] * 8

        def bc4(x):
            return x.unsqueeze(1).to_broadcast([P, 4, P])

        def b4(bank):
            return bank.ap.rearrange("p (m j) -> p m j", m=4)

        def delta(p, S0):
            B = S0["B"]

            def cols(b, i):
                return B[:, b, i * P:(i + 1) * P]

            q_ = lambda m, i: cols(m, i)
            k_ = lambda m, i: cols(2 + m, i)
            v_ = lambda m, i: cols(4 + m, i)
            mats = [(m, i) for m in range(2) for i in range(2)]
            tq, tk, tv = S0["q"], S0["k"], S0["v"]
            kk, gbk = banks.take(), banks.take()
            for n, (m, i) in enumerate(mats):
                t_kk = mm(kk[:, n * P:(n + 1) * P], [(k_(m, i), k_(m, i))], [tk] + kk.free)
            for n, (m, i) in enumerate(mats):
                h = 2 * p + m
                t_gb = mm(gbk[:, n * P:(n + 1) * P],
                          [(gg[:, i, h:h + 1].to_broadcast([P, P]), cn("tri"))], [t_g] + gbk.free)
            yield
            hw = hws[p % 2]
            X, A, D2, AT, M, N = (Ws[p % 2][n] for n in ("X", "A", "D2", "AT", "M", "N"))
            UO, PB, QK = A, X, D2
            for n, (m, i) in enumerate(mats):
                h = 2 * p + m
                t = ts(dve, X[:, n, :], gbk[:, n * P:(n + 1) * P], gc[:, i, h:h + 1], None, ALU.subtract, None,
                       [t_gb, t_gc] + X.free)
            t1 = tt(pool, A[:, :, :], X[:, :, :], bc4(cg("pm1")), ALU.add, [t, cg.tok] + A.free)
            t2 = tt(dve, D2[:, :, :], X[:, :, :], bc4(cg("pm2")), ALU.subtract, [t, cg.tok] + D2.free)
            t1 = actf(A[:, :, :], A[:, :, :], ACT.Exp, [t1], scale=-1.0)
            t2 = actf(D2[:, :, :], D2[:, :, :], ACT.Exp, [t2])
            t_x = actf(X[:, :, :], b4(gbk), ACT.Exp, [t1, t2, t])
            gbk.free = [t, t_x]
            t3 = tt(dve, A[:, :, :], b4(kk), A[:, :, :], ALU.mult, [t1, t_kk])
            kk.free = [t3]
            for n, (m, i) in enumerate(mats):
                h = 2 * p + m
                t3b = ts(dve, A[:, n, :], A[:, n, :], beta[:, i, h:h + 1], None, ALU.mult, None, [t3, t_beta])
            yield
            qk = banks.take()
            for n, (m, i) in enumerate(mats):
                t_qk = mm(qk[:, n * P:(n + 1) * P], [(k_(m, i), q_(m, i))], [tq, tk] + qk.free)
            t_qkd = tt(dve, QK[:, :, :], b4(qk), D2[:, :, :], ALU.mult, [t_qk, t2])
            qk.free = [t_qkd]
            yield
            atb = banks.take()
            for n in range(4):
                t4 = tr(atb[:, n * P:(n + 1) * P], A[:, n, :], [t3b] + atb.free)
            t5 = copy(act, AT[:, :, :], b4(atb), [t4] + AT.free)
            atb.free = [t5]
            t6 = tt(pool, M[:, :, :], A[:, :, :], bc4(cg("lo1")), ALU.mult, [t3b] + M.free)
            t_m = tt(pool, M[:, :, :], bc4(ident), M[:, :, :], ALU.subtract, [t6])
            t7 = tt(dve, N[:, :, :], AT[:, :, :], bc4(cg("up1")), ALU.mult, [t5] + N.free)
            t_n = tt(dve, N[:, :, :], bc4(ident), N[:, :, :], ALU.subtract, [t7])
            t_uo = tt(pool, UO[:, :, :], AT[:, :, :], bc4(cg("up2")), ALU.mult, [t5, t4, t6])
            yield
            tt_ = {}
            for m in range(2):
                h = 2 * p + m
                w_ = hw[m]
                tb = banks.take()
                ta = tr(tb[:, 0:P], v_(m, 0), [tv] + tb.free)
                ta = tr(tb[:, P:2 * P], v_(m, 1), [])
                ta = tr(tb[:, 2 * P:3 * P], k_(m, 0), [tk])
                e0 = ts(dve, w_["vb0"].ap, tb[:, 0:P], beta[:, 0, h:h + 1], None, ALU.mult, None, [ta, t_beta] + w_["vb0"].free)
                e1 = ts(dve, w_["vb1"].ap, tb[:, P:2 * P], beta[:, 1, h:h + 1], None, ALU.mult, None, [ta] + w_["vb1"].free)
                e2 = ts(dve, w_["kd"].ap, tb[:, 2 * P:3 * P], kdf[:, 0, h:h + 1], None, ALU.mult, None, [ta, t_kdf] + w_["kd"].free)
                tb.free = [e2]
                e3 = tt(pool, w_["qd"].ap, q_(m, 1), X[:, 2 * m + 1, :], ALU.mult, [t_x, tq] + w_["qd"].free)
                tt_[m] = [e0, e1, e2, e3]
            t_pb = [tt_[1][3]]
            yield
            for s in LEVELS[1:]:
                last = s == 64
                p1 = banks.take()
                for n in range(4):
                    tp = mm(p1[:, n * P:(n + 1) * P], [(UO[:, n, :], M[:, n, :])], [t_uo, t_m] + p1.free)
                tpc = copy(act, PB[:, :, :], b4(p1), [tp] + t_pb)
                p1.free = [tpc]
                if not last:
                    t_uo = tt(pool, UO[:, :, :], AT[:, :, :], bc4(cg(f"up{2 * s}")), ALU.mult, [tp])
                yield
                p3 = banks.take()
                tmm = None
                if not last:
                    p2 = banks.take()
                    for n in range(4):
                        tmm = mm(p2[:, n * P:(n + 1) * P], [(N[:, n, :], PB[:, n, :])], [tpc, t_n] + p2.free)
                    t_m = tt(dve, M[:, :, :], M[:, :, :], b4(p2), ALU.subtract, [tmm, tp])
                    p2.free = [t_m]
                for n in range(4):
                    tn = mm(p3[:, n * P:(n + 1) * P], [(PB[:, n, :], N[:, n, :])], [tpc, t_n] + p3.free)
                t_pb = [tn]
                t_n = tt(dve, N[:, :, :], N[:, :, :], b4(p3), ALU.subtract, [tn, tmm])
                p3.free = [t_n]
                yield
            A.free = AT.free = M.free = X.free = [t_n, t_m, t_uo]

            def small(dst, lhs, rhs, waits, lfree, q=act):
                bu = banks.take()
                a = mm(bu[:, 0:P], [(lhs, rhs)], list(waits) + bu.free)
                c = copy(q, dst.ap, bu[:, 0:P], [a] + dst.free)
                bu.free = [c]
                for f in lfree:
                    f.free = [a]
                return a, c

            for m in range(2):
                w_ = hw[m]
                tt_[m].append(small(w_["u0"], N[:, 2 * m, :], w_["vb0"].ap, [t_n, tt_[m][0]], [w_["vb0"]])[1])
            yield
            for m in range(2):
                w_ = hw[m]
                tt_[m].append(small(w_["S1"], w_["kd"].ap, w_["u0"].ap, [tt_[m][4], tt_[m][2]], [w_["kd"]])[1])
            yield
            for m in range(2):
                w_ = hw[m]
                bu = banks.take()
                a = mm(bu[:, 0:P], [(k_(m, 1), w_["S1"].ap)], [tt_[m][5]] + bu.free)
                c = stt(w_["r1"].ap, bu[:, 0:P], nbeg[:, 1, 2 * p + m:2 * p + m + 1], w_["vb1"].ap, ALU.mult, ALU.add,
                        [a, t_nbeg, tt_[m][1]] + w_["r1"].free)
                bu.free = [c]
                w_["vb1"].free = [c]
                tt_[m].append(c)
            yield
            for m in range(2):
                w_ = hw[m]
                a, c = small(w_["u1"], N[:, 2 * m + 1, :], w_["r1"].ap, [tt_[m][6]], [w_["r1"]])
                tt_[m].append(c)
            N.free = [a]
            yield
            outs = []
            for m in range(2):
                w_ = hw[m]
                bo = banks.take()
                a = mm(bo[:, 0:P], [(w_["u0"].ap, QK[:, 2 * m, :])], [tt_[m][4], t_qkd] + bo.free)
                a = mm(bo[:, P:2 * P], [(w_["S1"].ap, w_["qd"].ap), (w_["u1"].ap, QK[:, 2 * m + 1, :])],
                       [tt_[m][7], tt_[m][3], tt_[m][5]])
                for nm in ("u0", "S1", "qd", "u1"):
                    w_[nm].free = [a]
                f, s = (x.ap.rearrange("p (h m) j -> p h (m j)", h=2)[:, m, :] for x in (A, M))
                c = copy(dve, f, bo[:, 0:T], [a, t_n, t_m, t_uo])
                bo.free = [c]
                d = tt(pool, s, f, f, ALU.mult, [c])
                outs.append((f, s, d))
            D2.free = [a]
            yield
            rs = [Rstd(s, (0, P), 1.0 / P, [d]) for f, s, d in outs]
            yield
            for m in range(2):
                h = 2 * p + m
                f, s, d = outs[m]
                bs, f2 = rs[m].spread()
                g1 = stt(f, f, sm("gdn_g"), bs[:, 0:T], ALU.mult, ALU.mult, [f2])
                bs.free = [g1]
                g2 = tt(pool, f, f, B[:, 6 + m, :], ALU.mult, [g1, S0["z"]])
                t_y[h] = split(YH[0][:, h, :], YH[1][:, h, :], f, [g2])
            A.free = [t_y[2 * p], t_y[2 * p + 1]]
            M.free = [rs[1].sq]
            qkvz[p].free = [g2, t_y[2 * p], t_y[2 * p + 1], a]
            yield

        def gate(first, G, tg, war):
            for u in range(4):
                for r in unit2(("w_in", first + u), [], tx=t_h):
                    if r is None:
                        yield
                bk, t = r
                c = actf(G[:, 2 * u:2 * u + 2, :], bk.ap.rearrange("p (m t) -> p m t", m=2), ACT.Sigmoid, [t] + war)
                bk.free = [c]
                tg[u] = c
                yield

        t_ga, t_gb_ = [None] * 4, [None] * 4
        Ss = [{} for _ in range(4)]
        beta, gg, gc, egc, nbeg, kdf, tmp16 = (gb[:, 16 * i:16 * i + 16].rearrange("p (t h) -> p t h", t=2) for i in range(7))
        ea = gb[:, 112:120]
        t_wba = split(wb_[0], wb_[1], wb, [t_wb])
        first = project_pair(0, Ss[0])
        t_beta = t_g = t_gc = t_kdf = t_nbeg = None

        def decays():
            nonlocal t_beta, t_g, t_gc, t_kdf, t_nbeg
            bk = banks.take()
            t = mm3(bk[0:16, 0:T], [((wb_[0][:, 16 * k:16 * k + 16], wb_[1][:, 16 * k:16 * k + 16]), two(HX, slice(None), k, slice(None)))
                                    for k in range(KB)], t_h + [t_wba] + bk.free)
            bat = sqr.take()
            t = copy(act, bat[0:16, 0:T], bk[0:16, 0:T], [t] + bat.free)
            bk.free = [t]
            yield
            bk = banks.take()
            ba = bk[:, 0:32].rearrange("p (t c) -> p t c", t=2)
            for i in range(2):
                t = tr(ba[:, i, :], bat[0:16, i * P:(i + 1) * P], [t] + bk.free, n=16)
            bat.free = [t]
            t_e = actf(ea, sm("a_log"), ACT.Exp, [t_sm])
            t1 = actf(beta, ba[:, :, 0:8], ACT.Exp, [t], scale=-1.0)
            t2 = tt(dve, gg, ba[:, :, 8:16], sm("dt").unsqueeze(1).to_broadcast([P, 2, 8]), ALU.add, [t, t1])
            bk.free = [t2]
            t3 = ts(dve, beta, beta, 1.0, None, ALU.add, None, [t1])
            t_beta = recip(beta, beta, [t3])
            ab = tmp16
            t4 = actf(ab, gg, ACT.Abs, [t2])
            t5 = actf(ab, ab, ACT.Exp, [t4], scale=-1.0)
            t6 = actf(ab, ab, ACT.Ln, [t5], bias=1.0)
            t7 = stt(gg, gg, 0.0, ab, ALU.max, ALU.add, [t6])
            t_g = stt(gg, gg, -1.0, ea.unsqueeze(1).to_broadcast([P, 2, 8]), ALU.mult, ALU.mult, [t7, t_e])
            yield
            bk = banks.take()
            ta = mm(bk[:, 0:16], [(cn("tri"), gb[:, 16:32])], [t_g] + bk.free)
            ta = mm(bk[:, 16:24], [(ones, gb[:, 16:24])], [t_g])
            t_gc = copy(dve, gb[:, 32:48], bk[:, 0:16], [ta])
            t10 = tt(dve, kdf[:, 0, :], bk[:, 16:24], gc[:, 0, :], ALU.subtract, [t_gc])
            bk.free = [t10]
            t_kdf = actf(kdf[:, 0, :], kdf[:, 0, :], ACT.Exp, [t10])
            t12 = actf(egc, gc, ACT.Exp, [t_gc])
            t_nbeg = stt(nbeg, egc, -1.0, beta, ALU.mult, ALU.mult, [t12, t_beta])
            yield

        for _ in range(16):
            next(first)
        second = project_pair(1, Ss[1])
        weave([first, decays()], second, 1, 1)
        drain(second)

        def more_pairs():
            yield from project_pair(2, Ss[2])
            yield from project_pair(3, Ss[3])

        def both_gates():
            yield from gate(34, GA, t_ga, qkvz[0].free)
            yield from gate(38, GB, t_gb_, qkvz[1].free)

        side = more_pairs()
        weave([delta(0, Ss[0]), delta(1, Ss[1])], side, 8, 5)
        drain(side)
        side = both_gates()
        weave([delta(2, Ss[2]), delta(3, Ss[3])], side, 1, 1)
        drain(side)
        t_mod2 = Ss[3]["mod"]
        sg.close()

        t_qd = [None] * 24
        t_vd = [None] * 6

        def project_dil(which):
            before = []
            for u in which:
                for r in unit2(("w_in", 16 + u), [], tx=t_h):
                    if r is None:
                        yield
                bk, t = r
                ys = QD[:, 2 * u:2 * u + 2, :]
                y1 = bk.ap.rearrange("p (m t) -> p m t", m=2)
                c = copy(dve, ys, y1, [t] + over)
                s = sqr.take()
                d = tt(pool, s.ap.rearrange("p (m t) -> p m t", m=2), ys, ys, ALU.mult, [c] + s.free)
                bk.free = [c]
                if before:
                    before.pop()()
                rs = Rstd(s, FOUR, 1.0 / P, [d])
                s.free = [rs.sq]

                def norm(rs=rs, ys=ys, u=u, c=c):
                    bs, f2 = rs.spread()
                    t = stt(ys, ys, sm("dq_g" if u < 6 else "dk_g"), bs.ap.rearrange("p (m t) -> p m t", m=2), ALU.mult, ALU.mult, [f2, c])
                    bs.free = [t]
                    t_qd[2 * u] = t_qd[2 * u + 1] = t
                before.append(norm)
                yield
            yield
            before.pop()()

        se = ExitStack()
        YB = tuple(a.rearrange("p (h t) -> p h t", h=4) for a in sbr("YB", 1024, se))
        sf = ExitStack()
        QD = sb("QD", 6144, scope=sf)[:, :].rearrange("p (b t) -> p b t", b=24)
        VD = sb("VD", 3072, scope=sf)[:, :].rearrange("p (t n) -> p t n", t=2)
        pr = Ring([sb(f"pr{i}", 768, scope=sf)[:, :] for i in range(2)])
        ptr = Ring([sb(f"pt{i}", 768, scope=sf)[:, :] for i in range(2)])
        over = t_y[4:] + qkvz[2].free + qkvz[3].free + [x for w_ in Ws for b in w_.values() for x in b.free] + \
            [x for hw in hws for w_ in hw for b in w_.values() for x in b.free]
        for b in pr.bufs + ptr.bufs:
            b.free = over
        cd = fetch("cd", sf, over)
        t_yb = [None] * NSLOT

        def project_v(which):
            for u in which:
                w = weights("w_in", 28 + u)
                bk = banks.take()
                for i in range(2):
                    for k in range(KB):
                        t = mm3(bk[:, i * T:(i + 1) * T], [(two(HX, slice(None), k, slice(i * P, (i + 1) * P)), block_of(w, k, 0, 256))],
                                [w.split, t_h[k]] + bk.free, start=k == 0, stop=k == KB - 1)
                used_up(w, t)
                c = copy(act, VD[:, :, u * 256:(u + 1) * 256], bk.ap.rearrange("p (t n) -> p t n", t=2), [t] + over)
                bk.free = [c]
                t_vd[u] = c
                yield


        def dil_attention(s):
            if True:
                yb = banks.take()
                for i in range(2):
                    nk = P * (i + 1)
                    b1 = banks.take()
                    b2 = banks.take() if i else None
                    for g in range(NG):
                        h = g * NSLOT + s
                        o_ = (b2 if i and g == 2 else b1)
                        c0 = 0 if (i and g == 2) else g * nk
                        t = mm(o_[:, c0:c0 + nk], [(QD[:, h, i * P:(i + 1) * P], QD[:, 12 + h, 0:nk])],
                               [t_qd[h], t_qd[12 + h]] + o_.free)
                    pb = pr.take()
                    sc = float(P) ** -0.5
                    dmk = cd("dm1") if i else cd("dm0")
                    if i:
                        ta = stt(pb[:, 0:512], b1[:, 0:512], sc, dmk[:, 0:512], ALU.mult, ALU.add, [t, cd.tok] + pb.free)
                        tb = stt(pb[:, 512:768], b2[:, 0:256], sc, dmk[:, 512:768], ALU.mult, ALU.add, [t])
                        b1.free, b2.free = [ta], [tb]
                        n = 768
                    else:
                        tb = stt(pb[:, 0:384], b1[:, 0:384], sc, dmk, ALU.mult, ALU.add, [t, cd.tok] + pb.free)
                        b1.free = [tb]
                        n = 384
                    sv = str_.take()
                    t = rmax(sv[:, 0:1], pb[:, 0:n], AX.X, [tb] + sv.free)
                    t = ts(dve, sv[:, 1:2], sv[:, 0:1], -1.0, None, ALU.mult, None, [t])
                    t = actf(pb[:, 0:n], pb[:, 0:n], ACT.Exp, [t], bias=sv[:, 1:2], accum_out=sv[:, 2:3])
                    t = recip(sv[:, 3:4], sv[:, 2:3], [t])
                    t = ts(dve, pb[:, 0:n], pb[:, 0:n], sv[:, 3:4], None, ALU.mult, None, [t])
                    sv.free = [t]
                    yield
                    pt = ptr.take()
                    nb = n // P
                    for j0 in range(0, nb, 4):
                        bt = banks.take()
                        j1 = min(nb, j0 + 4)
                        for j in range(j0, j1):
                            tx = tr(bt[:, (j - j0) * P:(j - j0 + 1) * P], pb[:, j * P:(j + 1) * P], [t] + bt.free)
                        c1 = copy(act, pt[:, j0 * P:j1 * P], bt[:, 0:(j1 - j0) * P], [tx] + pt.free)
                        bt.free = [c1]
                    pb.free = [tx]
                    yield
                    pairs = []
                    for g in range(NG):
                        h = g * NSLOT + s
                        for kt in range(i + 1):
                            j = g * (i + 1) + kt
                            pairs.append((VD[:, kt, h * P:(h + 1) * P], pt[:, j * P:(j + 1) * P]))
                    t = mm(yb[:, i * P:(i + 1) * P], pairs, [c1] + t_vd[s // 2::2] + yb.free)
                    pt.free = [t]
                c = copy(act, YB[0][:, s, :], yb[:, 0:T], [t] + over)
                c = tt(dve, YB[1][:, s, :], yb[:, 0:T], f32(YB[0][:, s, :]), ALU.subtract, [c])
                yb.free = [c]
                t_yb[s] = c
                yield

        over2 = []

        def up_gdn():
            for u in range(4):
                for r in unit2(("w_up_gdn", u), [], x=YH, tx=t_y):
                    if r is None:
                        yield
                bk, t = r
                g = GA[:, 2 * u:2 * u + 2, :]
                c = tt(dve, g, g, bk.ap.rearrange("p (m t) -> p m t", m=2), ALU.mult, [t, t_ga[u]])
                bk.free = [c]
                t_ga[u] = c
                tg = t
                yield
            over2.append(tg)

        def project_set(o):
            yield from project_dil([o, o + 2, o + 4, o + 6, o + 8, o + 10])
            yield from project_v([o, o + 2, o + 4])

        drain(project_set(0))
        side = project_set(1)
        weave([dil_attention(0), dil_attention(1)], side, 2, 1)
        drain(side)
        side = up_gdn()
        weave([dil_attention(2), dil_attention(3)], side, 5, 3)
        drain(side)
        sf.close()
        t_mg = [None] * KB
        for u in range(2):
            w = weights("w_up_dil", u)
            for v in range(2):
                bk = banks.take()
                for m in range(2):
                    t = mm3(bk[:, m * T:(m + 1) * T],
                            [(block_of(w, k, (2 * v + m) * P, parts=4), two(YB, slice(None), k, slice(None))) for k in range(4)],
                            [w.split] + t_yb + bk.free)
                j = 4 * u + 2 * v
                b, a = GB[:, j:j + 2, :], GA[:, j:j + 2, :]
                c = tt(dve, b, b, bk.ap.rearrange("p (m t) -> p m t", m=2), ALU.mult, [t, t_gb_[j // 2]])
                bk.free = [c]
                c = tt(pool, b, b, a, ALU.add, [c, t_ga[j // 2]])
                t_mg[j] = t_mg[j + 1] = split(YH[0][:, j:j + 2, :], YH[1][:, j:j + 2, :], b, [c] + over2)
            used_up(w, t)
        t_r = [None] * KB
        st = Stats(T)
        for u in range(4):
            for r in unit2(("w_out", u), [], x=YH, tx=t_mg):
                pass
            bk, t = r
            for m in range(2):
                j = 2 * u + m
                t_r[j] = stt(R[:, j, META:L], bk[:, m * T:(m + 1) * T], mod[:, 16 + j:17 + j], R[:, j, META:L],
                             ALU.mult, ALU.add, [t, t_mod2])
            bk.free = [t_r[2 * u + 1]]
            for m in range(2):
                st.add(R[:, 2 * u + m, META:L], t_r[2 * u + m])
        se.close()
        sd.close()

        t = ts(dve, s1g[:, :], mod[:, 32:40], 1.0, None, ALU.add, None, [t_mod2])
        t_s2 = tt(dve, s1g[:, :], s1g[:, :], sm("g_ffn"), ALU.mult, [t])
        t_h2 = to_h(META, st.done(), t_r, lambda k: s1g[:, k:k + 1], shift=lambda k: mod[:, 24 + k:25 + k], t_g=t_s2)
        sx = ExitStack()
        rt = sb("rt", 704, scope=sx)
        sco = rt[:, 0:128].rearrange("p (t e) -> p t e", t=2)
        sel = rt[:, 128:256].rearrange("p (t e) -> p t e", t=2)
        cmb = rt[:, 256:384].rearrange("p (t e) -> p t e", t=2)
        mk = rt[:, 384:512].rearrange("p (t e) -> p t e", t=2)
        g8 = rt[:, 512:640].rearrange("p (t g e) -> p t g e", t=2, g=8)
        gs8 = rt[:, 640:656].rearrange("p (t g) -> p t g", t=2)
        m8 = rt[:, 656:672].rearrange("p (t g) -> p t g", t=2)
        gm = rt[:, 672:688].rearrange("p (t g) -> p t g", t=2)
        sm2 = rt[:, 688:692]
        CT = sb("CT", T, scope=sx)[:, :]
        wr_ = sbr("wr", 512, sx)
        wr, t_wr = fetch_all("w_r", 512, sx, [t_r[7]])
        t_wr = split(wr_[0], wr_[1], wr, [t_wr, t_r[7]])
        acc = banks.bufs[0:4]
        mb = Ring([])
        mb.bufs = banks.bufs[4:8]
        for b in acc:
            assert not b.held
        t_ct = None

        def route():
            nonlocal t_ct
            bk = mb.take()
            t = mm3(bk[0:64, 0:T], [((wr_[0][:, 64 * k:64 * k + 64], wr_[1][:, 64 * k:64 * k + 64]), two(HX, slice(None), k, slice(None)))
                                    for k in range(KB)], t_h2 + [t_wr] + bk.free)
            t = copy(act, CT[0:64, :], bk[0:64, 0:T], [t, t_r[7]])
            bk.free = [t]
            yield
            bk = mb.take()
            for i in range(2):
                t = tr(bk[:, i * 64:(i + 1) * 64], CT[0:64, i * P:(i + 1) * P], [t] + bk.free, n=64)
            t = actf(sco, bk[:, 0:128].rearrange("p (t e) -> p t e", t=2), ACT.Sigmoid, [t])
            bk.free = [t]
            t = tt(dve, sel, sco, sm("rbias").unsqueeze(1).to_broadcast([P, 2, 64]), ALU.add, [t])
            for i in range(2):
                for g in range(8):
                    tl = dve.add(lambda e, i=i, g=g: e.max(g8[:, i, g, :], sel[:, i, 8 * g:8 * g + 8]), [t])
            t = tt(dve, gs8, g8[:, :, :, 0], g8[:, :, :, 1], ALU.add, [tl])
            for i in range(2):
                tl = dve.add(lambda e, i=i: e.max(m8[:, i, :], gs8[:, i, :]), [t])
            t = dve.add(lambda e: e.memset(m8[:, :, 4:8], BIG), [tl])
            for i in range(2):
                tl = dve.add(lambda e, i=i: e.match_replace(gm[:, i, :], m8[:, i, :], gs8[:, i, :], -BIG), [t])
            t = ts(dve, gm, gm, -BIG, None, ALU.is_equal, None, [tl])
            gmb = gm.unsqueeze(3).to_broadcast([P, 2, 8, 8])
            mk4 = mk.rearrange("p t (g e) -> p t g e", g=8)
            t1 = tt(dve, mk4, sel.rearrange("p t (g e) -> p t g e", g=8), gmb, ALU.mult, [t])
            t2 = ts(dve, gm, gm, -1.0, BIG, ALU.add, ALU.mult, [t1])
            t = tt(dve, mk4, mk4, gmb, ALU.add, [t2])
            for i in range(2):
                tl = dve.add(lambda e, i=i: e.max(m8[:, i, :], mk[:, i, :]), [t])
            for i in range(2):
                t = dve.add(lambda e, i=i: e.match_replace(sel[:, i, :], m8[:, i, :], mk[:, i, :], 2 * BIG), [tl])
            t = ts(dve, sel, sel, 2 * BIG, None, ALU.is_equal, None, [t])
            t = tt(dve, cmb, sco, sel, ALU.mult, [t])
            t = dve.add(lambda e: e.tensor_reduce(sm2[:, 0:2], cmb, AX.X, ALU.add), [t])
            t = recip(sm2[:, 2:4], sm2[:, 0:2], [t])
            for i in range(2):
                t_c = ts(dve, cmb[:, i, :], cmb[:, i, :], sm2[:, 2 + i:3 + i], 2.5, ALU.mult, ALU.mult, [t])
            yield
            bk = mb.take()
            for i in range(2):
                t = tr(bk[0:64, i * P:(i + 1) * P], cmb[:, i, :], [t_c] + bk.free)
            t_ct = copy(dve, CT[0:64, :], bk[0:64, 0:T], [t])
            bk.free = [t_ct]
            yield

        afr = Ring([sb(f"af{i}", 512, scope=sx)[:, :] for i in range(2)])
        arr = [sbr(f"ar{i}", 512, sx) for i in range(2)]
        arr_free = [[], []]
        cbs = Ring([sb(f"cb{i}", 256, scope=sx)[:, :] for i in range(2)])
        def down(e, i, ta):
            w = weights("w_ed", e)
            ah, al = arr[i]
            tj = [None] * KB
            for j in range(KB):
                bi = j // 2
                t = mm3(acc[bi][:, (j % 2) * T:(j % 2 + 1) * T],
                        [(block_of(w, f, j * P, parts=2), (ah[:, f * T:(f + 1) * T], al[:, f * T:(f + 1) * T])) for f in range(2)],
                        [ta, w.split] + acc[bi].free, start=(e == NE and j % 2 == 0), stop=(e == NE - 1), skip=True)
                tj[j] = t
            used_up(w, t)
            arr_free[i] = [t]
            return tj

        state["eager"] = True
        prev = None
        router = route()
        for e in [NE] + list(range(NE)):
            bg, bu = mb.take(), mb.take()
            w = weights("w_eg", e)
            for f in range(2):
                tg = proj(w, f, bg[:, f * T:(f + 1) * T], bg.free, tx=t_h2)
                if e == NE:
                    next(router)
            used_up(w, tg)
            if e == 0:
                next(router)
            w = weights("w_eu", e)
            if e < NE:
                bc, cb = mb.take(), cbs.take()
                tcb = mm(bc[:, 0:T], [(cn_t[0:64, CN["ident"][0] + e:CN["ident"][0] + e + 1].to_broadcast([64, P]), CT[0:64, :])],
                         [t_ct] + bc.free)
                tcc = copy(act, cb[:, 0:T], bc[:, 0:T], [tcb] + cb.free)
                bc.free = [tcc]
            for f in range(2):
                tu = proj(w, f, bu[:, f * T:(f + 1) * T], bu.free, tx=t_h2)
            if e != NE - 1:
                used_up(w, tu)
            a = afr.take()
            t1 = actf(a.ap, bg[:, :], ACT.Silu, [tg] + a.free)
            bg.free = [t1]
            if prev is not None and e != NE - 1:
                down(*prev)
            a3 = a.ap.rearrange("p (f t) -> p f t", f=2)
            if e < NE:
                t1 = tt(pool, a3, a3, cb[:, 0:T].unsqueeze(1).to_broadcast([P, 2, T]), ALU.mult, [t1, tcc])
                cb.free = [t1]
            t2 = tt(dve, a.ap, a.ap, bu[:, :], ALU.mult, [t1, tu])
            bu.free = [t2]
            i = e % 2 if e < NE else 1
            t3 = split(arr[i][0], arr[i][1], a.ap, [t2] + arr_free[i], dve if e == NE - 1 else pool)
            a.free = [t3]
            if e == NE - 1:
                used_up(w, tu)
                down(*prev)
            prev = (e, i, t3)
        t_acc = down(*prev)
        t_acc = [t_acc[j | 1] for j in range(KB)]
        st = Stats(L, by=(act,), bank=mb.take())
        for j in range(KB):
            t_r[j] = stt(R[:, j, META:L], acc[j // 2][:, (j % 2) * T:(j % 2 + 1) * T], mod[:, 40 + j:41 + j], R[:, j, META:L],
                         ALU.mult, ALU.add, [t_acc[j]])
            acc[j // 2].free = [t_r[j]]
            st.add(R[:, j, :], t_r[j])
        t_acc = t_acc[KB - 1]
        sx.close()

        n2 = sm("norm2").rearrange("p (i k) -> p i k", i=8)
        s2 = ExitStack()
        MT = sb("MT", KB * L, scope=s2)[:, :].rearrange("p (b t) -> p b t", b=KB)
        HF = (HH, HL)
        OT = tuple(a.rearrange("p (b t) -> p b t", b=KB) for a in YR)
        QT = [(0, 16), (16, 128), (144, 128)]

        def one(bk):
            return bk[:, 0:L]

        def add_mix(rs, t_src, gi, c0, st=None):
            def put(k, f, t):
                t = tt(dve, R[:, k, c0:L], R[:, k, c0:L], f, ALU.add, [t])
                if st is not None:
                    st.add(R[:, k, c0:L], t)
                return t, [t]
            return scaled(MT, c0, rs, t_src, lambda k: n2[:, gi, k:k + 1], put)

        def mixer_out(layer, tx):
            toks = []
            sm_ = Stats(L, 1)
            for u in range(4):
                w = weights("w_out2", 4 * layer + u)
                for m in range(2):
                    bk = banks.take()
                    t = proj(w, m, one(bk), bk.free, x=OT, tx=tx)
                    used(m, w, t)
                    c = copy(act if m else dve, MT[:, 2 * u + m, :], one(bk), [t])
                    bk.free = [c]
                    toks.append(c)
                    sm_.add(MT[:, 2 * u + m, :], c)
            st_ = Stats(L, by=(act,))
            return add_mix(sm_.done(), toks, 4 * layer + 1, 0, st_), st_

        def mlp(layer, tr_, rs, c0):
            th = to_h(0, rs, tr_, lambda k: n2[:, 4 * layer + 2, k:k + 1])
            n = L - c0
            sc_ = ExitStack()
            X2 = tuple(a.rearrange("p (b t) -> p b t", b=32) for a in sbr(f"X{layer}", 32 * L, sc_))
            toks, later = [], []
            for u in range(16):
                w = weights("w_up2", 16 * layer + u)
                for m in range(2):
                    bk = banks.take()
                    t = proj(w, m, bk[:, 0:n], bk.free, x=(HH[:, :, c0:L], HL[:, :, c0:L]), tx=th)
                    used(m, w, t)
                    if later:
                        later.pop()()
                    b = 2 * u + m
                    f = tfr.take()
                    c = actf(f[:, 0:n], bk[:, 0:n], ACT.Relu, [t] + f.free)
                    c2 = tt(dve, f[:, 0:n], f[:, 0:n], bk[:, 0:n], ALU.mult, [c])
                    bk.free = [c2]

                    def parts(b=b, f=f, c2=c2):
                        c3 = split(X2[0][:, b, c0:L], X2[1][:, b, c0:L], f[:, 0:n], [c2])
                        f.free = [c3]
                        toks.append(c3)
                    later.append(parts)
            later.pop()()
            dt_ = []
            sm_ = Stats(n, 2)
            for g in range(4):
                bks = [banks.take(), banks.take()]
                for kc in range(4):
                    w = weights("w_down2", 16 * layer + 4 * g + kc)
                    for m in range(2):
                        for k in range(KB):
                            t = mm3(bks[m][:, 0:n], [(block_of(w, k, m * P), two(X2, slice(None), 8 * kc + k, slice(c0, L)))],
                                    [w.split, toks[8 * kc + k]] + bks[m].free, start=kc == 0 and k == 0, stop=kc == 3 and k == KB - 1)
                    used_up(w, t)
                for m in range(2):
                    c = copy(act if m else dve, MT[:, 2 * g + m, c0:L], bks[m][:, 0:n], [t])
                    bks[m].free = [c]
                    dt_.append(c)
                    sm_.add(MT[:, 2 * g + m, c0:L], c)
            sc_.close()
            st_ = None if layer else Stats(L, by=(act,))
            return add_mix(sm_.done(), dt_, 4 * layer + 3, c0, st_), st_

        t_hh = to_h(0, st.done(), t_r, lambda k: n2[:, 0, k:k + 1])
        sa = ExitStack()
        lam_, t_l = fetch_all("lam", 256, sa, [t_acc])
        s = sqr.take()
        sv_ = s[:, 0:128].rearrange("p (a d) -> p a d", a=2)
        lv2 = lam_.rearrange("p (a b d) -> p a b d", a=2, b=2)
        t = tt(dve, sv_, lv2[:, :, 0, :], lv2[:, :, 1, :], ALU.mult, [t_l] + s.free)
        t = dve.add(lambda e: e.tensor_reduce(lm[:, 0:2], sv_, AX.X, ALU.add), [t])
        s.free = [t]
        t = actf(lm[:, 0:2], lm[:, 0:2], ACT.Exp, [t])
        t = tt(dve, lm[:, 2:3], lm[:, 0:1], lm[:, 1:2], ALU.subtract, [t])
        t_lam = ts(dve, lm[:, 2:3], lm[:, 2:3], LAM0, None, ALU.add, None, [t])
        t_sub = ts(dve, lm[:, 3:4], sm("subln"), 1.0 - LAM0, None, ALU.mult, None, [t_sm])

        QK2 = sb("QK2", 16 * L, scope=sa)[:, :].rearrange("p (b t) -> p b t", b=16)
        VV = sb("VV", 3072, scope=sa)[:, :].rearrange("p (t n) -> p t n", t=3)
        ps_ = Ring([sb(f"pp{i}", 544, scope=sa)[:, :].rearrange("p (c k) -> p c k", c=2) for i in range(3)])
        at_ = Ring([sb(f"at{i}", 384, scope=sa)[:, :].rearrange("p (j q) -> p j q", j=3) for i in range(2)])
        t_over = t_acc
        t_vz = memset(pool, VV[:, 0, :], 0.0, [t_over, t_r[7]])
        for b in at_.bufs:
            b.free = [memset(pool, b[:, 0, :], 0.0, [t_over, t_r[7]])]
        for b in ps_.bufs:
            b.free = [t_over, t_r[7], t3]
        c2 = fetch("c2", sa, [t_over, t_r[7], t3])
        tqk = [None] * 16
        t_vv = [None] * 4
        t_ot = [None] * NH

        def project_heads(p):
            for j in range(2):
                w = weights("w_in2", 4 * j + p)
                for m in range(2):
                    bk = banks.take()
                    for k in (0, 4):
                        t = proj(w, m, one(bk), bk.free, x=HF, tx=t_hh, k0=k, k1=k + 4)
                        if k == 0:
                            yield
                    used(m, w, t)
                    b = 8 * j + 2 * p + m
                    c = actf(QK2[:, b, :], one(bk), ACT.Copy, [t, t_over, t3], scale=1.0 if j else 0.125)
                    bk.free = [c]
                    tqk[b] = c
                    yield
            w = weights("w_in2", 8 + p)
            for i, (q0, nq) in enumerate(QT):
                bk = banks.take()
                for k in range(KB):
                    t = mm3(bk[:, 0:256], [(two(HF, slice(None), k, slice(q0, q0 + P)), block_of(w, k, 0, 256))],
                            [w.split, t_hh[k]] + bk.free, start=k == 0, stop=k == KB - 1)
                if i == 2:
                    used_up(w, t)
                c = copy(dve, VV[0:nq, i, p * 256:(p + 1) * 256], bk[0:nq, 0:256], [t, t_vz])
                bk.free = [c]
                yield
            t_vv[p] = c

        def attend(h):
            p = h // 2
            if True:
                slope = 2.0 ** (-(h + 1))
                ob = banks.take()
                for i, (q0, nq) in enumerate(QT):
                    nk = q0 + nq
                    bc = [banks.take(), banks.take()]
                    for c in range(2):
                        t = mm(bc[c][0:nq, 0:nk], [(QK2[64 * c:64 * c + 64, h, q0:q0 + nq], QK2[64 * c:64 * c + 64, 8 + h, 0:nk])],
                               [tqk[h], tqk[8 + h]] + bc[c].free)
                    pb = ps_.take()
                    for c in range(2):
                        tb = stt(pb[0:nq, c, 0:nk], c2(f"nd{i}")[0:nq, :], slope, bc[c][0:nq, 0:nk], ALU.mult, ALU.add, [t, c2.tok] + pb.free)
                        bc[c].free = [tb]
                    sv = str_.take()
                    t = rmax(sv[0:nq, 0:2], pb[0:nq, :, 0:nk], AX.X, [tb] + sv.free)
                    t = ts(dve, sv[0:nq, 2:4], sv[0:nq, 0:2], -1.0, None, ALU.mult, None, [t])
                    for c in range(2):
                        te = actf(pb[0:nq, c, 0:nk], pb[0:nq, c, 0:nk], ACT.Exp, [t], bias=sv[0:nq, 2 + c:3 + c],
                                  accum_out=sv[0:nq, 4 + c:5 + c])
                    t = recip(sv[0:nq, 6:8], sv[0:nq, 4:6], [te])
                    t = ts(dve, sv[0:nq, 7:8], sv[0:nq, 7:8], lm[0:nq, 2:3], None, ALU.mult, None, [t, t_lam])
                    t1 = ts(dve, pb[0:nq, 1, 0:nk], pb[0:nq, 1, 0:nk], sv[0:nq, 7:8], None, ALU.mult, None, [t])
                    t1 = stt(pb[0:nq, 0, 0:nk], pb[0:nq, 0, 0:nk], sv[0:nq, 6:7], pb[0:nq, 1, 0:nk], ALU.mult, ALU.subtract, [t1])
                    sv.free = [t1]
                    yield
                    bt = banks.take()
                    for j in range(i + 1):
                        k0, n_ = QT[j]
                        tx = tr(bt[0:n_, j * P:j * P + nq], pb[0:nq, 0, k0:k0 + n_], [t1] + bt.free, n=nq)
                    at = at_.take()
                    c1 = copy(act, at[0:16, 0, 0:nq], bt[0:16, 0:nq], [tx] + at.free)
                    if i:
                        c1 = copy(act, at[:, 1:i + 1, 0:nq], bt[:, P:(i + 1) * P].rearrange("p (j q) -> p j q", j=i), [tx])
                    bt.free = [c1]
                    pb.free = [tx]
                    yield
                    t = mm(ob[:, q0:q0 + nq], [(VV[:, j, h * P:(h + 1) * P], at[:, j, 0:nq]) for j in range(i + 1)],
                           [c1, t_vv[p]] + ob.free)
                    at.free = [t]
                f = tfr.take()
                c = copy(act, f[:, 0:L], one(ob), [t] + f.free)
                ob.free = [c]
                s = sqr.take()
                d = tt(pool, s[:, 0:L], f[:, 0:L], f[:, 0:L], ALU.mult, [c] + s.free)
                yield
                rs = Rstd(s, (0, P, L - P), 1.0 / P, [d])
                s.free = [rs.sq]
                yield
                bs, f2 = rs.spread()
                t = stt(f[:, 0:L], f[:, 0:L], lm[:, 3:4], bs[:, 0:L], ALU.mult, ALU.mult, [f2, c, t_sub])
                bs.free = [t]
                t_ot[h] = split(OT[0][:, h, :], OT[1][:, h, :], f[:, 0:L], [t])
                f.free = [t_ot[h]]
                yield

        state["eager"] = False
        drain(project_heads(0))
        for p in range(4):
            side = project_heads(p + 1) if p < 3 else iter(())
            weave([attend(2 * p), attend(2 * p + 1)], side, 7, 9)
            drain(side)
        state["eager"] = True
        tr_, st = mixer_out(0, t_ot)
        sa.close()
        tr_, st = mlp(0, tr_, st.done(), 0)

        t_hh = to_h(0, st.done(), tr_, lambda k: n2[:, 4, k:k + 1])
        sa = ExitStack()
        BCU = sb("BCU", 24 * L, scope=sa)[:, :].rearrange("p (b t) -> p b t", b=24)
        yv = Ring([sb(f"yv{i}", L, scope=sa)[:, :] for i in range(2)])
        cv = sm("conv2").rearrange("p (b j) -> p b j", b=8)
        t_ot = [None] * KB
        later = []

        def short_conv(k, tb_, tb1, tb2):
            u_ = BCU[:, 16 + k, :]
            y_ = yv.take()
            t = tt(pool, u_, u_, BCU[:, 8 + k, :], ALU.mult, [tb1, tb2])
            t = ts(dve, y_.ap, u_, cv[:, k, 2:3], None, ALU.mult, None, [t] + y_.free)
            for j in (1, 2):
                t = stt(y_[:, j:L], u_[:, 0:L - j], cv[:, k, 2 - j:3 - j], y_[:, j:L], ALU.mult, ALU.add, [t])
            t = tt(pool, y_.ap, y_.ap, BCU[:, k, :], ALU.mult, [t, tb_])
            t_ot[k] = split(OT[0][:, k, :], OT[1][:, k, :], y_.ap, [t])
            y_.free = [t_ot[k]]

        for p in range(4):
            tb_ = {}
            for j in range(3):
                w = weights("w_in2", 12 + 4 * j + p)
                for m in range(2):
                    bk = banks.take()
                    t = proj(w, m, one(bk), bk.free, x=HF, tx=t_hh)
                    used(m, w, t)
                    c = copy(act, BCU[:, 8 * j + 2 * p + m, :], one(bk), [t, tr_[7]])
                    bk.free = [c]
                    tb_[j, m] = c
                    if later and m == 1:
                        short_conv(*later.pop(0))
            later += [(2 * p + m, tb_[0, m], tb_[1, m], tb_[2, m]) for m in range(2)]
        for a in later:
            short_conv(*a)
        tr_, st = mixer_out(1, t_ot)
        sa.close()
        tr_, _ = mlp(1, tr_, st.done(), META)
        t_out = misc[3].start(sp, out, R[:, :, META:L], tr_)

        s2.close()

        for q in (pe, act, dve, pool, sp):
            q.number()
        block = ctx.enter_context(nc.Block())

        @block.tensor
        def _(e):
            pe.emit(e)

        @block.scalar
        def _(e):
            act.emit(e)

        @block.vector
        def _(e):
            dve.emit(e)

        @block.gpsimd
        def _(e):
            pool.emit(e)

        @block.sync
        def _(e):
            sp.emit(e)
            e.wait_ge(t_out.q.sem, t_out.value)


def tile_weights(w, cols=256):
    K, N = w.shape
    return np.ascontiguousarray(w.reshape(K // P, P, N // cols, cols).transpose(2, 1, 0, 3)).reshape(N // cols, P, -1)


def by_feature(v):
    v = np.asarray(v)
    return v.reshape(-1, P).T


def kernel(**inputs):
    import concourse.bacc as bacc
    from concourse.bass_utils import run_bass_kernel_spmd

    a = {k: np.asarray(v) for k, v in inputs.items()}
    wi = a["w_in"][0]
    q3, z, ba, rest = wi[:, :3072], wi[:, 3072:4096], wi[:, 4096:4112], wi[:, 4112:]
    w_in = np.concatenate([tile_weights(x) for x in (q3, z, rest)])
    every = lambda v: np.broadcast_to(np.asarray(v).reshape(1, -1), (P, v.size))
    small = {
        "c": by_feature(a["c"][0]), "b_ada": by_feature(a["b_ada"][0]), "g_mix": by_feature(a["g_mix"][0]),
        "g_ffn": by_feature(a["g_ffn"][0]),
        "conv": a["gdn_conv_w"][0].reshape(4, 24, P).transpose(2, 1, 0).reshape(P, 96),
        "gdn_g": a["gdn_norm_g"].reshape(P, 1), "dq_g": a["dil_q_norm_g"].reshape(P, 1),
        "dk_g": a["dil_k_norm_g"].reshape(P, 1),
        "norm2": by_feature(a["norm_g_2"]),
        "conv2": a["conv_w_2"][0].reshape(3, 8, P).transpose(2, 1, 0).reshape(P, 24),
        "subln": a["subln_g_2"].reshape(P, 1), "a_log": every(a["gdn_a_log"]), "dt": every(a["gdn_dt_bias"]),
        "rbias": every(a["router_bias"]), 
    }
    extra = {
        "lam": every(a["lambda_params_2"]),
        "w_ba": ba.reshape(8, P, 16).transpose(1, 0, 2).reshape(P, 128),
        "w_r": a["w_router"][0].reshape(8, P, 64).transpose(1, 0, 2).reshape(P, 512),
    }
    x = np.concatenate([a["meta_tokens_2"], a["x"][0]], axis=0)
    arrays = {
        "x": x.T.reshape(8, P, L).transpose(1, 0, 2),
        "small": np.concatenate([small[n] for n, _ in SMALL], axis=1),
        **constants(),
        **extra,
        "w_ada": tile_weights(a["w_ada"][0]),
        "w_in": w_in,
        "w_up_gdn": tile_weights(a["w_up_gdn"][0]),
        "w_up_dil": tile_weights(a["w_up_dil"][0], 512),
        "w_out": tile_weights(a["w_out"][0]),
        "w_eg": a["w_exp_gate"][0].reshape(NE, 8, P, 256).transpose(0, 2, 1, 3).reshape(NE, P, 2048),
        "w_eu": a["w_exp_up"][0].reshape(NE, 8, P, 256).transpose(0, 2, 1, 3).reshape(NE, P, 2048),
        "w_ed": a["w_exp_down"][0].reshape(NE, 2, P, 1024).transpose(0, 2, 1, 3).reshape(NE, P, 2048),
        "w_sg": tile_weights(a["w_sh_gate"][0])[0],
        "w_su": tile_weights(a["w_sh_up"][0])[0],
        "w_sd": tile_weights(a["w_sh_down"][0], 1024)[0],
        "w_in2": np.concatenate([tile_weights(a["w_in_2"][i]) for i in range(2)]),
        "w_out2": np.concatenate([tile_weights(a["w_out_2"][i]) for i in range(2)]),
        "w_up2": np.concatenate([tile_weights(a["w_up_2"][i]) for i in range(2)]),
        "w_down2": np.ascontiguousarray(a["w_down_2"].reshape(2, 4, 8, P, 4, 256).transpose(0, 4, 1, 3, 2, 5)).reshape(32, P, 2048),
    }
    nc = bacc.Bacc("TRN2", target_bir_lowering=False, num_devices=1)
    arrays = {f"in_{k}": np.ascontiguousarray(v) for k, v in arrays.items()}
    ins = {k[3:]: nc.dram_tensor(k, v.shape, F32, kind="ExternalInput").ap() for k, v in arrays.items()}
    out = nc.dram_tensor("out_0", (P, KB, T), F32, kind="ExternalOutput").ap()
    program(nc, ins, out)
    r = run_bass_kernel_spmd(nc, [arrays], core_ids=[0])
    y = r.results[0]["out_0"]
    return y.transpose(1, 0, 2).reshape(D, T).T.reshape(1, T, D)
```
